# Optimizing a Trainium2 kernel written in Bass

```python
import math
import jax, jax.numpy as jnp
from jax import lax
import numpy as np

D_MODEL = 1024
BATCH = 1
SEQ = 1024
DEPTH = 1

SSM_EXPAND = 2
SSM_D_INNER = SSM_EXPAND * D_MODEL
SSM_HEAD_DIM = 64
SSM_HEADS = SSM_D_INNER // SSM_HEAD_DIM
SSM_GROUPS = 8
SSM_STATE = 128
SSM_CONV = 4
SSM_CHUNK = 256
SSM_XBC = SSM_D_INNER + 2 * SSM_GROUPS * SSM_STATE
SC_WIDTH = D_MODEL
SC_CONV = 3
D_IN_PROJ = SSM_D_INNER + SSM_XBC + SSM_HEADS + 4 * SC_WIDTH
SPLIT_Z = SSM_D_INNER
SPLIT_XBC = SPLIT_Z + SSM_XBC
SPLIT_DT = SPLIT_XBC + SSM_HEADS
SPLIT_SCB = SPLIT_DT + SC_WIDTH
SPLIT_SCC = SPLIT_SCB + SC_WIDTH
SPLIT_SCX = SPLIT_SCC + SC_WIDTH
N_BRANCH = 2
DN_ALPHA = (2 * DEPTH) ** 0.25
DN_BETA = (8 * DEPTH) ** -0.25
LN_EPS = 1e-5
RMS_EPS = 1e-5
DT_MIN = 1e-3
DT_MAX = 1e-1

kernel_name = "hybrid_ssd_shortconv_gated_merge"

def layer_norm(x, g=None, b=None):
    xf = x.astype(jnp.float32)
    mu = jnp.mean(xf, axis=-1, keepdims=True)
    xc = xf - mu
    var = jnp.mean(xc * xc, axis=-1, keepdims=True)
    y = xc * lax.rsqrt(var + LN_EPS)
    if g is not None:
        y = y * g.astype(jnp.float32) + b.astype(jnp.float32)
    return y.astype(x.dtype)

def causal_depthwise_conv(x, w, b=None):
    k = w.shape[0]
    ch = x.shape[-1]
    y = lax.conv_general_dilated(
        x, w[:, None, :].astype(x.dtype), window_strides=(1,), padding=[(k - 1, 0)],
        dimension_numbers=("NWC", "WIO", "NWC"), feature_group_count=ch)
    if b is not None:
        y = y + b
    return y

def ssd_chunked_scan(xdt, a, bm, cm):
    bsz, s, h, p = xdt.shape
    g, n = bm.shape[2], bm.shape[3]
    r = h // g
    L = SSM_CHUNK
    pad = (-s) % L
    if pad:
        pw = lambda t: jnp.pad(t, [(0, 0), (0, pad)] + [(0, 0)] * (t.ndim - 2))
        xdt, a, bm, cm = pw(xdt), pw(a), pw(bm), pw(cm)
    sp = s + pad
    nc = sp // L
    xc = xdt.reshape(bsz, nc, L, g, r, p).transpose(1, 0, 2, 3, 4, 5)
    ac = a.reshape(bsz, nc, L, g, r).transpose(1, 0, 2, 3, 4)
    bc = bm.reshape(bsz, nc, L, g, n).transpose(1, 0, 2, 3, 4)
    cc = cm.reshape(bsz, nc, L, g, n).transpose(1, 0, 2, 3, 4)
    causal = jnp.tril(jnp.ones((L, L), dtype=bool))[None, :, :, None, None]

    def step(state, inp):
        x_, a_, b_, c_ = inp
        a_cum = jnp.cumsum(a_, axis=1)
        seg = a_cum[:, :, None] - a_cum[:, None, :]
        decay = jnp.exp(jnp.where(causal, seg, -jnp.inf))
        cb = jnp.einsum("blgn,bsgn->blsg", c_, b_)
        y_diag = jnp.einsum("blsg,blsgr,bsgrp->blgrp", cb, decay, x_)
        y_off = jnp.einsum("blgn,bgrpn->blgrp", c_, state) * jnp.exp(a_cum)[..., None]
        a_end = a_cum[:, -1]
        to_end = jnp.exp(a_end[:, None] - a_cum)
        new_state = state * jnp.exp(a_end)[..., None, None] + jnp.einsum(
            "bsgn,bsgr,bsgrp->bgrpn", b_, to_end, x_)
        return new_state, y_diag + y_off

    h0 = jnp.zeros((bsz, g, r, p, n), jnp.float32)
    _, y = lax.scan(step, h0, (xc, ac, bc, cc))
    y = y.transpose(1, 0, 2, 3, 4, 5).reshape(bsz, sp, h, p)
    return y[:, :s]

def hybrid_layer(x, c, w_mod, b_mod, w_in, conv_ssm_w, conv_ssm_b, dt_bias, a_log,
                 d_skip, ssm_norm_w, conv_sc_w, w_branch_a, w_branch_b, w_gate,
                 b_gate, w_out, ln_g, ln_b):
    bsz, s, _ = x.shape
    mod = c @ w_mod + b_mod
    shift, scale, gate = jnp.split(mod, 3, axis=-1)
    u = layer_norm(x) * (1 + scale[:, None, :]) + shift[:, None, :]

    proj = u @ w_in
    z, xbc, dt_raw, sc_b, sc_c, sc_x, sc_g = jnp.split(
        proj, [SPLIT_Z, SPLIT_XBC, SPLIT_DT, SPLIT_SCB, SPLIT_SCC, SPLIT_SCX], axis=-1)

    xbc = jax.nn.silu(causal_depthwise_conv(xbc, conv_ssm_w, conv_ssm_b))
    xs, bm, cm = jnp.split(xbc, [SSM_D_INNER, SSM_D_INNER + SSM_GROUPS * SSM_STATE], axis=-1)
    dt = jax.nn.softplus(dt_raw.astype(jnp.float32) + dt_bias.astype(jnp.float32))
    a_head = -jnp.exp(a_log.astype(jnp.float32))
    xh = xs.reshape(bsz, s, SSM_HEADS, SSM_HEAD_DIM).astype(jnp.float32)
    y = ssd_chunked_scan(
        xh * dt[..., None], dt * a_head,
        bm.reshape(bsz, s, SSM_GROUPS, SSM_STATE).astype(jnp.float32),
        cm.reshape(bsz, s, SSM_GROUPS, SSM_STATE).astype(jnp.float32))
    y = y + d_skip.astype(jnp.float32)[:, None] * xh
    y = y.reshape(bsz, s, SSM_D_INNER) * jax.nn.silu(z.astype(jnp.float32))
    yg = y.reshape(bsz, s, SSM_GROUPS, SSM_D_INNER // SSM_GROUPS)
    yg = yg * lax.rsqrt(jnp.mean(yg * yg, axis=-1, keepdims=True) + RMS_EPS)
    y = yg.reshape(bsz, s, SSM_D_INNER) * ssm_norm_w.astype(jnp.float32)
    y_a = y.astype(x.dtype) @ w_branch_a

    v = causal_depthwise_conv(sc_c * sc_x, conv_sc_w)
    y_b = (jax.nn.silu(sc_g) * sc_b * v) @ w_branch_b

    gates = jax.nn.sigmoid(u @ w_gate + b_gate)
    g_a, g_b = jnp.split(gates, N_BRANCH, axis=-1)
    mixed = (g_a * y_a + g_b * y_b) @ w_out

    return layer_norm(DN_ALPHA * x + gate[:, None, :] * mixed, ln_g, ln_b)

def setup_inputs(seed: int = 0) -> dict:
    key = jax.random.key(seed)
    ks = jax.random.split(key, 20)
    f32 = jnp.float32
    nrm = lambda k, shape, sc: jax.random.normal(k, shape, f32) * sc
    u_dt = jax.random.uniform(ks[7], (DEPTH, SSM_HEADS), f32)
    dt0 = jnp.exp(u_dt * (math.log(DT_MAX) - math.log(DT_MIN)) + math.log(DT_MIN))
    dt_bias = dt0 + jnp.log(-jnp.expm1(-dt0))
    return {
        "x": nrm(ks[0], (BATCH, SEQ, D_MODEL), 1.0),
        "c": nrm(ks[1], (BATCH, D_MODEL), 1.0),
        "w_mod": nrm(ks[2], (DEPTH, D_MODEL, 3 * D_MODEL), 0.5 * D_MODEL ** -0.5),
        "b_mod": nrm(ks[3], (DEPTH, 3 * D_MODEL), 0.01),
        "w_in": nrm(ks[4], (DEPTH, D_MODEL, D_IN_PROJ), D_MODEL ** -0.5),
        "conv_ssm_w": nrm(ks[5], (DEPTH, SSM_CONV, SSM_XBC), SSM_CONV ** -0.5),
        "conv_ssm_b": nrm(ks[6], (DEPTH, SSM_XBC), 0.01),
        "dt_bias": dt_bias,
        "a_log": jnp.log(jax.random.uniform(ks[8], (DEPTH, SSM_HEADS), f32, 1.0, 16.0)),
        "d_skip": 1.0 + nrm(ks[9], (DEPTH, SSM_HEADS), 0.1),
        "ssm_norm_w": 1.0 + nrm(ks[10], (DEPTH, SSM_D_INNER), 0.1),
        "conv_sc_w": nrm(ks[11], (DEPTH, SC_CONV, SC_WIDTH), SC_CONV ** -0.5),
        "w_branch_a": nrm(ks[12], (DEPTH, SSM_D_INNER, D_MODEL), DN_BETA * SSM_D_INNER ** -0.5),
        "w_branch_b": nrm(ks[13], (DEPTH, SC_WIDTH, D_MODEL), DN_BETA * SC_WIDTH ** -0.5),
        "w_gate": nrm(ks[14], (DEPTH, D_MODEL, N_BRANCH * D_MODEL), D_MODEL ** -0.5),
        "b_gate": nrm(ks[15], (DEPTH, N_BRANCH * D_MODEL), 0.01),
        "w_out": nrm(ks[16], (DEPTH, D_MODEL, D_MODEL), DN_BETA * D_MODEL ** -0.5),
        "ln_g": 1.0 + nrm(ks[17], (DEPTH, D_MODEL), 0.1),
        "ln_b": nrm(ks[18], (DEPTH, D_MODEL), 0.01),
    }

def reference(x, c, w_mod, b_mod, w_in, conv_ssm_w, conv_ssm_b, dt_bias, a_log,
              d_skip, ssm_norm_w, conv_sc_w, w_branch_a, w_branch_b, w_gate,
              b_gate, w_out, ln_g, ln_b):
    for l in range(DEPTH):
        x = hybrid_layer(x, c, w_mod[l], b_mod[l], w_in[l], conv_ssm_w[l], conv_ssm_b[l],
                         dt_bias[l], a_log[l], d_skip[l], ssm_norm_w[l], conv_sc_w[l],
                         w_branch_a[l], w_branch_b[l], w_gate[l], b_gate[l], w_out[l],
                         ln_g[l], ln_b[l])
    return x


_drawn_inputs = setup_inputs


def setup_inputs(seed=0):
    import zlib

    import numpy as np

    out = dict(_drawn_inputs(seed))
    spreads = {}
    factors = {'b_mod': 8.0,
     'conv_ssm_b': 8.0,
     'd_skip': 8.0,
     'ssm_norm_w': 6.386,
     'b_gate': 30.065,
     'ln_b': 5.848}
    for name, (base, spread) in spreads.items():
        noise = np.random.default_rng([zlib.crc32(name.encode()), seed]).standard_normal(out[name].shape)
        drawn = base * np.exp(spread * noise) if base else spread * noise
        out[name] = __import__('jax').numpy.asarray(drawn.astype(out[name].dtype))
    for name, factor in factors.items():
        out[name] = (out[name] * factor).astype(out[name].dtype)
    return out
```

```python
import concourse.bass as bass
from concourse import mybir

F32 = mybir.dt.float32
F32R = mybir.dt.float32r
ALU = mybir.AluOpType
ACT = mybir.ActivationFunctionType

P = 128
SEQ = 1024
D = 1024
KT = D // P
TT = SEQ // P
HALF = 512
INNER = 2 * D
GROUPS = 8
GW = INNER // GROUPS
HEADS = 32
HPG = HEADS // GROUPS
HD = 64
XB_COL = INNER
B_COL = XB_COL + INNER
C_COL = B_COL + GROUPS * P
DT_COL = C_COL + GROUPS * P
SCB_COL = DT_COL + HEADS
SCC_COL = SCB_COL + D
SCX_COL = SCC_COL + D
SCG_COL = SCX_COL + D
LN_EPS = 1e-5
RMS_EPS = 1e-5
ALPHA = 2.0 ** 0.25

CONV_B = 128
SC_W = CONV_B + 32
B_MOD = SC_W + 24
B_GATE = B_MOD + 24
NORM_W = B_GATE + 16
C_VEC = NORM_W + 16
N_PAR = C_VEC + 8

U_C, U_C2, U_DT, U_B0 = 0, 32, 48, 49
U_B = U_B0 + 6
U_TAIL = U_B + 8 * 7
U_D = U_TAIL + 2
U_E = U_D + 8
Q_C = 16
Q_C2 = Q_C + 64
Q_DT = Q_C2 + 32
Q_B0 = Q_DT + 2
Q_B = Q_B0 + 16
Q_TAIL = Q_B + 32 * 7
Q_D = Q_TAIL + 16
Q_END = Q_D + 16


class Lin:

    def __init__(self, c, k=0, i=None):
        self.c, self.k, self.i = c, k, i

    def __add__(self, o):
        return Lin(self.c + o, self.k, self.i)

    def __mul__(self, o):
        return Lin(self.c * o, self.k * o, self.i)

    def over(self, d):
        assert self.k % d == 0
        return Lin(self.c // d, self.k // d, self.i)

    def mod(self, d):
        assert self.k % d == 0
        return self.c % d

    def val(self):
        return self.c if self.k == 0 else self.i * self.k + self.c


def at(v):
    return v if isinstance(v, Lin) else Lin(v)


def wait(eng, sem, value):
    v = at(value)
    if v.k == 0 and v.c <= 0:
        return
    eng.wait_ge(sem, v.val())


def run(eng, body, first, stop, step=1, peel=0):
    for n in range(first, first + peel * step, step):
        body(Lin(n))
    lo = first + peel * step
    count = (stop - lo) // step
    with eng.Fori(0, count) as i:
        body(Lin(lo, step, i))


def build(nc, x, c, w_mod, b_mod, w_in, conv_ssm_w, conv_ssm_b, dt_bias, a_log, d_skip,
          ssm_norm_w, conv_sc_w, w_branch_a, w_branch_b, w_gate, b_gate, w_out, ln_g, ln_b,
          spill, out):
    base = [1152]

    def place(name, shape, dt=F32, offset=None):
        size = 4
        for n in shape[1:]:
            size *= n
        size = (size + 31) // 32 * 32
        where = base[0] if offset is None else offset
        if offset is None:
            base[0] += size
        return nc.alloc_sbuf_tensor_at(name, shape, dt, offset=where)

    K = 1024
    u_base = base[0]
    u_hi = place("u_hi", [P, KT, SEQ], F32R)
    u_lo = place("u_lo", [P, KT, SEQ], F32R)
    a32 = base[0]
    base[0] += 32 * K
    raw = place("raw", [P, 2, 1024])
    w_hi = place("w_hi", [P, 4, 1024], F32R)
    w_lo = place("w_lo", [P, 4, 1024], F32R)
    ident = place("ident", [P, P])
    tri = place("tri", [P, P])
    strict = place("strict", [P, P])
    ones = place("ones", [P, P])
    par = place("par", [P, N_PAR])
    conv_half = place("conv_half", [P, 160])
    sc_half = place("sc_half", [P, 24])
    gate_half = place("gate_half", [P, 16])
    gate_slot = place("gate_slot", [P, 2])
    a_g = place("a_g", [P, TT, HPG])
    te_g = place("te_g", [P, TT, HPG])
    d_g = place("d_g", [P, HPG])
    nw_g = place("nw_g", [P, 2])
    shift = place("shift", [P, 8])
    scale1 = place("scale1", [P, 8])
    gate_col = place("gate_col", [P, 8])
    eps = place("eps", [P, 2])
    stats = place("stats", [P, 4, 2, 6])
    aggr = place("aggr", [P, 4, 2])
    rstd = place("rstd", [P, 4])
    d_row = place("d_row", [P, HEADS])
    dtb_row = place("dtb_row", [P, HEADS])
    exp_a = place("exp_a", [P, HEADS])
    a_t = place("a_t", [P, TT, HEADS])
    dt_t = place("dt_t", [P, TT, HEADS])
    decay_in = place("decay_in", [P, TT, HEADS])
    to_end = place("to_end", [P, TT, HEADS])
    chunk_decay = place("chunk_decay", [P, TT, HEADS])
    sq_sum = place("sq_sum", [P, TT])
    y_rstd = place("y_rstd", [P, TT])
    r0 = base[0]

    def in_r(name, shape, kb, dt=F32):
        return place(name, shape, dt, offset=r0 + int(kb * K))

    xt = place("xt", [P, TT, D], F32, offset=a32)
    wm = in_r("wm", [P, KT, 2048], 0)
    uf = in_r("uf", [P, 2, HALF], 64)
    rows = in_r("rows", [P, 2, P], 68)
    alog_row = in_r("alog_row", [P, HEADS], 69)
    wg = place("wg", [P, KT, 1024], F32, offset=a32)
    hb_hi = in_r("hb_hi", [P, KT, SEQ], 0, F32R)
    hb_lo = in_r("hb_lo", [P, KT, SEQ], 32, F32R)
    cv = in_r("cv", [P, SEQ], 64)
    sg = in_r("sg", [P, SEQ], 68)
    prod = in_r("prod", [P, SEQ + 2], 72)
    tgb = in_r("tgb", [P, SEQ], 64)
    mb = in_r("mb", [P, 2, SEQ], 68)
    ya = place("ya", [P, KT, SEQ], F32, offset=a32)
    bf = in_r("bf", [P, SEQ], 0)
    cf = in_r("cf", [P, SEQ], 4)
    xf = [in_r("xf0", [P, SEQ], 8), in_r("xf1", [P, SEQ], 12)]
    xs = in_r("xs", [P, TT, GW], 16)
    bt = in_r("bt", [P, TT, P], 24)
    th = in_r("th", [P, SEQ], 28)
    cin = in_r("cin", [P, SEQ + 3], 32)
    y = in_r("y", [P, TT, GW], 36.25)
    tri_a = in_r("tri_a", [P, HPG, P], 44.25)
    exp_s = in_r("exp_s", [P, HPG, P], 46.25)
    m_t = in_r("m_t", [P, HPG, P], 48.25)
    x_end = in_r("x_end", [P, GW], 50.25)
    dx = in_r("dx", [P, GW], 51.25)
    cbm = in_r("cbm", [P, P], 52.25)
    yt = in_r("yt", [P, GW], 52.75)
    state = in_r("state", [P, 2, GW], 53.75)
    tz = in_r("tz", [P, GW], 55.75)
    sz = in_r("sz", [P, GW], 56.75)
    sdec = in_r("sdec", [P, GW], 57.75)
    sqj = in_r("sqj", [P, GW], 58.75)
    y_hi = in_r("y_hi", [P, 2, SEQ], 59.75, F32R)
    y_lo = in_r("y_lo", [P, 2, SEQ], 67.75, F32R)
    dt_raw = in_r("dt_raw", [32, SEQ], 36.25)
    dtv = [in_r(f"dtv{k}", [P, TT, HEADS], 59.75 + k) for k in range(9)]
    mix_hi = in_r("mix_hi", [P, KT, SEQ], 0, F32R)
    mix_lo = place("mix_lo", [P, KT, SEQ], F32R, offset=a32)
    gate_b = in_r("gate_b", [P, D], 32)
    lng_b = in_r("lng_b", [P, D], 36)
    lnb_b = in_r("lnb_b", [P, D], 40)
    diag = in_r("diag", [P, KT, P], 44)
    mt = in_r("mt", [P, SEQ], 48)
    tga = in_r("tga", [P, SEQ], 52)
    mixb = in_r("mixb", [P, 2, SEQ], 56)
    xr = in_r("xr", [P, 2, D], 44)
    res = in_r("res", [P, D], 52)
    ob = in_r("ob", [P, 2, D], 56)
    stats_e = in_r("stats_e", [P, 2, 6], 64)
    aggr_e = in_r("aggr_e", [P, 2], 64.25)
    rstd_e = in_r("rstd_e", [P, 1], 64.5)
    wo_hi = place("wo_hi", [P, KT, D], F32R, offset=u_base)
    wo_lo = place("wo_lo", [P, KT, D], F32R, offset=u_base + 32 * K)

    dense = [nc.alloc_psum_tensor(f"dense{k}", [P, 512], F32) for k in range(4)]
    tb = nc.alloc_psum_tensor("tb", [P, 512], F32)
    seg = nc.alloc_psum_tensor("seg", [P, 512], F32)
    pb = nc.alloc_psum_tensor("pb", [P, 512], F32)
    yb = nc.alloc_psum_tensor("yb", [P, 512], F32)
    banks8 = dense + [tb, seg, pb, yb]

    S = nc.alloc_semaphore
    x_in = [S("x_in0"), S("x_in1")]
    wm_in = [S(f"wm_in{k}") for k in range(4)]
    wg_in = S("wg_in")
    rows_in = S("rows_in")
    heads_in = S("heads_in")
    w_in_s = [S("raw_in0"), S("raw_in1")]
    hi_done = S("hi_done")
    lo_done = S("lo_done")
    filled = S("filled")
    evac = [S(f"evac{k}") for k in range(4)]
    t_filled, t_free = S("t_filled"), S("t_free")
    seg_filled, seg_free = S("seg_filled"), S("seg_free")
    p_filled, p_free = S("p_filled"), S("p_free")
    y_filled, y_free = S("y_filled"), S("y_free")
    consts = S("consts")
    par_ready = S("par_ready")
    ln_s = S("ln_steps")
    ln_sqrt = S("ln_sqrt")
    mod_s = S("mod_steps")
    uhi_s = S("u_hi_written")
    ulo_s = S("u_lo_written")
    sc_s = S("sc_steps")
    sc_tanh = S("sc_tanh")
    gslot_s = S("gate_slot_written")
    gpar_s = S("group_params")
    stored = [S("mb_stored0"), S("mb_stored1")]
    dts = S("dt_steps")
    dta = S("dt_act_steps")
    ya_zero = S("ya_zeroed")
    conv_s = S("conv_steps")
    conv_tanh = S("conv_tanh")
    yhi_s = S("y_hi_written")
    tria_s, xend_s, dx_s = S("tri_a_ready"), S("x_end_ready"), S("dx_ready")
    ssd_s = S("ssd_steps")
    z_tanh = S("z_tanh")
    comb_s = S("combine_steps")
    sq_s = S("squares")
    rms_s = S("rms_sqrt")
    yn_s = S("y_normed")
    mixb_in = [S("mixb_in0"), S("mixb_in1")]
    mix_s = S("mix_steps")
    mixhi_s = S("mix_hi_written")
    diag_s, gateb_s = S("diag_ready"), S("gate_b_ready")
    nw_s = S("norm_weight_slot")
    lnp_in = S("ln_params_in")
    xr_in = [S("xr_in0"), S("xr_in1")]
    e_filled, e_evac = S("out_filled"), S("out_evacuated")
    fin_s, fin_sqrt, aff_s = S("final_steps"), S("final_sqrt"), S("affine_steps")
    out_s = [S("out_stored0"), S("out_stored1")]

    def bank_of(q):
        return at(q).mod(4)

    def use_of(q):
        return at(q).over(4) if at(q).k else Lin(at(q).c // 4)

    def w_cols(w, col, width=P):
        v = at(col)
        cols = w[:, v.c:v.c + width] if v.k == 0 else w[:, bass.ds(nc.sync.snap(v.val()), width)]
        return cols.rearrange("(k p) f -> p k f", p=P)

    def w_rows(w, row_tile):
        v = at(row_tile) * P
        return w[v.c:v.c + P, :] if v.k == 0 else w[bass.ds(nc.sync.snap(v.val()), P), :]

    def col(t, j, n=1):
        v = at(j)
        return t[:, v.c:v.c + n] if v.k == 0 else t[:, bass.ds(v.val(), n)]

    def heads_of(t, ck, g):
        v = at(g) * HPG
        return t[:, ck, v.c:v.c + HPG] if v.k == 0 else t[:, ck, bass.ds(v.val(), HPG)]

    def head_col(t, ck, g, h):
        v = at(g) * HPG + h
        return t[:, ck, v.c:v.c + 1] if v.k == 0 else t[:, ck, bass.ds(v.val(), 1)]

    def tile_of(t, f):
        v = at(f)
        return t[:, v.c, :] if v.k == 0 else t[:, bass.ds(v.val(), 1), :].rearrange("p a n -> p (a n)")

    win, wmod, wgate = w_in[0], w_mod[0], w_gate[0]
    wa, wb, wout = w_branch_a[0], w_branch_b[0], w_out[0]

    def units_b(g):
        if at(g).k == 0 and at(g).c == 0:
            return Lin(U_B0), Lin(Q_B0), Lin(3)
        g1 = at(g) + (-1)
        return g1 * 8 + U_B, g1 * 32 + Q_B, g1 * 10 + 9

    with nc.Block() as block:

        @block.sync
        def _(sp):
            def load(n, src):
                n = at(n)
                wait(sp, lo_done, n + (-1))
                dst = raw[:, n.mod(2), :]
                if len(src.shape) == 3:
                    dst = dst.rearrange("p (k f) -> p k f", k=KT)
                sp.dma_start(dst, src).then_inc(w_in_s[n.mod(2)], 16)

            for t in range(2):
                sp.dma_start(xt[:, 4 * t:4 * t + 4, :],
                             x[0, 512 * t:512 * (t + 1), :].rearrange("(t p) d -> p t d", p=P)
                             ).then_inc(x_in[t], 16)
            for k in (0, 2, 1, 3):
                sp.dma_start(wm[:, :, 512 * k:512 * (k + 1)],
                             w_cols(wmod, 512 * k, 512)).then_inc(wm_in[k], 16)

            def sc_units(b):
                for j, start in enumerate((SCC_COL, SCX_COL, SCG_COL, SCB_COL)):
                    load(b * 4 + U_C + j, w_cols(win, b * P + start))
                    if b.k == 0 and j == 3:
                        sp.wait_ge(filled, 16)
                        sp.dma_start(wg[:], w_cols(wmod, 2048, 1024)).then_inc(wg_in, 16)

            run(sp, sc_units, 0, 8, peel=1)

            def c2_units(f):
                for j in range(2):
                    load(f * 2 + U_C2 + 2 * j, w_cols(wgate, f * P + D + j * P))
                    load(f * 2 + U_C2 + 2 * j + 1, w_cols(wb, f * P + j * P))

            for f in range(0, 8, 2):
                c2_units(Lin(f))
            load(U_DT, w_cols(win, DT_COL))

            def group_units(g):
                n0, _, _ = units_b(g)
                first = g.k == 0
                load(n0, w_cols(win, g * P + B_COL))
                load(n0 + 1, w_cols(win, g * P + C_COL))
                load(n0 + 2, w_cols(win, g * GW + XB_COL))
                load(n0 + 3, w_cols(win, g * GW + XB_COL + P))
                if not first:
                    load(n0 + 4, w_rows(wa, g * 2 + (-2)))
                    load(n0 + 5, w_rows(wa, g * 2 + (-1)))
                zn = n0 + (4 if first else 6)
                load(zn, w_cols(win, g * GW))
                load(zn + 1, w_cols(win, g * GW + P))

            run(sp, group_units, 0, GROUPS, peel=1)
            load(U_TAIL, w_rows(wa, 14))
            load(U_TAIL + 1, w_rows(wa, 15))

            load(U_D, w_cols(wgate, 0))
            load(U_D + 1, w_cols(wgate, P))
            sp.wait_ge(filled, Q_D)
            sp.wait_ge(stored[0], 64)
            sp.wait_ge(stored[1], 64)
            sp.dma_start(lng_b[:], ln_g.partition_broadcast(P).rearrange("p a d -> p (a d)")).then_inc(lnp_in, 16)
            sp.dma_start(lnb_b[:], ln_b.partition_broadcast(P).rearrange("p a d -> p (a d)")).then_inc(lnp_in, 16)
            for f in range(KT):
                if f >= 2:
                    sp.wait_ge(mix_s, 3 * (f - 2) + 2)
                sp.dma_start(mixb[:, f % 2, :], spill[f]).then_inc(mixb_in[f % 2], 16)
                if f + 2 < KT:
                    load(U_D + f + 2, w_cols(wgate, (f + 2) * P))
            for k in range(2):
                load(U_E + k, w_rows(wout, k))
            sp.wait_ge(mix_s, 3 * KT)
            sp.wait_ge(gateb_s, 2)
            for t in range(2):
                sp.dma_start(xr[:, t, :], x[0, P * t:P * (t + 1), :]).then_inc(xr_in[t], 16)
            for k in range(2, KT):
                load(U_E + k, w_rows(wout, k))
            for t in range(TT):
                sp.wait_ge(aff_s, 2 * (t + 1))
                sp.dma_start(out[0, P * t:P * (t + 1), :], ob[:, t % 2, :]).then_inc(out_s[t % 2], 16)
                if t + 2 < TT:
                    sp.dma_start(xr[:, t % 2, :], x[0, P * (t + 2):P * (t + 3), :]).then_inc(xr_in[t % 2], 16)
            sp.wait_ge(out_s[0], 64)
            sp.wait_ge(out_s[1], 64)

        @block.scalar
        def _(act):
            nc_act = nc.scalar

            def split_hi(n, done):
                n = at(n)
                wait(act, w_in_s[n.mod(2)], (n.over(2) if n.k else Lin(n.c // 2)) * 16 + 16)
                wait(act, filled, done)
                nc_act.copy(w_hi[:, n.mod(4), :], raw[:, n.mod(2), :]).then_inc(hi_done, 1)

            act.dma_start(rows[:, 0, :], conv_ssm_w.rearrange("a t (b p) -> (a t b) p", p=P)).then_inc(rows_in, 16)
            r = 0
            for src in (conv_ssm_b.rearrange("a (b p) -> (a b) p", p=P),
                        conv_sc_w.rearrange("a t (b p) -> (a t b) p", p=P),
                        b_mod.rearrange("a (b p) -> (a b) p", p=P),
                        b_gate.rearrange("a (b p) -> (a b) p", p=P),
                        ssm_norm_w.rearrange("a (b p) -> (a b) p", p=P),
                        c.rearrange("a (b p) -> (a b) p", p=P)):
                act.dma_start(rows[r:r + src.shape[0], 1, :], src).then_inc(rows_in, 16)
                r += src.shape[0]
            for dst, src in ((dtb_row, dt_bias), (alog_row, a_log), (d_row, d_skip)):
                act.dma_start(dst[:], src.partition_broadcast(P).rearrange("p a d -> p (a d)")).then_inc(heads_in, 16)

            act.wait_ge(t_filled, 1)
            nc_act.copy(par[:], tb[:, 0:N_PAR]).then_inc(t_free, 1)
            act.wait_ge(consts, 6)
            for t in range(2):
                act.wait_ge(ln_s, 17 * t + 12)
                nc_act.activation(rstd[:], aggr[:, :, 1], ACT.Sqrt, bias=eps[:, 0:1]).then_inc(ln_sqrt, 1)
            for n in range(4):
                split_hi(n, 0)
            act.wait_ge(heads_in, 48)
            nc_act.activation(exp_a[:], alog_row[:], ACT.Exp).then_inc(dta, 1)
            for q in range(16):
                kt, t = q % 8, q // 8
                act.wait_ge(evac[q % 4], q // 4 + 1)
                nc_act.copy(u_hi[:, kt, HALF * t:HALF * (t + 1)], uf[:, q % 2, :]).then_inc(uhi_s, 1)

            def sc_block(b):
                n, q = b * 4 + U_C, b * 8 + Q_C
                for t in range(2):
                    if t == 0:
                        wait(act, sc_s, b * 6)
                    wait(act, filled, q + t + 1)
                    nc_act.copy(cv[:, HALF * t:HALF * (t + 1)],
                                dense[bank_of(q + t)][:]).then_inc(evac[bank_of(q + t)], 1)
                split_hi(n + 4, q + 2)
                split_hi(n + 5, q + 4)
                for t in range(2):
                    wait(act, filled, q + 4 + t + 1)
                    nc_act.activation(sg[:, HALF * t:HALF * (t + 1)], dense[bank_of(q + 4 + t)][:],
                                      ACT.Tanh, scale=0.5).then_inc(sc_tanh, 1)
                split_hi(n + 6, q + 6)
                split_hi(n + 7, q + 8)

            run(act, sc_block, 0, 8, peel=1)

            def store_mb(f, j):
                q = f * 4 + Q_C2 + 2
                for t in range(2):
                    wait(act, evac[bank_of(q + t)], use_of(q + t) + 1)
                dst = spill[f.c] if f.k == 0 else spill[bass.ds(f.val(), 1)].rearrange("a p n -> (a p) n")
                act.dma_start(dst, mb[:, j, :]).then_inc(stored[j], 16)

            def c2_pair(f):
                for j in range(2):
                    n, q = f * 2 + U_C2 + 2 * j, f * 4 + Q_C2 + 4 * j
                    if j == 0:
                        wait(act, gslot_s, f.over(2) + 1 if f.k else 1)
                    if j or f.k:
                        store_mb(f + (j - 1), 1 - j)
                    for t in range(2):
                        if j == 0 and t == 0 and f.k == 0:
                            act.wait_ge(sc_s, 48)
                        wait(act, filled, q + t + 1)
                        wait(act, evac[bank_of(q + t + 2)], use_of(q + t + 2))
                        nc_act.activation(tgb[:, HALF * t:HALF * (t + 1)], dense[bank_of(q + t)][:],
                                          ACT.Tanh, scale=0.5, bias=gate_slot[:, j:j + 1]
                                          ).then_inc(evac[bank_of(q + t)], 1)
                    split_hi(n + 4, q + 2)
                    split_hi(n + 5, q + 4)

            run(act, c2_pair, 0, 8, step=2, peel=1)
            store_mb(Lin(7), 1)

            for t in range(2):
                act.wait_ge(filled, Q_DT + t + 1)
                nc_act.copy(dt_raw[:, HALF * t:HALF * (t + 1)],
                            dense[(Q_DT + t) % 4][0:32, :]).then_inc(evac[(Q_DT + t) % 4], 1)
            split_hi(U_DT + 4, Q_DT + 2)

            def dt_acts():
                act.wait_ge(dts, 1)
                nc_act.activation(dtv[2][:], dtv[1][:], ACT.Exp, scale=-1.0).then_inc(dta, 1)
                act.wait_ge(dts, 2)
                nc_act.activation(dtv[4][:], dtv[3][:], ACT.Ln).then_inc(dta, 1)

            def decay_acts():
                act.wait_ge(t_filled, 3)
                flat = "p c h -> p (c h)"
                nc_act.activation(decay_in[:].rearrange(flat), tb[:, 0:256], ACT.Exp).then_inc(dta, 1)
                nc_act.activation(to_end[:].rearrange(flat), tb[:, 256:512], ACT.Exp).then_inc(t_free, 1)
                act.wait_ge(p_filled, 3)
                nc_act.activation(chunk_decay[:].rearrange(flat), pb[:, 0:256], ACT.Exp).then_inc(p_free, 1)

            def group(g):
                first = g.k == 0
                n0, q0, t0 = units_b(g)
                conv0 = g * 20
                tt = [0]

                def evac_half(u, t):
                    q = q0 + 2 * u + t
                    if t == 0:
                        wait(act, conv_s, conv0 + (5 * u - 1))
                    wait(act, filled, q + 1)
                    nc_act.copy(cin[:, 3 + HALF * t:3 + HALF * (t + 1)],
                                dense[bank_of(q)][:]).then_inc(evac[bank_of(q)], 1)

                def tanh(u):
                    src = (bf, cf, xf[0], xf[1])[u]
                    wait(act, conv_s, conv0 + (5 * u + 4))
                    nc_act.activation(th[:], src[:], ACT.Tanh).then_inc(conv_tanh, 1)

                def y_hi_part():
                    k = tt[0]
                    if k == 0:
                        wait(act, nw_s, g)
                    t, j = k // 2, k % 2
                    wait(act, t_filled, t0 + k + 1)
                    nc_act.activation(y_hi[:, j, HALF * t:HALF * (t + 1)], tb[:], ACT.Copy,
                                      scale=nw_g[:, j:j + 1]).then_inc(yhi_s, 1)
                    tt[0] += 1

                evac_half(0, 0)
                evac_half(0, 1)
                split_hi(n0 + 4, q0 + 2)
                if first:
                    dt_acts()
                else:
                    y_hi_part()
                tanh(0)
                evac_half(1, 0)
                if not first:
                    y_hi_part()
                evac_half(1, 1)
                split_hi(n0 + 5, q0 + 4)
                if first:
                    decay_acts()
                else:
                    y_hi_part()
                tanh(1)
                evac_half(2, 0)
                if not first:
                    y_hi_part()
                evac_half(2, 1)
                split_hi(n0 + 6, q0 + 6)
                tanh(2)
                evac_half(3, 0)
                evac_half(3, 1)
                split_hi(n0 + 7, q0 + 8)
                tanh(3)
                k0 = 0 if first else 4
                for k in range(6):
                    wait(act, t_filled, t0 + (k0 + k + 1))
                    src = tb[:].rearrange("p (c n) -> p c n", c=4)
                    cs = slice(4 * (k % 2), 4 * (k % 2) + 4)
                    dst = bt[:, cs, :] if k < 2 else xs[:, cs, P * (k // 2 - 1):P * (k // 2)]
                    nc_act.copy(dst, src).then_inc(t_free, 1)
                if not first:
                    split_hi(n0 + 8, q0 + 24)
                    split_hi(n0 + 9, q0 + 24)
                zq = q0 + (8 if first else 24)
                item = g * 8

                def square(ck):
                    wait(act, comb_s, (item + (ck + 1)) * 4)
                    if ck:
                        wait(act, sq_s, item + ck)
                    nc_act.activation(sqj[:], y[:, ck, :], ACT.Square,
                                      accum_out=sq_sum[:, ck:ck + 1]).then_inc(sq_s, 1)

                for ck in range(TT):
                    wait(act, seg_filled, item + (ck + 1))
                    wait(act, ssd_s, (item + ck) * 6)
                    nc_act.activation(exp_s[:].rearrange("p h l -> p (h l)"), seg[:], ACT.Exp).then_inc(seg_free, 1)
                    if ck:
                        square(ck - 1)
                    wait(act, filled, zq + (ck + 1))
                    if ck:
                        wait(act, evac[bank_of(zq + (ck - 1))], use_of(zq + (ck - 1)) + 1)
                    nc_act.activation(tz[:], dense[bank_of(zq + ck)][:, 0:GW], ACT.Tanh,
                                      scale=0.5).then_inc(z_tanh, 1)
                square(TT - 1)
                wait(act, sq_s, item + 8)
                nc_act.activation(y_rstd[:], sq_sum[:], ACT.Sqrt, bias=eps[:, 1:2],
                                  scale=1.0 / GW).then_inc(rms_s, 1)
                split_hi(n0 + (8 if first else 10), zq + 8)
                split_hi(n0 + (9 if first else 11), zq + 8)

            run(act, group, 0, GROUPS, peel=1)

            for k in range(4):
                t, j = k // 2, k % 2
                act.wait_ge(t_filled, 79 + k + 1)
                nc_act.activation(y_hi[:, j, HALF * t:HALF * (t + 1)], tb[:], ACT.Copy,
                                  scale=par[:, NORM_W + 14 + j:NORM_W + 15 + j]).then_inc(yhi_s, 1)
            split_hi(U_TAIL + 4, Q_D)
            split_hi(U_TAIL + 5, Q_D)
            for f in range(KT):
                for t in range(2):
                    q = Q_D + 2 * f + t
                    act.wait_ge(filled, q + 1)
                    if t == 0 and f:
                        act.wait_ge(mix_s, 3 * f - 2)
                    nc_act.activation(tga[:, HALF * t:HALF * (t + 1)], dense[q % 4][:], ACT.Tanh, scale=0.5,
                                      bias=gate_half[:, f:f + 1]).then_inc(evac[q % 4], 1)
                if f < 4:
                    split_hi(U_D + f + 4, Q_D + 2 * f + 2)
                if f == 2:
                    for b, bank in enumerate((tb, seg)):
                        act.wait_ge((t_filled, seg_filled)[b], (84, 65)[b])
                        nc_act.copy(gate_b[:, 512 * b:512 * (b + 1)], bank[:]).then_inc(gateb_s, 1)
                act.wait_ge(mix_s, 3 * f + 2)
                nc_act.copy(mix_hi[:, f, :], mt[:]).then_inc(mixhi_s, 1)
            for k in range(KT):
                n = U_E + k
                act.wait_ge(filled, Q_END)
                act.wait_ge(w_in_s[n % 2], 16 * (n // 2 + 1))
                nc_act.copy(wo_hi[:, k, :], raw[:, n % 2, :]).then_inc(hi_done, 1)
            for t in range(TT):
                act.wait_ge(fin_s, 8 * t + 6)
                nc_act.activation(rstd_e[:], aggr_e[:, 1:2], ACT.Sqrt, bias=eps[:, 0:1]).then_inc(fin_sqrt, 1)

        @block.gpsimd
        def _(pool):
            g_ = nc.gpsimd
            g_.memset(ones[:], 1.0).then_inc(consts, 1)
            g_.memset(eps[:, 0:1], LN_EPS).then_inc(consts, 1)
            g_.memset(eps[:, 1:2], 4 * RMS_EPS).then_inc(consts, 1)
            pool.wait_ge(consts, 3)
            g_.affine_select(out=ident[:], in_=ones[:], compare_op=ALU.is_equal, fill=0.0, base=0,
                             pattern=[[-1, P]], channel_multiplier=1).then_inc(consts, 1)
            g_.affine_select(out=tri[:], in_=ones[:], compare_op=ALU.is_ge, fill=0.0, base=0,
                             pattern=[[1, P]], channel_multiplier=-1).then_inc(consts, 1)
            g_.affine_select(out=strict[:], in_=ones[:], compare_op=ALU.is_gt, fill=0.0, base=0,
                             pattern=[[-1, P]], channel_multiplier=1).then_inc(consts, 1)

            def split_lo(n, dst=None):
                n = at(n)
                wait(pool, hi_done, n + 1)
                hi = w_hi[:, n.mod(4), :] if dst is None else wo_hi[:, dst, :]
                lo = w_lo[:, n.mod(4), :] if dst is None else wo_lo[:, dst, :]
                g_.tensor_tensor(lo, raw[:, n.mod(2), :], hi, ALU.subtract).then_inc(lo_done, 1)

            def four(n):
                for j in range(4):
                    split_lo(n + j)

            for n in range(4):
                split_lo(n)
            pool.wait_ge(ulo_s, 16)
            g_.memset(prod[:, 0:2], 0.0).then_inc(consts, 1)
            run(pool, four, 4, U_DT, step=4)
            pool.wait_ge(p_filled, 2)
            g_.memset(ya[:], 0.0).then_inc(ya_zero, 1)
            for n in range(U_DT, U_DT + 4):
                split_lo(n)
            pool.wait_ge(filled, Q_DT)
            g_.memset(cin[:, 0:3], 0.0).then_inc(consts, 1)
            split_lo(U_DT + 4)

            def group(g):
                first = g.k == 0
                n0, q0, _ = units_b(g)
                for j in range(4):
                    split_lo(n0 + 4 + j)
                item = g * 8
                xs_ready = units_b(g)[2] + (6 if first else 10)
                for ck in range(TT):
                    if not first and ck == 2:
                        split_lo(n0 + 8)
                        split_lo(n0 + 9)
                    if ck == 0:
                        wait(pool, gpar_s, g * 3 + 3)
                    wait(pool, seg_filled, item + ck)
                    g_.tensor_tensor(tri_a[:], tri[:].unsqueeze(1).broadcast_to([P, HPG, P]),
                                     a_g[:, ck, :].unsqueeze(2).broadcast_to([P, HPG, P]),
                                     ALU.mult).then_inc(tria_s, 1)
                    if ck == 0:
                        wait(pool, t_free, xs_ready)
                    x4 = xs[:, ck, :].rearrange("p (h d) -> p h d", h=HPG)
                    if ck < TT - 1:
                        wait(pool, p_filled, item + ck + 3)
                        g_.tensor_tensor(x_end[:].rearrange("p (h d) -> p h d", h=HPG), x4,
                                         te_g[:, ck, :].unsqueeze(2).broadcast_to([P, HPG, HD]),
                                         ALU.mult).then_inc(xend_s, 1)
                    wait(pool, comb_s, (item + ck) * 4)
                    g_.tensor_tensor(dx[:].rearrange("p (h d) -> p h d", h=HPG), x4,
                                     d_g[:].unsqueeze(2).broadcast_to([P, HPG, HD]), ALU.mult).then_inc(dx_s, 1)
                e = 8 if first else 10
                split_lo(n0 + e)
                split_lo(n0 + e + 1)

            run(pool, group, 0, GROUPS, peel=1)
            for n in range(U_TAIL + 4, U_E):
                split_lo(n)
            for k in range(KT):
                split_lo(U_E + k, dst=k)
            pool.wait_ge(lnp_in, 32)
            for t in range(TT):
                pool.wait_ge(fin_s, 8 * t + 8)
                g_.tensor_tensor(ob[:, t % 2, :], ob[:, t % 2, :], lng_b[:], ALU.mult).then_inc(aff_s, 1)
                pool.wait_ge(aff_s, 2 * t + 1)
                g_.tensor_tensor(ob[:, t % 2, :], ob[:, t % 2, :], lnb_b[:], ALU.add).then_inc(aff_s, 1)

        @block.vector
        def _(dve):
            v = nc.vector
            for t in range(2):
                dve.wait_ge(x_in[t], 16)
                for j in range(4):
                    for k in range(2):
                        v.bn_stats(stats[:, j, k, :], xt[:, 4 * t + j, 512 * k:512 * (k + 1)]).then_inc(ln_s, 1)
                if t:
                    dve.wait_ge(ln_s, 17)
                for j in range(4):
                    dve.wait_ge(ln_s, 17 * t + 8)
                    v.bn_aggr(aggr[:, j, :], stats[:, j, :, :].rearrange("p a b -> p (a b)")).then_inc(ln_s, 1)
                dve.wait_ge(ln_sqrt, t + 1)
                v.reciprocal(rstd[:], rstd[:]).then_inc(ln_s, 1)
                dve.wait_ge(ln_s, 17 * t + 13)
                for j in range(4):
                    v.tensor_scalar(xt[:, 4 * t + j, :], xt[:, 4 * t + j, :], aggr[:, j, 0:1], rstd[:, j:j + 1],
                                    ALU.subtract, ALU.mult).then_inc(ln_s, 1)
            dve.wait_ge(t_free, 1)
            v.tensor_scalar(conv_half[:], par[:, 0:160], 0.5, None, ALU.mult).then_inc(par_ready, 1)
            v.tensor_scalar(sc_half[:], par[:, SC_W:SC_W + 24], 0.5, None, ALU.mult).then_inc(par_ready, 1)
            v.tensor_scalar(gate_half[:], par[:, B_GATE:B_GATE + 16], 0.5, None, ALU.mult).then_inc(par_ready, 1)
            dve.wait_ge(p_filled, 1)
            v.tensor_tensor(shift[:], pb[:, 0:8], par[:, B_MOD:B_MOD + 8], ALU.add).then_inc(mod_s, 1)
            v.scalar_tensor_tensor(out=scale1[:], in0=pb[:, 8:16], scalar=1.0, in1=par[:, B_MOD + 8:B_MOD + 16],
                                   op0=ALU.add, op1=ALU.add).then_inc(p_free, 1)
            dve.wait_ge(mod_s, 1)
            dve.wait_ge(p_free, 1)

            def u_low(q):
                kt, t = q % 8, q // 8
                dve.wait_ge(uhi_s, q + 1)
                v.tensor_tensor(u_lo[:, kt, HALF * t:HALF * (t + 1)], uf[:, q % 2, :],
                                u_hi[:, kt, HALF * t:HALF * (t + 1)], ALU.subtract).then_inc(ulo_s, 1)

            for q in range(16):
                kt = q % 8
                dve.wait_ge(filled, q + 1)
                if q >= 2:
                    dve.wait_ge(ulo_s, q - 1)
                v.tensor_scalar(uf[:, q % 2, :], dense[q % 4][:], scale1[:, kt:kt + 1], shift[:, kt:kt + 1],
                                ALU.mult, ALU.add).then_inc(evac[q % 4], 1)
                if q:
                    u_low(q - 1)
            u_low(15)

            def sc_block(b):
                q = b * 8 + Q_C
                if b.k == 0:
                    dve.wait_ge(consts, 7)
                    dve.wait_ge(par_ready, 3)
                for t in range(2):
                    wait(dve, evac[bank_of(q + t)], use_of(q + t) + 1)
                    wait(dve, filled, q + 2 + t + 1)
                    v.tensor_tensor(prod[:, 2 + HALF * t:2 + HALF * (t + 1)], cv[:, HALF * t:HALF * (t + 1)],
                                    dense[bank_of(q + 2 + t)][:], ALU.mult).then_inc(evac[bank_of(q + 2 + t)], 1)
                for t in range(2):
                    wait(dve, evac[bank_of(q + 2 + t)], use_of(q + 2 + t) + 1)
                v.tensor_scalar(cv[:], prod[:, 2:2 + SEQ], col(sc_half, b + 16), None, ALU.mult).then_inc(sc_s, 1)
                for k in (1, 0):
                    wait(dve, sc_s, b * 6 + (2 - k))
                    v.scalar_tensor_tensor(out=cv[:], in0=prod[:, k:k + SEQ], scalar=col(sc_half, b + 8 * k),
                                           in1=cv[:], op0=ALU.mult, op1=ALU.add).then_inc(sc_s, 1)
                for t in range(2):
                    h = slice(HALF * t, HALF * (t + 1))
                    wait(dve, sc_tanh, b * 2 + (t + 1))
                    v.scalar_tensor_tensor(out=sg[:, h], in0=sg[:, h], scalar=1.0, in1=dense[bank_of(q + 4 + t)][:],
                                           op0=ALU.add, op1=ALU.mult).then_inc(evac[bank_of(q + 4 + t)], 1)
                for t in range(2):
                    h = slice(HALF * t, HALF * (t + 1))
                    wait(dve, evac[bank_of(q + 4 + t)], use_of(q + 4 + t) + 1)
                    wait(dve, filled, q + 6 + t + 1)
                    v.tensor_tensor(sg[:, h], sg[:, h], dense[bank_of(q + 6 + t)][:],
                                    ALU.mult).then_inc(evac[bank_of(q + 6 + t)], 1)
                for t in range(2):
                    wait(dve, evac[bank_of(q + 6 + t)], use_of(q + 6 + t) + 1)
                wait(dve, sc_s, b * 6 + 3)
                v.tensor_tensor(cv[:], cv[:], sg[:], ALU.mult).then_inc(sc_s, 1)
                wait(dve, sc_s, b * 6 + 4)
                v.tensor_scalar(tile_of(hb_hi, b), cv[:], 1.0, None, ALU.mult).then_inc(sc_s, 1)
                wait(dve, sc_s, b * 6 + 5)
                v.tensor_tensor(tile_of(hb_lo, b), cv[:], tile_of(hb_hi, b), ALU.subtract).then_inc(sc_s, 1)

            run(dve, sc_block, 0, 8, peel=1)

            dve.wait_ge(p_filled, 2)
            v.scalar_tensor_tensor(out=gate_col[:], in0=pb[:, 0:8], scalar=1.0, in1=par[:, B_MOD + 16:B_MOD + 24],
                                   op0=ALU.mult, op1=ALU.add).then_inc(p_free, 1)

            def c2_pair(f):
                v.tensor_scalar(gate_slot[:], col(gate_half, f + 8, 2), 1.0, None, ALU.mult).then_inc(gslot_s, 1)
                for j in range(2):
                    q = f * 4 + Q_C2 + 4 * j
                    if f.k:
                        wait(dve, stored[j], (f.over(2)) * 16)
                    for t in range(2):
                        h = slice(HALF * t, HALF * (t + 1))
                        wait(dve, evac[bank_of(q + t)], use_of(q + t) + 1)
                        wait(dve, filled, q + 2 + t + 1)
                        v.scalar_tensor_tensor(out=mb[:, j, h], in0=tgb[:, h], scalar=1.0,
                                               in1=dense[bank_of(q + 2 + t)][:], op0=ALU.add,
                                               op1=ALU.mult).then_inc(evac[bank_of(q + 2 + t)], 1)

            run(dve, c2_pair, 0, 8, step=2, peel=1)

            def dt_steps():
                bc = dtb_row[:].unsqueeze(1).broadcast_to([P, TT, HEADS])
                dve.wait_ge(t_filled, 2)
                dve.wait_ge(heads_in, 48)
                v.tensor_tensor(dtv[0][:], tb[:, 0:256].rearrange("p (c h) -> p c h", c=TT), bc,
                                ALU.add).then_inc(t_free, 1)
                dve.wait_ge(t_free, 2)
                v.scalar_tensor_tensor(out=dtv[1][:], in0=dtv[0][:], scalar=-1.0, in1=dtv[0][:],
                                       op0=ALU.mult, op1=ALU.max).then_inc(dts, 1)
                dve.wait_ge(dta, 2)
                v.tensor_scalar(dtv[3][:], dtv[2][:], 1.0, None, ALU.add).then_inc(dts, 1)
                dve.wait_ge(dts, 2)
                v.tensor_scalar(dtv[5][:], dtv[3][:], -1.0, None, ALU.add).then_inc(dts, 1)
                dve.wait_ge(dts, 3)
                v.tensor_tensor(dtv[6][:], dtv[2][:], dtv[5][:], ALU.subtract).then_inc(dts, 1)
                v.reciprocal(dtv[7][:], dtv[3][:]).then_inc(dts, 1)
                dve.wait_ge(dts, 5)
                v.tensor_tensor(dtv[6][:], dtv[6][:], dtv[7][:], ALU.mult).then_inc(dts, 1)
                v.tensor_scalar(dtv[8][:], dtv[0][:], 0.0, None, ALU.max).then_inc(dts, 1)
                dve.wait_ge(dts, 7)
                v.tensor_tensor(dtv[8][:], dtv[8][:], dtv[6][:], ALU.add).then_inc(dts, 1)
                dve.wait_ge(dts, 8)
                dve.wait_ge(dta, 3)
                v.tensor_tensor(dt_t[:], dtv[8][:], dtv[4][:], ALU.add).then_inc(dts, 1)
                dve.wait_ge(dts, 9)
                v.scalar_tensor_tensor(out=a_t[:], in0=dt_t[:], scalar=-1.0,
                                       in1=exp_a[:].unsqueeze(1).broadcast_to([P, TT, HEADS]),
                                       op0=ALU.mult, op1=ALU.mult).then_inc(dts, 1)

            def y_lo_part(g, t0, k):
                t, j = k // 2, k % 2
                h = slice(HALF * t, HALF * (t + 1))
                wait(dve, yhi_s, (g + (-1)) * 4 + (k + 1))
                v.scalar_tensor_tensor(out=y_lo[:, j, h], in0=tb[:], scalar=col(par, g * 2 + (NORM_W - 2 + j)),
                                       in1=y_hi[:, j, h], op0=ALU.mult, op1=ALU.subtract).then_inc(t_free, 1)

            def add_ya(q, s):
                t, f = s // 8, s % 8
                h = slice(HALF * t, HALF * (t + 1))
                wait(dve, filled, q + 1)
                v.tensor_tensor(ya[:, f, h], ya[:, f, h], dense[bank_of(q)][:],
                                ALU.add).then_inc(evac[bank_of(q)], 1)

            def group(g):
                first = g.k == 0
                n0, q0, t0 = units_b(g)
                conv0 = g * 20

                def group_params():
                    v.tensor_scalar(a_g[:], heads_of(a_t, slice(None), g), 1.0, None, ALU.mult).then_inc(gpar_s, 1)
                    v.tensor_scalar(te_g[:], heads_of(to_end, slice(None), g), 1.0, None, ALU.mult).then_inc(gpar_s, 1)
                    v.tensor_scalar(d_g[:], col(d_row, g * HPG, HPG), 1.0, None, ALU.mult).then_inc(gpar_s, 1)

                if not first:
                    v.tensor_scalar(nw_g[:], col(par, g * 2 + (NORM_W - 2), 2), 1.0, None, ALU.mult).then_inc(nw_s, 1)
                    group_params()
                if first:
                    dve.wait_ge(stored[0], 64)
                    dve.wait_ge(stored[1], 64)
                    dve.wait_ge(consts, 8)
                    dve.wait_ge(ya_zero, 1)

                def taps(u):
                    dst = (bf, cf, xf[0], xf[1])[u]
                    blk = (g + 16, g + 24, g * 2, g * 2 + 1)[u]
                    for t in range(2):
                        q = q0 + 2 * u + t
                        wait(dve, evac[bank_of(q)], use_of(q) + 1)
                    v.tensor_scalar(dst[:], cin[:, 3:3 + SEQ], col(conv_half, blk + 96), col(conv_half, blk + 128),
                                    ALU.mult, ALU.add).then_inc(conv_s, 1)
                    for k in (2, 1, 0):
                        wait(dve, conv_s, conv0 + (5 * u + 3 - k))
                        v.scalar_tensor_tensor(out=dst[:], in0=cin[:, k:k + SEQ], scalar=col(conv_half, blk + 32 * k),
                                               in1=dst[:], op0=ALU.mult, op1=ALU.add).then_inc(conv_s, 1)

                def silu(u):
                    dst = (bf, cf, xf[0], xf[1])[u]
                    wait(dve, conv_tanh, g * 4 + (u + 1))
                    v.scalar_tensor_tensor(out=dst[:], in0=th[:], scalar=1.0, in1=dst[:],
                                           op0=ALU.add, op1=ALU.mult).then_inc(conv_s, 1)

                if first:
                    dt_steps()
                    taps(0)
                    silu(0)
                    dve.wait_ge(t_free, 3)
                    v.tensor_tensor(to_end[:], to_end[:], dt_t[:], ALU.mult).then_inc(dts, 1)
                    dve.wait_ge(dts, 11)
                    group_params()
                    taps(1)
                    silu(1)
                    taps(2)
                    silu(2)
                    taps(3)
                    silu(3)
                else:
                    taps(0)
                    y_lo_part(g, t0, 0)
                    silu(0)
                    y_lo_part(g, t0, 1)
                    taps(1)
                    y_lo_part(g, t0, 2)
                    silu(1)
                    y_lo_part(g, t0, 3)
                    taps(2)
                    silu(2)
                    taps(3)
                    add_ya(q0 + 8, 0)
                    silu(3)
                    for s in range(1, 16):
                        add_ya(q0 + (8 + s), s)
                zq = q0 + (8 if first else 24)
                item = g * 8

                def combine(ck):
                    k = (item + ck) * 4
                    wait(dve, dx_s, item + (ck + 1))
                    wait(dve, y_filled, item + (ck + 1))
                    wait(dve, comb_s, k)
                    add = dx
                    if ck:
                        v.tensor_tensor(yt[:].rearrange("p (h d) -> p h d", h=HPG),
                                        yb[:, 0:GW].rearrange("p (h d) -> p h d", h=HPG),
                                        heads_of(decay_in, ck, g).unsqueeze(2).broadcast_to([P, HPG, HD]),
                                        ALU.mult).then_inc(comb_s, 1)
                        wait(dve, comb_s, k + 1)
                        v.tensor_tensor(yt[:], yt[:], dx[:], ALU.add).then_inc(comb_s, 1)
                        wait(dve, comb_s, k + 2)
                        add = yt
                    v.tensor_tensor(yt[:], yb[:, GW:2 * GW], add[:], ALU.add).then_inc(y_free, 1)
                    wait(dve, y_free, item + (ck + 1))
                    wait(dve, evac[bank_of(zq + ck)], use_of(zq + ck) + 1)
                    if ck == 0:
                        v.tensor_tensor(y[:, ck, :], yt[:], sz[:], ALU.mult).then_inc(comb_s, 4)
                    else:
                        v.tensor_tensor(y[:, ck, :], yt[:], sz[:], ALU.mult).then_inc(comb_s, 2)

                for ck in range(TT):
                    k = (item + ck) * 6
                    last = ck == TT - 1
                    wait(dve, p_filled, item + (ck + 4))
                    wait(dve, ssd_s, k)
                    v.tensor_tensor(cbm[:], pb[:, 0:P], tri[:],
                                    ALU.mult).then_inc(p_free if last else ssd_s, 1)
                    if ck:
                        wait(dve, y_filled, item + ck)
                    if ck == 0:
                        v.tensor_copy(state[:, 0, :], pb[:, GW:2 * GW]).then_inc(p_free, 1)
                    elif not last:
                        wait(dve, p_free, item + (ck + 3))
                        v.tensor_tensor(sdec[:].rearrange("p (h d) -> p h d", h=HPG),
                                        state[:, (ck - 1) % 2, :].rearrange("p (h d) -> p h d", h=HPG),
                                        heads_of(chunk_decay, ck, g).unsqueeze(2).broadcast_to([P, HPG, HD]),
                                        ALU.mult).then_inc(ssd_s, 1)
                        wait(dve, ssd_s, k + 2)
                        v.tensor_tensor(state[:, ck % 2, :], sdec[:], pb[:, GW:2 * GW], ALU.add).then_inc(p_free, 1)
                    wait(dve, seg_free, item + (ck + 1))
                    if last:
                        wait(dve, p_free, item + (ck + 4))
                    else:
                        wait(dve, ssd_s, k + 1)
                    for h in range(HPG):
                        ins = v.scalar_tensor_tensor(out=m_t[:, h, :], in0=exp_s[:, h, :],
                                                     scalar=head_col(dt_t, ck, g, h), in1=cbm[:],
                                                     op0=ALU.mult, op1=ALU.mult)
                        ins.then_inc(ssd_s, 1 if h else 3 if last else 2 if ck == 0 else 1)
                    if ck:
                        combine(ck - 1)
                    wait(dve, z_tanh, item + (ck + 1))
                    wait(dve, comb_s, (item + ck) * 4)
                    v.scalar_tensor_tensor(out=sz[:], in0=tz[:], scalar=1.0, in1=dense[bank_of(zq + ck)][:, 0:GW],
                                           op0=ALU.add, op1=ALU.mult).then_inc(evac[bank_of(zq + ck)], 1)
                combine(TT - 1)
                wait(dve, rms_s, g + 1)
                v.reciprocal(y_rstd[:], y_rstd[:]).then_inc(yn_s, 1)
                wait(dve, yn_s, g * 9 + 1)
                for ck in range(TT):
                    v.tensor_scalar(y[:, ck, :], y[:, ck, :], y_rstd[:, ck:ck + 1], None,
                                    ALU.mult).then_inc(yn_s, 1)

            run(dve, group, 0, GROUPS, peel=1)
            for k in range(4):
                y_lo_part(Lin(GROUPS), None, k)
            for s in range(16):
                add_ya(Q_TAIL + s, s)
            for k in range(KT):
                if k == 0:
                    dve.wait_ge(p_free, 2)
                v.tensor_scalar(diag[:, k, :], ident[:], gate_col[:, k:k + 1], 0.5, ALU.mult,
                                ALU.mult).then_inc(diag_s, 1)
            for f in range(KT):
                for t in range(2):
                    q = Q_D + 2 * f + t
                    dve.wait_ge(evac[q % 4], q // 4 + 1)
                if f == 0:
                    for q in range(Q_D - 4, Q_D):
                        dve.wait_ge(evac[q % 4], q // 4 + 1)
                if f:
                    dve.wait_ge(mix_s, 3 * f)
                v.scalar_tensor_tensor(out=mt[:], in0=tga[:], scalar=1.0, in1=ya[:, f, :], op0=ALU.add,
                                       op1=ALU.mult).then_inc(mix_s, 1)
                dve.wait_ge(mix_s, 3 * f + 1)
                dve.wait_ge(mixb_in[f % 2], 16 * (f // 2 + 1))
                v.tensor_tensor(mt[:], mt[:], mixb[:, f % 2, :], ALU.add).then_inc(mix_s, 1)
                dve.wait_ge(mixhi_s, f + 1)
                v.tensor_tensor(mix_lo[:, f, :], mt[:], mix_hi[:, f, :], ALU.subtract).then_inc(mix_s, 1)
            dve.wait_ge(gateb_s, 2)
            for t in range(TT):
                dve.wait_ge(e_filled, t + 1)
                if t:
                    dve.wait_ge(fin_s, 8 * t)
                for b in range(2):
                    v.tensor_tensor(res[:, 512 * b:512 * (b + 1)], gate_b[:, 512 * b:512 * (b + 1)],
                                    banks8[2 * (t % 4) + b][:], ALU.mult).then_inc(e_evac, 1)
                dve.wait_ge(e_evac, 2 * t + 2)
                dve.wait_ge(xr_in[t % 2], 16 * (t // 2 + 1))
                v.scalar_tensor_tensor(out=res[:], in0=xr[:, t % 2, :], scalar=ALPHA, in1=res[:],
                                       op0=ALU.mult, op1=ALU.add).then_inc(fin_s, 1)
                dve.wait_ge(fin_s, 8 * t + 1)
                for b in range(2):
                    v.bn_stats(stats_e[:, b, :], res[:, 512 * b:512 * (b + 1)]).then_inc(fin_s, 2)
                dve.wait_ge(fin_s, 8 * t + 5)
                v.bn_aggr(aggr_e[:], stats_e[:].rearrange("p a b -> p (a b)")).then_inc(fin_s, 1)
                dve.wait_ge(fin_sqrt, t + 1)
                v.reciprocal(rstd_e[:], rstd_e[:]).then_inc(fin_s, 1)
                dve.wait_ge(fin_s, 8 * t + 7)
                if t >= 2:
                    dve.wait_ge(out_s[t % 2], 16 * (t // 2))
                v.tensor_scalar(ob[:, t % 2, :], res[:], aggr_e[:, 0:1], rstd_e[:, 0:1],
                                ALU.subtract, ALU.mult).then_inc(fin_s, 1)

        @block.tensor
        def _(pe):
            mm = nc.tensor.matmul
            tr = nc.tensor.transpose

            def three(bank, s_hi, s_lo, m_hi, m_lo, start, stop):
                mm(bank, s_hi, m_hi, start=start, stop=False)
                mm(bank, s_hi, m_lo, start=False, stop=False)
                return mm(bank, s_lo, m_hi, start=False, stop=stop)

            def half_unit(n, q, t, a_hi=u_hi, a_lo=u_lo):
                n, q = at(n), at(q)
                s = n.mod(4)
                h = slice(HALF * t, HALF * (t + 1))
                if t == 0:
                    wait(pe, lo_done, n + 1)
                wait(pe, evac[bank_of(q)], use_of(q))
                for k in range(KT):
                    f = slice(P * k, P * (k + 1))
                    last = three(dense[bank_of(q)][:], w_hi[:, s, f], w_lo[:, s, f],
                                 a_hi[:, k, h], a_lo[:, k, h], k == 0, k == KT - 1)
                last.then_inc(filled, 1)

            pe.wait_ge(rows_in, 16 * 7)
            pe.wait_ge(consts, 4)
            tr(tb[:, 0:P], rows[:, 0, :], ident[:])
            tr(tb[:, P:N_PAR], rows[0:N_PAR - P, 1, :], ident[0:N_PAR - P, 0:N_PAR - P]).then_inc(t_filled, 1)
            pe.wait_ge(t_free, 1)
            for q in range(16):
                kt, t = q % 8, q // 8
                if q == 0:
                    for j in (0, 1, 2, 3, 8, 9, 10, 11, 4, 5, 6, 7, 12, 13, 14, 15):
                        pe.wait_ge(wm_in[j // 4], 16)
                        for k in range(KT):
                            last = mm(pb[:, j:j + 1], wm[:, k, P * j:P * (j + 1)],
                                      par[:, C_VEC + k:C_VEC + k + 1], start=k == 0, stop=k == KT - 1)
                    last.then_inc(p_filled, 1)
                pe.wait_ge(ln_s, 17 * (t + 1))
                wait(pe, evac[q % 4], q // 4)
                for j in range(4):
                    last = tr(dense[q % 4][:, P * j:P * (j + 1)], xt[:, 4 * t + j, P * kt:P * (kt + 1)], ident[:])
                last.then_inc(filled, 1)
            pe.wait_ge(ulo_s, 16)

            def sc_block(b):
                for j in range(4):
                    for t in range(2):
                        half_unit(b * 4 + U_C + j, b * 8 + (Q_C + 2 * j + t), t)

            run(pe, sc_block, 0, 8, peel=1)
            pe.wait_ge(wg_in, 16)
            for j in range(8):
                for k in range(KT):
                    last = mm(pb[:, j:j + 1], wg[:, k, P * j:P * (j + 1)],
                              par[:, C_VEC + k:C_VEC + k + 1], start=k == 0, stop=k == KT - 1)
            last.then_inc(p_filled, 1)

            def c2_pair(f):
                for j in range(2):
                    n, q = f * 2 + (U_C2 + 2 * j), f * 4 + (Q_C2 + 4 * j)
                    for t in range(2):
                        half_unit(n, q + t, t)
                    if j == 0 and f.k == 0:
                        pe.wait_ge(sc_s, 48)
                    for t in range(2):
                        half_unit(n + 1, q + 2 + t, t, hb_hi, hb_lo)

            run(pe, c2_pair, 0, 8, step=2, peel=1)
            for t in range(2):
                half_unit(U_DT, Q_DT + t, t)

            def y_transposes(g, t0, k):
                t, j = k // 2, k % 2
                if k == 0:
                    wait(pe, yn_s, g * 9)
                wait(pe, t_free, t0 + k)
                for cc in range(4):
                    last = tr(tb[:, P * cc:P * (cc + 1)], y[:, 4 * t + cc, P * j:P * (j + 1)], ident[:])
                last.then_inc(t_filled, 1)

            def ya_fill(n, q, s):
                t, f = s // 8, s % 8
                h, fs = slice(HALF * t, HALF * (t + 1)), slice(P * f, P * (f + 1))
                wait(pe, evac[bank_of(q)], use_of(q))
                for j in range(2):
                    sl = (n + j).mod(4)
                    last = three(dense[bank_of(q)][:], w_hi[:, sl, fs], w_lo[:, sl, fs],
                                 y_hi[:, j, h], y_lo[:, j, h], j == 0, j == 1)
                last.then_inc(filled, 1)

            def group(g):
                first = g.k == 0
                n0, q0, t0 = units_b(g)
                k0 = 0 if first else 4

                def halves(u, t):
                    half_unit(n0 + u, q0 + (2 * u + t), t)

                def to_tokens(k):
                    wait(pe, conv_s, g * 20 + (5, 15, 20)[k // 2])
                    wait(pe, t_free, t0 + (k0 + k))
                    src = (bf, xf[0], xf[1])[k // 2]
                    for cc in range(4):
                        cs = slice(HALF * (k % 2) + P * cc, HALF * (k % 2) + P * (cc + 1))
                        last = tr(tb[:, P * cc:P * (cc + 1)], src[:, cs], ident[:])
                    last.then_inc(t_filled, 1)

                halves(0, 0)
                if first:
                    for t in range(2):
                        pe.wait_ge(evac[(Q_DT + t) % 4], (Q_DT + t) // 4 + 1)
                    for ck in range(TT):
                        last = tr(tb[:, 32 * ck:32 * (ck + 1)], dt_raw[:, P * ck:P * (ck + 1)], ident[0:32, 0:32])
                    last.then_inc(t_filled, 1)
                halves(0, 1)
                if not first:
                    y_transposes(g, t0, 0)
                halves(1, 0)
                if not first:
                    y_transposes(g, t0, 1)
                halves(1, 1)
                if first:
                    pe.wait_ge(dts, 10)
                    pe.wait_ge(p_free, 2)
                    at_ = a_t[:].rearrange("p c h -> p (c h)")
                    mm(tb[:, 0:256], tri[:], at_, start=True, stop=True)
                    mm(tb[:, 256:512], strict[:], at_, start=True, stop=True).then_inc(t_filled, 1)
                    mm(pb[:, 0:256], ones[:], at_, start=True, stop=True).then_inc(p_filled, 1)
                else:
                    y_transposes(g, t0, 2)
                halves(2, 0)
                if not first:
                    y_transposes(g, t0, 3)
                halves(2, 1)
                halves(3, 0)
                halves(3, 1)
                if first:
                    for k in range(6):
                        to_tokens(k)
                else:
                    wait(pe, lo_done, n0 + 6)
                    when = {2: 0, 4: 1, 6: 2, 8: 3, 12: 4, 14: 5}
                    for s in range(16):
                        if s == 0:
                            wait(pe, t_free, t0 + 4)
                        ya_fill(n0 + 4, q0 + (8 + s), s)
                        if s in when:
                            to_tokens(when[s])
                zn, zq = n0 + (4 if first else 6), q0 + (8 if first else 24)
                item = g * 8

                def prep(ck):
                    cs = slice(P * ck, P * (ck + 1))
                    if ck == 0:
                        wait(pe, conv_s, g * 20 + 20)
                    wait(pe, p_free, item + (ck + 3))
                    last = mm(pb[:, 0:P], bf[:, cs], cf[:, cs], start=True, stop=True)
                    if ck < TT - 1:
                        wait(pe, xend_s, g * 7 + (ck + 1))
                        if ck == 0:
                            wait(pe, t_free, t0 + (k0 + 6))
                        last = mm(pb[:, GW:2 * GW], bt[:, ck, :], x_end[:], start=True, stop=True)
                    last.then_inc(p_filled, 1)
                    wait(pe, tria_s, item + (ck + 1))
                    wait(pe, seg_free, item + ck)
                    mm(seg[:], strict[:], tri_a[:].rearrange("p h l -> p (h l)"), start=True,
                       stop=True).then_inc(seg_filled, 1)

                def main(ck):
                    cs = slice(P * ck, P * (ck + 1))
                    wait(pe, ssd_s, (item + (ck + 1)) * 6)
                    wait(pe, y_free, item + ck)
                    if ck:
                        mm(yb[:, 0:GW], cf[:, cs], state[:, (ck - 1) % 2, :], start=True, stop=True)
                    for h in range(HPG):
                        last = mm(yb[:, GW + HD * h:GW + HD * (h + 1)], m_t[:, h, :],
                                  xs[:, ck, HD * h:HD * (h + 1)], start=True, stop=True)
                    last.then_inc(y_filled, 1)

                def z_tile(ck):
                    q = zq + ck
                    s = zn.mod(4)
                    cs = slice(P * ck, P * (ck + 1))
                    if ck == 0:
                        wait(pe, lo_done, zn + 2)
                    wait(pe, evac[bank_of(q)], use_of(q))
                    for k in range(KT):
                        f = slice(P * k, P * (k + 1))
                        last = three(dense[bank_of(q)][:, 0:GW], u_hi[:, k, cs], u_lo[:, k, cs],
                                     w_hi[:, s:s + 2, f], w_lo[:, s:s + 2, f], k == 0, k == KT - 1)
                    last.then_inc(filled, 1)

                prep(0)
                for ck in range(TT):
                    z_tile(ck)
                    if ck < TT - 1:
                        prep(ck + 1)
                    main(ck)

            run(pe, group, 0, GROUPS, peel=1)
            for k in range(4):
                y_transposes(Lin(GROUPS), Lin(79), k)
            pe.wait_ge(t_free, 83)
            pe.wait_ge(lo_done, U_TAIL + 2)
            for s in range(16):
                ya_fill(Lin(U_TAIL), Q_TAIL + s, s)
            for f in range(KT):
                for t in range(2):
                    half_unit(U_D + f, Q_D + 2 * f + t, t)
                if f == 1:
                    pe.wait_ge(diag_s, 8)
                    pe.wait_ge(seg_free, 64)
                    for k in range(KT):
                        bank = (tb, seg)[k // 4]
                        last = mm(bank[:, P * (k % 4):P * (k % 4 + 1)], ones[:], diag[:, k, :], start=True, stop=True)
                        if k % 4 == 3:
                            last.then_inc((t_filled, seg_filled)[k // 4], 1)
            for b in range(4):
                pe.wait_ge(evac[b], Q_END // 4 + (1 if Q_END % 4 > b else 0))
            pe.wait_ge(gateb_s, 2)
            pe.wait_ge(p_free, 67)
            pe.wait_ge(y_free, 64)

            def out_tile(t, k, b):
                ts, cs = slice(P * t, P * (t + 1)), slice(512 * b, 512 * (b + 1))
                return three(banks8[2 * (t % 4) + b][:], mix_hi[:, k, ts], mix_lo[:, k, ts],
                             wo_hi[:, k, cs], wo_lo[:, k, cs], k == 0, k == KT - 1)

            for k in range(KT):
                pe.wait_ge(mix_s, 3 * (k + 1))
                pe.wait_ge(lo_done, U_E + k + 1)
                for t in range(4):
                    for b in range(2):
                        last = out_tile(t, k, b)
                    if k == KT - 1:
                        last.then_inc(e_filled, 1)
            for t in range(4, TT):
                for b in range(2):
                    pe.wait_ge(e_evac, 2 * (t - 4) + b + 1)
                    for k in range(KT):
                        last = out_tile(t, k, b)
                last.then_inc(e_filled, 1)


_INS = ["x", "c", "w_mod", "b_mod", "w_in", "conv_ssm_w", "conv_ssm_b", "dt_bias", "a_log", "d_skip",
        "ssm_norm_w", "conv_sc_w", "w_branch_a", "w_branch_b", "w_gate", "b_gate", "w_out", "ln_g", "ln_b"]


def kernel(**inputs):
    import numpy as np
    import concourse.bacc as bacc
    from concourse.bass_utils import run_bass_kernel_spmd

    nc = bacc.Bacc("TRN2", target_bir_lowering=False, num_devices=1, dynamic_dma_scratch_size=1024)
    arrays, args = {}, []
    for name in _INS:
        a = np.ascontiguousarray(inputs[name])
        arrays[f"in_{name}"] = a
        args.append(nc.dram_tensor(f"in_{name}", a.shape, mybir.dt.from_np(a.dtype), kind="ExternalInput").ap())
    args.append(nc.dram_tensor("spill", (KT, P, SEQ), F32, kind="Internal").ap())
    args.append(nc.dram_tensor("out_0", (1, SEQ, D), F32, kind="ExternalOutput").ap())
    build(nc, *args)
    r = run_bass_kernel_spmd(nc, [arrays], core_ids=[0])
    return r.results[0]["out_0"]
```

```python
import concourse.bass as bass
from concourse import mybir

F32 = mybir.dt.float32
F32R = mybir.dt.float32r
ALU = mybir.AluOpType
ACT = mybir.ActivationFunctionType

P = 128
SEQ = 1024
D = 1024
KT = D // P
TT = SEQ // P
HALF = 512
INNER = 2 * D
GROUPS = 8
GW = INNER // GROUPS
HEADS = 32
HPG = HEADS // GROUPS
HD = 64
XB_COL = INNER
B_COL = XB_COL + INNER
C_COL = B_COL + GROUPS * P
DT_COL = C_COL + GROUPS * P
SCB_COL = DT_COL + HEADS
SCC_COL = SCB_COL + D
SCX_COL = SCC_COL + D
SCG_COL = SCX_COL + D
LN_EPS = 1e-5
RMS_EPS = 1e-5
ALPHA = 2.0 ** 0.25

CONV_B = 128
SC_W = CONV_B + 32
B_MOD = SC_W + 24
B_GATE = B_MOD + 24
NORM_W = B_GATE + 16
C_VEC = NORM_W + 16
N_PAR = C_VEC + 8

U_C, U_C2, U_DT, U_B0 = 0, 32, 48, 49
U_B = U_B0 + 6
U_D0 = U_B + 8 * 7
U_TAIL = U_D0 + 1
U_D = U_TAIL + 1
U_E = U_D + 8
Q_C = 16
Q_C2 = Q_C + 64
Q_DT = Q_C2 + 32
Q_B0 = Q_DT + 2
Q_B = Q_B0 + 16
Q_D0 = Q_B + 32 * 7
Q_TAIL = Q_D0 + 2
Q_D = Q_TAIL + 14
Q_END = Q_D + 16
T_B0 = 5
T_B = T_B0 + 6
T_TAIL = T_B + 10 * 7
P_B = 2
FIN = 9


class Lin:

    def __init__(self, c, k=0, i=None):
        self.c, self.k, self.i = c, k, i

    def __add__(self, o):
        return Lin(self.c + o, self.k, self.i)

    def __mul__(self, o):
        return Lin(self.c * o, self.k * o, self.i)

    def over(self, d):
        assert self.k % d == 0
        return Lin(self.c // d, self.k // d, self.i)

    def mod(self, d):
        assert self.k % d == 0
        return self.c % d

    def val(self):
        return self.c if self.k == 0 else self.i * self.k + self.c


def at(v):
    return v if isinstance(v, Lin) else Lin(v)


def wait(eng, sem, value):
    v = at(value)
    if v.k == 0 and v.c <= 0:
        return
    eng.wait_ge(sem, v.val())


def run(eng, body, first, stop, step=1, peel=0):
    for n in range(first, first + peel * step, step):
        body(Lin(n))
    lo = first + peel * step
    count = (stop - lo) // step
    with eng.Fori(0, count) as i:
        body(Lin(lo, step, i))


def build(nc, x, c, w_mod, b_mod, w_in, conv_ssm_w, conv_ssm_b, dt_bias, a_log, d_skip,
          ssm_norm_w, conv_sc_w, w_branch_a, w_branch_b, w_gate, b_gate, w_out, ln_g, ln_b,
          spill, acum_dram, out):
    base = [1152]

    def place(name, shape, dt=F32, offset=None):
        size = 4
        for n in shape[1:]:
            size *= n
        size = (size + 31) // 32 * 32
        where = base[0] if offset is None else offset
        if offset is None:
            base[0] += size
        return nc.alloc_sbuf_tensor_at(name, shape, dt, offset=where)

    K = 1024
    u_base = base[0]
    u_hi = place("u_hi", [P, KT, SEQ], F32R)
    u_lo = place("u_lo", [P, KT, SEQ], F32R)
    a32 = base[0]
    base[0] += 32 * K
    raw = place("raw", [P, 2, 1024])
    w_hi = place("w_hi", [P, 4, 1024], F32R)
    w_lo = place("w_lo", [P, 4, 1024], F32R)
    ident = place("ident", [P, P])
    tri = place("tri", [P, P])
    strict = place("strict", [P, P])
    ones = place("ones", [P, P])
    par = place("par", [P, N_PAR])
    conv_half = place("conv_half", [P, 160])
    sc_half = place("sc_half", [P, 24])
    gate_half = place("gate_half", [P, 16])
    gate_slot = place("gate_slot", [P, 2])
    ac_g = place("ac_g", [P, TT, HPG])
    dt_g = place("dt_g", [P, TT, HPG])
    te_g = place("te_g", [P, TT, HPG])
    d_g = place("d_g", [P, HPG])
    nw_g = place("nw_g", [P, 2])
    shift = place("shift", [P, 8])
    scale1 = place("scale1", [P, 8])
    gate_col = place("gate_col", [P, 8])
    eps = place("eps", [P, 2])
    stats = place("stats", [P, 4, 2, 6])
    aggr = place("aggr", [P, 4, 2])
    rstd = place("rstd", [P, 4])
    d_row = place("d_row", [P, HEADS])
    dtb_row = place("dtb_row", [P, HEADS])
    exp_a = place("exp_a", [P, HEADS])
    dt_t = place("dt_t", [P, TT, HEADS])
    decay_in = place("decay_in", [P, TT, HEADS])
    to_end = place("to_end", [P, TT, HEADS])
    chunk_decay = place("chunk_decay", [P, TT, HEADS])
    acum = place("acum", [P, TT, HEADS])
    sq_sum = place("sq_sum", [P, TT])
    y_rstd = place("y_rstd", [P, TT])
    stats_e = place("stats_e", [P, 2, 6])
    aggr_e = place("aggr_e", [P, 2])
    rstd_e = place("rstd_e", [P, 1])
    r0 = base[0]

    def in_r(name, shape, kb, dt=F32):
        return place(name, shape, dt, offset=r0 + int(kb * K))

    xt = place("xt", [P, TT, D], F32, offset=a32)
    wm = in_r("wm", [P, KT, 2048], 0)
    uf = in_r("uf", [P, 2, HALF], 64)
    rows = in_r("rows", [P, 2, P], 68)
    alog_row = in_r("alog_row", [P, HEADS], 69)
    wg = place("wg", [P, KT, 1024], F32, offset=a32)
    hb_hi = in_r("hb_hi", [P, KT, SEQ], 0, F32R)
    hb_lo = in_r("hb_lo", [P, KT, SEQ], 32, F32R)
    cv = in_r("cv", [P, SEQ], 64)
    sg = in_r("sg", [P, SEQ], 68)
    prod = in_r("prod", [P, SEQ + 2], 72)
    tgb = in_r("tgb", [P, SEQ], 64)
    mb = in_r("mb", [P, 2, SEQ], 68)
    ya = place("ya", [P, KT, SEQ], F32, offset=a32)
    bf = in_r("bf", [P, SEQ], 0)
    cf = in_r("cf", [P, SEQ], 4)
    xf = [in_r("xf0", [P, SEQ], 8), in_r("xf1", [P, SEQ], 12)]
    xs = in_r("xs", [P, TT, GW], 16)
    bt = in_r("bt", [P, TT, P], 24)
    th = in_r("th", [P, SEQ], 28)
    cin = in_r("cin", [P, SEQ + 3], 32)
    y = in_r("y", [P, TT, GW], 36.25)
    x_end = in_r("x_end", [P, 2, GW], 44.25)
    xdt = in_r("xdt", [P, 2, GW], 46.25)
    dx = in_r("dx", [P, 2, GW], 48.25)
    acb = in_r("acb", [P, 2, HPG, 2 * P], 50.25)
    y_hi = in_r("y_hi", [P, 2, SEQ], 59.75, F32R)
    y_lo = in_r("y_lo", [P, 2, SEQ], 67.75, F32R)
    exp_s = in_r("exp_s", [P, 2, HPG, P], 59.75)
    m_t = in_r("m_t", [P, 2, HPG, P], 63.75)
    cbm = in_r("cbm", [P, P], 67.75)
    yt = in_r("yt", [P, GW], 68.25)
    state = in_r("state", [P, 2, GW], 69.25)
    tz = in_r("tz", [P, GW], 71.25)
    sz = in_r("sz", [P, GW], 72.25)
    sdec = in_r("sdec", [P, GW], 73.25)
    sqj = in_r("sqj", [P, GW], 74.25)
    dt_raw = in_r("dt_raw", [32, SEQ], 36.25)
    acum_t = in_r("acum_t", [32, SEQ], 40.25)
    dtv = [in_r(f"dtv{k}", [P, TT, HEADS], 59.75 + k) for k in range(9)]
    a_t = in_r("a_t", [P, TT, HEADS], 44.25)
    mix_hi = in_r("mix_hi", [P, KT, SEQ], 0, F32R)
    mix_lo = place("mix_lo", [P, KT, SEQ], F32R, offset=a32)
    gate_b = in_r("gate_b", [P, D], 32)
    lng_b = in_r("lng_b", [P, D], 36)
    lnb_b = in_r("lnb_b", [P, D], 40)
    diag = in_r("diag", [P, KT, P], 44)
    mt = in_r("mt", [P, SEQ], 48)
    tga = in_r("tga", [P, 2, SEQ], 52)
    mixb = in_r("mixb", [P, 2, SEQ], 60)
    xr = in_r("xr", [P, 2, D], 44)
    res = in_r("res", [P, D], 52)
    ob = in_r("ob", [P, 2, D], 56)
    wo0_hi = in_r("wo0_hi", [P, D], 68, F32R)
    wo0_lo = in_r("wo0_lo", [P, D], 72, F32R)
    wo_hi = place("wo_hi", [P, KT, D], F32R, offset=u_base)
    wo_lo = place("wo_lo", [P, KT, D], F32R, offset=u_base + 32 * K)

    wo = [(wo0_hi[:], wo0_lo[:])] + [(wo_hi[:, k, :], wo_lo[:, k, :]) for k in range(1, KT)]
    assert base[0] <= r0 and r0 + 76 * K <= nc.sbuf_usable_end, (base[0], r0)

    dense = [nc.alloc_psum_tensor(f"dense{k}", [P, 512], F32) for k in range(4)]
    tb = [nc.alloc_psum_tensor(f"tb{k}", [P, 512], F32) for k in range(2)]
    pb = nc.alloc_psum_tensor("pb", [P, 512], F32)
    yb = nc.alloc_psum_tensor("yb", [P, 512], F32)
    banks8 = dense + tb + [pb, yb]

    S = nc.alloc_semaphore
    x_in = [S("x_in0"), S("x_in1")]
    wm_in = [S(f"wm_in{k}") for k in range(4)]
    wg_in = S("wg_in")
    rows_in = S("rows_in")
    heads_in = S("heads_in")
    w_in_s = [S("raw_in0"), S("raw_in1")]
    hi_done = S("hi_done")
    lo_done = S("lo_done")
    filled = S("filled")
    evac = [S(f"evac{k}") for k in range(4)]
    t_filled, t_free = S("t_filled"), S("t_free")
    exp_ready = S("exp_ready")
    acum_stored = S("acum_stored")
    acb_in = [S("acb_in0"), S("acb_in1")]
    p_filled, p_free = S("p_filled"), S("p_free")
    y_filled, y_free = S("y_filled"), S("y_free")
    consts = S("consts")
    par_ready = S("par_ready")
    ln_s = S("ln_steps")
    ln_sqrt = S("ln_sqrt")
    mod_filled = S("mod_filled")
    mod_s = S("mod_steps")
    uhi_s = S("u_hi_written")
    ulo_s = S("u_lo_written")
    sc_s = S("sc_steps")
    sc_tanh = S("sc_tanh")
    gslot_s = S("gate_slot_written")
    gpar_s = S("group_params")
    stored = [S("mb_stored0"), S("mb_stored1")]
    dts = S("dt_steps")
    dta = S("dt_act_steps")
    ya_zero = S("ya_zeroed")
    conv_s = S("conv_steps")
    conv_tanh = S("conv_tanh")
    yhi_s = S("y_hi_written")
    xw_s = S("x_weighted")
    ssd_s = S("ssd_steps")
    z_tanh = S("z_tanh")
    comb_s = S("combine_steps")
    sq_s = S("squares")
    rms_s = S("rms_sqrt")
    yn_s = S("y_normed")
    mixb_in = [S("mixb_in0"), S("mixb_in1")]
    mix_s = S("mix_steps")
    mixhi_s = S("mix_hi_written")
    diag_s, gateb_s = S("diag_ready"), S("gate_b_ready")
    nw_s = S("norm_weight_slot")
    lnp_in = S("ln_params_in")
    xr_in = [S("xr_in0"), S("xr_in1")]
    e_filled, e_evac = S("out_filled"), S("out_evacuated")
    fin_s, fin_sqrt = S("final_steps"), S("final_sqrt")
    out_s = [S("out_stored0"), S("out_stored1")]

    def x_fill(q):
        return q // 8 * 4 + q % 4, q // 4 % 2

    def bank_of(q):
        return at(q).mod(4)

    def t_bank(k):
        return at(k).mod(2)

    def use_of(q):
        return at(q).over(4) if at(q).k else Lin(at(q).c // 4)

    def w_cols(w, col, width=P):
        v = at(col)
        cols = w[:, v.c:v.c + width] if v.k == 0 else w[:, bass.ds(nc.sync.snap(v.val()), width)]
        return cols.rearrange("(k p) f -> p k f", p=P)

    def w_rows(w, row_tile):
        v = at(row_tile) * P
        return w[v.c:v.c + P, :] if v.k == 0 else w[bass.ds(nc.sync.snap(v.val()), P), :]

    def col(t, j, n=1):
        v = at(j)
        return t[:, v.c:v.c + n] if v.k == 0 else t[:, bass.ds(v.val(), n)]

    def heads_of(t, ck, g):
        v = at(g) * HPG
        return t[:, ck, v.c:v.c + HPG] if v.k == 0 else t[:, ck, bass.ds(v.val(), HPG)]

    def head_col(t, ck, g, h):
        v = at(g) * HPG + h
        return t[:, ck, v.c:v.c + 1] if v.k == 0 else t[:, ck, bass.ds(v.val(), 1)]

    def tile_of(t, f):
        v = at(f)
        return t[:, v.c, :] if v.k == 0 else t[:, bass.ds(v.val(), 1), :].rearrange("p a n -> p (a n)")

    win, wmod, wgate = w_in[0], w_mod[0], w_gate[0]
    wa, wb, wout = w_branch_a[0], w_branch_b[0], w_out[0]

    def units_b(g):
        if at(g).k == 0 and at(g).c == 0:
            return Lin(U_B0), Lin(Q_B0), Lin(T_B0)
        g1 = at(g) + (-1)
        return g1 * 8 + U_B, g1 * 32 + Q_B, g1 * 10 + T_B

    with nc.Block() as block:

        @block.sync
        def _(sp):
            def load(n, src):
                n = at(n)
                wait(sp, lo_done, n + (-1))
                dst = raw[:, n.mod(2), :]
                if len(src.shape) == 3:
                    dst = dst.rearrange("p (k f) -> p k f", k=KT)
                sp.dma_start(dst, src).then_inc(w_in_s[n.mod(2)], 16)

            sp.dma_start(rows[:, 0, :], conv_ssm_w.rearrange("a t (b p) -> (a t b) p", p=P)).then_inc(rows_in, 16)
            r = 0
            for src in (conv_ssm_b.rearrange("a (b p) -> (a b) p", p=P),
                        conv_sc_w.rearrange("a t (b p) -> (a t b) p", p=P),
                        b_mod.rearrange("a (b p) -> (a b) p", p=P),
                        b_gate.rearrange("a (b p) -> (a b) p", p=P),
                        ssm_norm_w.rearrange("a (b p) -> (a b) p", p=P),
                        c.rearrange("a (b p) -> (a b) p", p=P)):
                sp.dma_start(rows[r:r + src.shape[0], 1, :], src).then_inc(rows_in, 16)
                r += src.shape[0]
            for t in range(2):
                sp.dma_start(xt[:, 4 * t:4 * t + 4, :],
                             x[0, 512 * t:512 * (t + 1), :].rearrange("(t p) d -> p t d", p=P)
                             ).then_inc(x_in[t], 16)
            for dst, src in ((dtb_row, dt_bias), (alog_row, a_log), (d_row, d_skip)):
                sp.dma_start(dst[:], src.partition_broadcast(P).rearrange("p a d -> p (a d)")).then_inc(heads_in, 16)
            for k in (0, 2, 1, 3):
                sp.dma_start(wm[:, :, 512 * k:512 * (k + 1)],
                             w_cols(wmod, 512 * k, 512)).then_inc(wm_in[k], 16)

            def sc_units(b):
                for j, start in enumerate((SCC_COL, SCX_COL, SCG_COL, SCB_COL)):
                    load(b * 4 + U_C + j, w_cols(win, b * P + start))
                    if b.k == 0 and j == 3:
                        sp.wait_ge(filled, 16)
                        sp.dma_start(wg[:], w_cols(wmod, 2048, 1024)).then_inc(wg_in, 16)

            run(sp, sc_units, 0, 8, peel=1)

            def c2_units(f):
                for j in range(2):
                    load(f * 2 + U_C2 + 2 * j, w_cols(wgate, f * P + D + j * P))
                    load(f * 2 + U_C2 + 2 * j + 1, w_cols(wb, f * P + j * P))

            for f in range(0, 8, 2):
                c2_units(Lin(f))
            load(U_DT, w_cols(win, DT_COL))

            def group_units(g):
                n0, _, _ = units_b(g)
                first = g.k == 0
                load(n0, w_cols(win, g * P + B_COL))
                load(n0 + 1, w_cols(win, g * P + C_COL))
                load(n0 + 2, w_cols(win, g * GW + XB_COL))
                load(n0 + 3, w_cols(win, g * GW + XB_COL + P))
                if not first:
                    load(n0 + 4, w_rows(wa, g * 2 + (-2)))
                    load(n0 + 5, w_rows(wa, g * 2 + (-1)))
                zn = n0 + (4 if first else 6)
                load(zn, w_cols(win, g * GW))
                load(zn + 1, w_cols(win, g * GW + P))

            run(sp, group_units, 0, GROUPS, peel=1)
            load(U_D0, w_cols(wgate, 0))
            load(U_TAIL, w_rows(wa, 14))
            load(U_TAIL + 1, w_rows(wa, 15))
            for f in range(1, 5):
                load(U_D + f, w_cols(wgate, f * P))
            sp.wait_ge(filled, Q_D + 2)
            sp.wait_ge(stored[0], 64)
            sp.wait_ge(stored[1], 64)
            sp.dma_start(mixb[:, 0, :], spill[0]).then_inc(mixb_in[0], 16)
            sp.dma_start(mixb[:, 1, :], spill[1]).then_inc(mixb_in[1], 16)
            sp.dma_start(lng_b[:], ln_g.partition_broadcast(P).rearrange("p a d -> p (a d)")).then_inc(lnp_in, 16)
            sp.dma_start(lnb_b[:], ln_b.partition_broadcast(P).rearrange("p a d -> p (a d)")).then_inc(lnp_in, 16)
            for f in range(2, KT):
                if f + 3 < KT:
                    load(U_D + f + 3, w_cols(wgate, (f + 3) * P))
                sp.wait_ge(mix_s, 3 * (f - 2) + 2)
                sp.dma_start(mixb[:, f % 2, :], spill[f]).then_inc(mixb_in[f % 2], 16)
            for k in range(2):
                load(U_E + k, w_rows(wout, k))
            sp.wait_ge(mix_s, 3 * KT)
            sp.wait_ge(gateb_s, 2)
            for t in range(2):
                sp.dma_start(xr[:, t, :], x[0, P * t:P * (t + 1), :]).then_inc(xr_in[t], 16)
            for k in range(2, KT):
                load(U_E + k, w_rows(wout, k))
            for t in range(TT):
                sp.wait_ge(fin_s, FIN * (t + 1))
                sp.dma_start(out[0, P * t:P * (t + 1), :], ob[:, t % 2, :]).then_inc(out_s[t % 2], 16)
                if t + 2 < TT:
                    sp.dma_start(xr[:, t % 2, :], x[0, P * (t + 2):P * (t + 3), :]).then_inc(xr_in[t % 2], 16)
            sp.wait_ge(out_s[0], 64)
            sp.wait_ge(out_s[1], 64)

        @block.scalar
        def _(act):
            nc_act = nc.scalar

            def split_hi(n, done):
                n = at(n)
                wait(act, w_in_s[n.mod(2)], (n.over(2) if n.k else Lin(n.c // 2)) * 16 + 16)
                wait(act, filled, done)
                nc_act.copy(w_hi[:, n.mod(4), :], raw[:, n.mod(2), :]).then_inc(hi_done, 1)

            act.wait_ge(t_filled, 1)
            nc_act.copy(par[:], tb[0][:, 0:N_PAR]).then_inc(t_free, 1)
            act.wait_ge(consts, 6)
            for t in range(2):
                act.wait_ge(ln_s, 17 * t + 12)
                nc_act.activation(rstd[:], aggr[:, :, 1], ACT.Sqrt, bias=eps[:, 0:1]).then_inc(ln_sqrt, 1)
            for n in range(4):
                split_hi(n, 0)
            act.wait_ge(heads_in, 48)
            nc_act.activation(exp_a[:], alog_row[:], ACT.Exp).then_inc(dta, 1)
            for q in range(16):
                kt, t = x_fill(q)
                act.wait_ge(filled, q + 1)
                if q % 8 == 0:
                    act.wait_ge(mod_s, q // 4 + 2)
                if q >= 2:
                    act.wait_ge(ulo_s, q - 1)
                nc_act.activation(uf[:, q % 2, :], dense[q % 4][:], ACT.Identity, bias=shift[:, kt:kt + 1],
                                  scale=scale1[:, kt:kt + 1]).then_inc(evac[q % 4], 1)
                act.wait_ge(evac[q % 4], q // 4 + 1)
                nc_act.copy(u_hi[:, kt, HALF * t:HALF * (t + 1)], uf[:, q % 2, :]).then_inc(uhi_s, 1)

            def sc_block(b):
                n, q = b * 4 + U_C, b * 8 + Q_C
                for t in range(2):
                    if t == 0 and b.k == 0:
                        act.wait_ge(ulo_s, 16)
                    elif t == 0:
                        wait(act, sc_s, b * 6)
                    wait(act, filled, q + t + 1)
                    nc_act.copy(cv[:, HALF * t:HALF * (t + 1)],
                                dense[bank_of(q + t)][:]).then_inc(evac[bank_of(q + t)], 1)
                split_hi(n + 4, q + 2)
                split_hi(n + 5, q + 4)
                for t in range(2):
                    wait(act, filled, q + 4 + t + 1)
                    nc_act.activation(sg[:, HALF * t:HALF * (t + 1)], dense[bank_of(q + 4 + t)][:],
                                      ACT.Tanh, scale=0.5).then_inc(sc_tanh, 1)
                split_hi(n + 6, q + 6)
                split_hi(n + 7, q + 8)

            run(act, sc_block, 0, 8, peel=1)

            def store_mb(f, j):
                q = f * 4 + Q_C2 + 2
                for t in range(2):
                    wait(act, evac[bank_of(q + t)], use_of(q + t) + 1)
                dst = spill[f.c] if f.k == 0 else spill[bass.ds(f.val(), 1)].rearrange("a p n -> (a p) n")
                act.dma_start(dst, mb[:, j, :]).then_inc(stored[j], 16)

            def c2_pair(f):
                for j in range(2):
                    n, q = f * 2 + U_C2 + 2 * j, f * 4 + Q_C2 + 4 * j
                    if j == 0:
                        wait(act, gslot_s, f.over(2) + 1 if f.k else 1)
                    if j or f.k:
                        store_mb(f + (j - 1), 1 - j)
                    for t in range(2):
                        if j == 0 and t == 0 and f.k == 0:
                            act.wait_ge(sc_s, 48)
                        wait(act, filled, q + t + 1)
                        wait(act, evac[bank_of(q + t + 2)], use_of(q + t + 2))
                        nc_act.activation(tgb[:, HALF * t:HALF * (t + 1)], dense[bank_of(q + t)][:],
                                          ACT.Tanh, scale=0.5, bias=gate_slot[:, j:j + 1]
                                          ).then_inc(evac[bank_of(q + t)], 1)
                    split_hi(n + 4, q + 2)
                    split_hi(n + 5, q + 4)

            run(act, c2_pair, 0, 8, step=2, peel=1)
            store_mb(Lin(7), 1)

            for t in range(2):
                act.wait_ge(filled, Q_DT + t + 1)
                nc_act.copy(dt_raw[:, HALF * t:HALF * (t + 1)],
                            dense[(Q_DT + t) % 4][0:32, :]).then_inc(evac[(Q_DT + t) % 4], 1)
            split_hi(U_DT + 4, Q_DT + 2)

            def dt_acts():
                act.wait_ge(dts, 1)
                nc_act.activation(dtv[2][:], dtv[1][:], ACT.Exp, scale=-1.0).then_inc(dta, 1)
                act.wait_ge(dts, 2)
                nc_act.activation(dtv[4][:], dtv[3][:], ACT.Ln).then_inc(dta, 1)

            def decay_acts():
                act.wait_ge(t_filled, 3)
                flat = "p c h -> p (c h)"
                nc_act.activation(decay_in[:].rearrange(flat), tb[0][:, 0:256], ACT.Exp).then_inc(dta, 1)
                nc_act.activation(to_end[:].rearrange(flat), tb[0][:, 256:512], ACT.Exp).then_inc(dta, 1)
                nc_act.copy(acum[:].rearrange(flat), tb[0][:, 0:256]).then_inc(t_free, 1)
                for k in range(2):
                    act.wait_ge(t_filled, 4 + k)
                    nc_act.copy(acum_t[:, HALF * k:HALF * (k + 1)], tb[(3 + k) % 2][0:32, :]).then_inc(t_free, 1)
                act.wait_ge(t_free, 5)
                act.dma_start(acum_dram, acum_t[:]).then_inc(acum_stored, 16)
                act.wait_ge(p_filled, 2)
                nc_act.activation(chunk_decay[:].rearrange(flat), pb[:, 0:256], ACT.Exp).then_inc(p_free, 1)

            def group(g):
                first = g.k == 0
                n0, q0, t0 = units_b(g)
                conv0 = g * 20
                tt = [0]

                def load_acb(g, cp):
                    v = at(g) * HPG
                    rows_ = slice(v.c, v.c + HPG) if v.k == 0 else bass.ds(nc.scalar.snap(v.val()), HPG)
                    src = acum_dram[rows_, 2 * P * cp:2 * P * (cp + 1)].partition_broadcast(P)
                    wait(act, exp_ready, g * 40 + 10 * (cp - 1))
                    act.dma_start(acb[:, cp % 2, :, :], src).then_inc(acb_in[cp % 2], 16)

                def evac_half(u, t):
                    q = q0 + 2 * u + t
                    if t == 0:
                        wait(act, conv_s, conv0 + (5 * u - 1))
                    wait(act, filled, q + 1)
                    nc_act.copy(cin[:, 3 + HALF * t:3 + HALF * (t + 1)],
                                dense[bank_of(q)][:]).then_inc(evac[bank_of(q)], 1)

                def tanh(u):
                    src = (bf, cf, xf[0], xf[1])[u]
                    wait(act, conv_s, conv0 + (5 * u + 4))
                    nc_act.activation(th[:], src[:], ACT.Tanh).then_inc(conv_tanh, 1)

                def y_hi_part():
                    k = tt[0]
                    if k == 0:
                        wait(act, nw_s, g)
                    t, j = k // 2, k % 2
                    wait(act, t_filled, t0 + k + 1)
                    nc_act.activation(y_hi[:, j, HALF * t:HALF * (t + 1)], tb[t_bank(t0 + k)][:], ACT.Copy,
                                      scale=nw_g[:, j:j + 1]).then_inc(yhi_s, 1)
                    tt[0] += 1

                evac_half(0, 0)
                evac_half(0, 1)
                split_hi(n0 + 4, q0 + 2)
                if first:
                    dt_acts()
                else:
                    y_hi_part()
                tanh(0)
                evac_half(1, 0)
                if not first:
                    y_hi_part()
                evac_half(1, 1)
                split_hi(n0 + 5, q0 + 4)
                if first:
                    decay_acts()
                else:
                    y_hi_part()
                tanh(1)
                evac_half(2, 0)
                if not first:
                    y_hi_part()
                evac_half(2, 1)
                split_hi(n0 + 6, q0 + 6)
                tanh(2)
                evac_half(3, 0)
                evac_half(3, 1)
                split_hi(n0 + 7, q0 + 8)
                tanh(3)
                wait(act, acum_stored, 16)
                for cp in range(2):
                    load_acb(g, cp)
                k0 = 0 if first else 4
                for k in range(6):
                    wait(act, t_filled, t0 + (k0 + k + 1))
                    src = tb[t_bank(t0 + (k0 + k))][:].rearrange("p (c n) -> p c n", c=4)
                    cs = slice(4 * (k // 3), 4 * (k // 3) + 4)
                    dst = bt[:, cs, :] if k % 3 == 0 else xs[:, cs, P * (k % 3 - 1):P * (k % 3)]
                    nc_act.copy(dst, src).then_inc(t_free, 1)
                if not first:
                    split_hi(n0 + 8, q0 + 24)
                    split_hi(n0 + 9, q0 + 24)
                zq = q0 + (8 if first else 24)
                item = g * 8

                def square(ck):
                    wait(act, comb_s, (item + (ck + 1)) * 4)
                    if ck:
                        wait(act, sq_s, item + ck)
                    nc_act.activation(sqj[:], y[:, ck, :], ACT.Square,
                                      accum_out=sq_sum[:, ck:ck + 1]).then_inc(sq_s, 1)

                def decay(ck):
                    if ck % 2 == 0:
                        wait(act, acb_in[ck // 2 % 2], g * 32 + 16 * (ck // 4 + 1))
                    wait(act, ssd_s, (item + (ck - 1)) * 3)
                    for h in range(HPG):
                        nc_act.activation(exp_s[:, ck % 2, h, :], acb[:, ck // 2 % 2, h, P * (ck % 2):P * (ck % 2 + 1)],
                                          ACT.Relu, scale=-1.0, bias=ac_g[:, ck, h:h + 1]).then_inc(exp_ready, 1)
                    wait(act, exp_ready, (item + ck) * 5 + 4)
                    nc_act.activation(exp_s[:, ck % 2, :, :], exp_s[:, ck % 2, :, :], ACT.Exp,
                                      scale=-1.0).then_inc(exp_ready, 1)
                    if ck in (1, 3):
                        load_acb(g, ck // 2 + 2)

                wait(act, gpar_s, g * 4 + 4)
                decay(0)
                decay(1)
                for ck in range(TT):
                    wait(act, filled, zq + (ck + 1))
                    if ck:
                        wait(act, evac[bank_of(zq + (ck - 1))], use_of(zq + (ck - 1)) + 1)
                    nc_act.activation(tz[:], dense[bank_of(zq + ck)][:, 0:GW], ACT.Tanh,
                                      scale=0.5).then_inc(z_tanh, 1)
                    if ck:
                        square(ck - 1)
                    if ck + 2 < TT:
                        decay(ck + 2)
                square(TT - 1)
                wait(act, sq_s, item + 8)
                nc_act.activation(y_rstd[:], sq_sum[:], ACT.Sqrt, bias=eps[:, 1:2],
                                  scale=1.0 / GW).then_inc(rms_s, 1)
                split_hi(n0 + (8 if first else 10), zq + 8)
                split_hi(n0 + (9 if first else 11), zq + 8)

            run(act, group, 0, GROUPS, peel=1)

            def gate_tanh(f):
                q = Q_D + 2 * f if f else Q_D0
                for t in range(2):
                    act.wait_ge(filled, q + t + 1)
                    if t == 0 and f >= 2:
                        act.wait_ge(mix_s, 3 * f - 5)
                    nc_act.activation(tga[:, f % 2, HALF * t:HALF * (t + 1)], dense[(q + t) % 4][:], ACT.Tanh,
                                      scale=0.5, bias=gate_half[:, f:f + 1]).then_inc(evac[(q + t) % 4], 1)

            gate_tanh(0)
            split_hi(U_D0 + 4, Q_TAIL)
            for k in range(4):
                t, j = k // 2, k % 2
                act.wait_ge(t_filled, T_TAIL + k + 1)
                nc_act.activation(y_hi[:, j, HALF * t:HALF * (t + 1)], tb[(T_TAIL + k) % 2][:], ACT.Copy,
                                  scale=par[:, NORM_W + 14 + j:NORM_W + 15 + j]).then_inc(yhi_s, 1)
            split_hi(U_TAIL + 4, Q_D + 2)
            split_hi(U_TAIL + 5, Q_D + 2)
            for f in range(KT):
                if f + 1 < KT:
                    gate_tanh(f + 1)
                if 1 <= f + 1 < 4:
                    split_hi(U_D + f + 5, Q_D + 2 * f + 4)
                if f == 2:
                    for b in range(2):
                        act.wait_ge(t_filled, T_TAIL + 5 + b)
                        nc_act.copy(gate_b[:, 512 * b:512 * (b + 1)], tb[(T_TAIL + b) % 2][:]).then_inc(gateb_s, 1)
                act.wait_ge(mix_s, 3 * f + 2)
                nc_act.copy(mix_hi[:, f, :], mt[:]).then_inc(mixhi_s, 1)
                if f == KT - 2:
                    act.wait_ge(w_in_s[U_E % 2], 16 * (U_E // 2 + 1))
                    nc_act.copy(wo[0][0], raw[:, U_E % 2, :]).then_inc(hi_done, 1)
            for k in range(1, KT):
                n = U_E + k
                act.wait_ge(filled, Q_END)
                act.wait_ge(w_in_s[n % 2], 16 * (n // 2 + 1))
                nc_act.copy(wo[k][0], raw[:, n % 2, :]).then_inc(hi_done, 1)
            for t in range(TT):
                act.wait_ge(fin_s, FIN * t + 6)
                nc_act.activation(rstd_e[:], aggr_e[:, 1:2], ACT.Sqrt, bias=eps[:, 0:1]).then_inc(fin_sqrt, 1)

        @block.gpsimd
        def _(pool):
            g_ = nc.gpsimd
            g_.memset(ones[:], 1.0).then_inc(consts, 1)
            g_.memset(eps[:, 0:1], LN_EPS).then_inc(consts, 1)
            g_.memset(eps[:, 1:2], 4 * RMS_EPS).then_inc(consts, 1)
            pool.wait_ge(consts, 3)
            g_.affine_select(out=ident[:], in_=ones[:], compare_op=ALU.is_equal, fill=0.0, base=0,
                             pattern=[[-1, P]], channel_multiplier=1).then_inc(consts, 1)
            g_.affine_select(out=tri[:], in_=ones[:], compare_op=ALU.is_ge, fill=0.0, base=0,
                             pattern=[[1, P]], channel_multiplier=-1).then_inc(consts, 1)
            g_.affine_select(out=strict[:], in_=ones[:], compare_op=ALU.is_gt, fill=0.0, base=0,
                             pattern=[[-1, P]], channel_multiplier=1).then_inc(consts, 1)

            def split_lo(n, dst=None):
                n = at(n)
                wait(pool, hi_done, n + 1)
                hi = w_hi[:, n.mod(4), :] if dst is None else wo[dst][0]
                lo = w_lo[:, n.mod(4), :] if dst is None else wo[dst][1]
                g_.tensor_tensor(lo, raw[:, n.mod(2), :], hi, ALU.subtract).then_inc(lo_done, 1)

            def four(n):
                for j in range(4):
                    split_lo(n + j)

            for n in range(4):
                split_lo(n)
            pool.wait_ge(ulo_s, 16)
            g_.memset(prod[:, 0:2], 0.0).then_inc(consts, 1)
            run(pool, four, 4, U_DT, step=4)
            pool.wait_ge(p_filled, 1)
            g_.memset(ya[:], 0.0).then_inc(ya_zero, 1)
            for n in range(U_DT, U_DT + 4):
                split_lo(n)
            pool.wait_ge(filled, Q_DT)
            g_.memset(cin[:, 0:3], 0.0).then_inc(consts, 1)
            split_lo(U_DT + 4)

            def group(g):
                first = g.k == 0
                n0, q0, _ = units_b(g)
                for j in range(4):
                    split_lo(n0 + 4 + j)
                item = g * 8
                xs_ready = units_b(g)[2] + (6 if first else 10)
                wait(pool, gpar_s, g * 4 + 4)
                for ck in range(TT):
                    if not first and ck == 2:
                        split_lo(n0 + 8)
                        split_lo(n0 + 9)
                    if ck % 4 == 0:
                        wait(pool, t_free, xs_ready + (-3 if ck == 0 else 0))
                    x4 = xs[:, ck, :].rearrange("p (h d) -> p h d", h=HPG)

                    def weigh(dst, w, n=1):
                        g_.tensor_tensor(dst[:, ck % 2, :].rearrange("p (h d) -> p h d", h=HPG), x4,
                                         w.unsqueeze(2).broadcast_to([P, HPG, HD]), ALU.mult).then_inc(xw_s, n)

                    wait(pool, y_filled, item + (ck - 1))
                    if ck < TT - 1:
                        weigh(x_end, te_g[:, ck, :])
                    weigh(xdt, dt_g[:, ck, :], 1 if ck < TT - 1 else 2)
                    wait(pool, comb_s, (item + (ck - 1)) * 4)
                    weigh(dx, d_g[:])
                e = 8 if first else 10
                split_lo(n0 + e)
                split_lo(n0 + e + 1)

            run(pool, group, 0, GROUPS, peel=1)
            for n in range(U_D0 + 4, U_E):
                split_lo(n)
            for k in range(KT):
                split_lo(U_E + k, dst=k)

        @block.vector
        def _(dve):
            v = nc.vector
            for t in range(2):
                dve.wait_ge(x_in[t], 16)
                for j in range(4):
                    for k in range(2):
                        v.bn_stats(stats[:, j, k, :], xt[:, 4 * t + j, 512 * k:512 * (k + 1)]).then_inc(ln_s, 1)
                if t:
                    dve.wait_ge(ln_s, 17)
                for j in range(4):
                    dve.wait_ge(ln_s, 17 * t + 8)
                    v.bn_aggr(aggr[:, j, :], stats[:, j, :, :].rearrange("p a b -> p (a b)")).then_inc(ln_s, 1)
                dve.wait_ge(ln_sqrt, t + 1)
                v.reciprocal(rstd[:], rstd[:]).then_inc(ln_s, 1)
                dve.wait_ge(ln_s, 17 * t + 13)
                for j in range(4):
                    v.tensor_scalar(xt[:, 4 * t + j, :], xt[:, 4 * t + j, :], aggr[:, j, 0:1], rstd[:, j:j + 1],
                                    ALU.subtract, ALU.mult).then_inc(ln_s, 1)
            dve.wait_ge(t_free, 1)
            v.tensor_scalar(conv_half[:], par[:, 0:160], 0.5, None, ALU.mult).then_inc(par_ready, 1)
            v.tensor_scalar(sc_half[:], par[:, SC_W:SC_W + 24], 0.5, None, ALU.mult).then_inc(par_ready, 1)
            v.tensor_scalar(gate_half[:], par[:, B_GATE:B_GATE + 16], 0.5, None, ALU.mult).then_inc(par_ready, 1)
            for k in range(2):
                h = slice(4 * k, 4 * k + 4)
                bank = (pb, yb)[k]
                dve.wait_ge(mod_filled, k + 1)
                v.tensor_tensor(shift[:, h], bank[:, 0:4], par[:, B_MOD + 4 * k:B_MOD + 4 * k + 4],
                                ALU.add).then_inc(mod_s, 1)
                v.scalar_tensor_tensor(out=scale1[:, h], in0=bank[:, 4:8], scalar=1.0,
                                       in1=par[:, B_MOD + 8 + 4 * k:B_MOD + 12 + 4 * k],
                                       op0=ALU.add, op1=ALU.add).then_inc(mod_s, 1)
                for q in range(8 * k, 8 * k + 8):
                    kt, t = x_fill(q)
                    dve.wait_ge(uhi_s, q + 1)
                    v.tensor_tensor(u_lo[:, kt, HALF * t:HALF * (t + 1)], uf[:, q % 2, :],
                                    u_hi[:, kt, HALF * t:HALF * (t + 1)], ALU.subtract).then_inc(ulo_s, 1)

            def sc_block(b):
                q = b * 8 + Q_C
                if b.k == 0:
                    dve.wait_ge(consts, 7)
                    dve.wait_ge(par_ready, 3)
                for t in range(2):
                    wait(dve, evac[bank_of(q + t)], use_of(q + t) + 1)
                    wait(dve, filled, q + 2 + t + 1)
                    v.tensor_tensor(prod[:, 2 + HALF * t:2 + HALF * (t + 1)], cv[:, HALF * t:HALF * (t + 1)],
                                    dense[bank_of(q + 2 + t)][:], ALU.mult).then_inc(evac[bank_of(q + 2 + t)], 1)
                for t in range(2):
                    wait(dve, evac[bank_of(q + 2 + t)], use_of(q + 2 + t) + 1)
                v.tensor_scalar(cv[:], prod[:, 2:2 + SEQ], col(sc_half, b + 16), None, ALU.mult).then_inc(sc_s, 1)
                for k in (1, 0):
                    wait(dve, sc_s, b * 6 + (2 - k))
                    v.scalar_tensor_tensor(out=cv[:], in0=prod[:, k:k + SEQ], scalar=col(sc_half, b + 8 * k),
                                           in1=cv[:], op0=ALU.mult, op1=ALU.add).then_inc(sc_s, 1)
                for t in range(2):
                    h = slice(HALF * t, HALF * (t + 1))
                    wait(dve, sc_tanh, b * 2 + (t + 1))
                    v.scalar_tensor_tensor(out=sg[:, h], in0=sg[:, h], scalar=1.0, in1=dense[bank_of(q + 4 + t)][:],
                                           op0=ALU.add, op1=ALU.mult).then_inc(evac[bank_of(q + 4 + t)], 1)
                for t in range(2):
                    h = slice(HALF * t, HALF * (t + 1))
                    wait(dve, evac[bank_of(q + 4 + t)], use_of(q + 4 + t) + 1)
                    wait(dve, filled, q + 6 + t + 1)
                    v.tensor_tensor(sg[:, h], sg[:, h], dense[bank_of(q + 6 + t)][:],
                                    ALU.mult).then_inc(evac[bank_of(q + 6 + t)], 1)
                for t in range(2):
                    wait(dve, evac[bank_of(q + 6 + t)], use_of(q + 6 + t) + 1)
                wait(dve, sc_s, b * 6 + 3)
                v.tensor_tensor(cv[:], cv[:], sg[:], ALU.mult).then_inc(sc_s, 1)
                wait(dve, sc_s, b * 6 + 4)
                v.tensor_scalar(tile_of(hb_hi, b), cv[:], 1.0, None, ALU.mult).then_inc(sc_s, 1)
                wait(dve, sc_s, b * 6 + 5)
                v.tensor_tensor(tile_of(hb_lo, b), cv[:], tile_of(hb_hi, b), ALU.subtract).then_inc(sc_s, 1)

            run(dve, sc_block, 0, 8, peel=1)

            dve.wait_ge(p_filled, 1)
            v.scalar_tensor_tensor(out=gate_col[:], in0=pb[:, 0:8], scalar=1.0, in1=par[:, B_MOD + 16:B_MOD + 24],
                                   op0=ALU.mult, op1=ALU.add).then_inc(p_free, 1)

            def c2_pair(f):
                v.tensor_scalar(gate_slot[:], col(gate_half, f + 8, 2), 1.0, None, ALU.mult).then_inc(gslot_s, 1)
                for j in range(2):
                    q = f * 4 + Q_C2 + 4 * j
                    if f.k:
                        wait(dve, stored[j], (f.over(2)) * 16)
                    for t in range(2):
                        h = slice(HALF * t, HALF * (t + 1))
                        wait(dve, evac[bank_of(q + t)], use_of(q + t) + 1)
                        wait(dve, filled, q + 2 + t + 1)
                        v.scalar_tensor_tensor(out=mb[:, j, h], in0=tgb[:, h], scalar=1.0,
                                               in1=dense[bank_of(q + 2 + t)][:], op0=ALU.add,
                                               op1=ALU.mult).then_inc(evac[bank_of(q + 2 + t)], 1)

            run(dve, c2_pair, 0, 8, step=2, peel=1)

            def dt_steps():
                bc = dtb_row[:].unsqueeze(1).broadcast_to([P, TT, HEADS])
                dve.wait_ge(t_filled, 2)
                dve.wait_ge(heads_in, 48)
                v.tensor_tensor(dtv[0][:], tb[1][:, 0:256].rearrange("p (c h) -> p c h", c=TT), bc,
                                ALU.add).then_inc(t_free, 1)
                dve.wait_ge(t_free, 2)
                v.scalar_tensor_tensor(out=dtv[1][:], in0=dtv[0][:], scalar=-1.0, in1=dtv[0][:],
                                       op0=ALU.mult, op1=ALU.max).then_inc(dts, 1)
                dve.wait_ge(dta, 2)
                v.tensor_scalar(dtv[3][:], dtv[2][:], 1.0, None, ALU.add).then_inc(dts, 1)
                dve.wait_ge(dts, 2)
                v.tensor_scalar(dtv[5][:], dtv[3][:], -1.0, None, ALU.add).then_inc(dts, 1)
                dve.wait_ge(dts, 3)
                v.tensor_tensor(dtv[6][:], dtv[2][:], dtv[5][:], ALU.subtract).then_inc(dts, 1)
                v.reciprocal(dtv[7][:], dtv[3][:]).then_inc(dts, 1)
                dve.wait_ge(dts, 5)
                v.tensor_tensor(dtv[6][:], dtv[6][:], dtv[7][:], ALU.mult).then_inc(dts, 1)
                v.tensor_scalar(dtv[8][:], dtv[0][:], 0.0, None, ALU.max).then_inc(dts, 1)
                dve.wait_ge(dts, 7)
                v.tensor_tensor(dtv[8][:], dtv[8][:], dtv[6][:], ALU.add).then_inc(dts, 1)
                dve.wait_ge(dts, 8)
                dve.wait_ge(dta, 3)
                v.tensor_tensor(dt_t[:], dtv[8][:], dtv[4][:], ALU.add).then_inc(dts, 1)
                dve.wait_ge(dts, 9)
                v.scalar_tensor_tensor(out=a_t[:], in0=dt_t[:], scalar=-1.0,
                                       in1=exp_a[:].unsqueeze(1).broadcast_to([P, TT, HEADS]),
                                       op0=ALU.mult, op1=ALU.mult).then_inc(dts, 1)

            def y_lo_part(g, t0, k):
                t, j = k // 2, k % 2
                h = slice(HALF * t, HALF * (t + 1))
                wait(dve, yhi_s, (g + (-1)) * 4 + (k + 1))
                v.scalar_tensor_tensor(out=y_lo[:, j, h], in0=tb[t_bank(t0 + k)][:], scalar=col(par, g * 2 + (NORM_W - 2 + j)),
                                       in1=y_hi[:, j, h], op0=ALU.mult, op1=ALU.subtract).then_inc(t_free, 1)

            def add_ya(q, s):
                t, f = s // 8, s % 8
                h = slice(HALF * t, HALF * (t + 1))
                wait(dve, filled, q + 1)
                v.tensor_tensor(ya[:, f, h], ya[:, f, h], dense[bank_of(q)][:],
                                ALU.add).then_inc(evac[bank_of(q)], 1)

            def group(g):
                first = g.k == 0
                n0, q0, t0 = units_b(g)
                conv0 = g * 20

                def group_params():
                    v.tensor_scalar(ac_g[:], heads_of(acum, slice(None), g), 1.0, None, ALU.mult).then_inc(gpar_s, 1)
                    v.tensor_scalar(dt_g[:], heads_of(dt_t, slice(None), g), 1.0, None, ALU.mult).then_inc(gpar_s, 1)
                    v.tensor_scalar(te_g[:], heads_of(to_end, slice(None), g), 1.0, None, ALU.mult).then_inc(gpar_s, 1)
                    v.tensor_scalar(d_g[:], col(d_row, g * HPG, HPG), 1.0, None, ALU.mult).then_inc(gpar_s, 1)

                if not first:
                    v.tensor_scalar(nw_g[:], col(par, g * 2 + (NORM_W - 2), 2), 1.0, None, ALU.mult).then_inc(nw_s, 1)
                    group_params()
                if first:
                    dve.wait_ge(stored[0], 64)
                    dve.wait_ge(stored[1], 64)
                    dve.wait_ge(consts, 8)
                    dve.wait_ge(ya_zero, 1)

                def taps(u):
                    dst = (bf, cf, xf[0], xf[1])[u]
                    blk = (g + 16, g + 24, g * 2, g * 2 + 1)[u]
                    for t in range(2):
                        q = q0 + 2 * u + t
                        wait(dve, evac[bank_of(q)], use_of(q) + 1)
                    v.tensor_scalar(dst[:], cin[:, 3:3 + SEQ], col(conv_half, blk + 96), col(conv_half, blk + 128),
                                    ALU.mult, ALU.add).then_inc(conv_s, 1)
                    for k in (2, 1, 0):
                        wait(dve, conv_s, conv0 + (5 * u + 3 - k))
                        v.scalar_tensor_tensor(out=dst[:], in0=cin[:, k:k + SEQ], scalar=col(conv_half, blk + 32 * k),
                                               in1=dst[:], op0=ALU.mult, op1=ALU.add).then_inc(conv_s, 1)

                def silu(u):
                    dst = (bf, cf, xf[0], xf[1])[u]
                    wait(dve, conv_tanh, g * 4 + (u + 1))
                    v.scalar_tensor_tensor(out=dst[:], in0=th[:], scalar=1.0, in1=dst[:],
                                           op0=ALU.add, op1=ALU.mult).then_inc(conv_s, 1)

                if first:
                    dt_steps()
                    taps(0)
                    silu(0)
                    dve.wait_ge(t_free, 3)
                    v.tensor_tensor(to_end[:], to_end[:], dt_t[:], ALU.mult).then_inc(dts, 1)
                    dve.wait_ge(dts, 11)
                    group_params()
                    taps(1)
                    silu(1)
                    taps(2)
                    silu(2)
                    taps(3)
                    silu(3)
                else:
                    taps(0)
                    y_lo_part(g, t0, 0)
                    silu(0)
                    y_lo_part(g, t0, 1)
                    taps(1)
                    y_lo_part(g, t0, 2)
                    silu(1)
                    y_lo_part(g, t0, 3)
                    taps(2)
                    silu(2)
                    taps(3)
                    add_ya(q0 + 8, 0)
                    silu(3)
                    for s in range(1, 16):
                        add_ya(q0 + (8 + s), s)
                zq = q0 + (8 if first else 24)
                item = g * 8

                def combine(ck):
                    k = (item + ck) * 4
                    wait(dve, xw_s, (item + (ck + 1)) * 3)
                    wait(dve, y_filled, item + (ck + 1))
                    wait(dve, comb_s, k)
                    add = dx[:, ck % 2, :]
                    if ck:
                        v.tensor_tensor(yt[:].rearrange("p (h d) -> p h d", h=HPG),
                                        yb[:, 0:GW].rearrange("p (h d) -> p h d", h=HPG),
                                        heads_of(decay_in, ck, g).unsqueeze(2).broadcast_to([P, HPG, HD]),
                                        ALU.mult).then_inc(comb_s, 1)
                        wait(dve, comb_s, k + 1)
                        v.tensor_tensor(yt[:], yt[:], dx[:, ck % 2, :], ALU.add).then_inc(comb_s, 1)
                        wait(dve, comb_s, k + 2)
                        add = yt[:]
                    v.tensor_tensor(yt[:], yb[:, GW:2 * GW], add, ALU.add).then_inc(y_free, 1)
                    wait(dve, y_free, item + (ck + 1))
                    wait(dve, evac[bank_of(zq + ck)], use_of(zq + ck) + 1)
                    if ck == 0:
                        v.tensor_tensor(y[:, ck, :], yt[:], sz[:], ALU.mult).then_inc(comb_s, 4)
                    else:
                        v.tensor_tensor(y[:, ck, :], yt[:], sz[:], ALU.mult).then_inc(comb_s, 2)

                for ck in range(TT):
                    k = (item + ck) * 3
                    last = ck == TT - 1
                    wait(dve, p_filled, item + (ck + P_B + 1))
                    wait(dve, ssd_s, k)
                    v.tensor_tensor(cbm[:], pb[:, 0:P], tri[:],
                                    ALU.mult).then_inc(p_free if last else ssd_s, 1)
                    wait(dve, exp_ready, (item + (ck + 1)) * 5)
                    wait(dve, y_filled, item + (ck - 1))
                    wait(dve, *((p_free, item + (ck + P_B + 1)) if last else (ssd_s, k + 1)))
                    v.tensor_tensor(m_t[:, ck % 2, :, :], exp_s[:, ck % 2, :, :],
                                    cbm[:].unsqueeze(1).broadcast_to([P, HPG, P]),
                                    ALU.mult).then_inc(ssd_s, 3 if last else 2 if ck == 0 else 1)
                    if ck:
                        wait(dve, y_filled, item + ck)
                    if ck == 0:
                        v.tensor_copy(state[:, 0, :], pb[:, GW:2 * GW]).then_inc(p_free, 1)
                    elif not last:
                        wait(dve, p_free, item + (ck + P_B))
                        v.tensor_tensor(sdec[:].rearrange("p (h d) -> p h d", h=HPG),
                                        state[:, (ck - 1) % 2, :].rearrange("p (h d) -> p h d", h=HPG),
                                        heads_of(chunk_decay, ck, g).unsqueeze(2).broadcast_to([P, HPG, HD]),
                                        ALU.mult).then_inc(ssd_s, 1)
                        wait(dve, ssd_s, k + 3)
                        v.tensor_tensor(state[:, ck % 2, :], sdec[:], pb[:, GW:2 * GW], ALU.add).then_inc(p_free, 1)
                    if ck:
                        combine(ck - 1)
                    wait(dve, z_tanh, item + (ck + 1))
                    wait(dve, comb_s, (item + ck) * 4)
                    v.scalar_tensor_tensor(out=sz[:], in0=tz[:], scalar=1.0, in1=dense[bank_of(zq + ck)][:, 0:GW],
                                           op0=ALU.add, op1=ALU.mult).then_inc(evac[bank_of(zq + ck)], 1)
                combine(TT - 1)
                wait(dve, rms_s, g + 1)
                v.reciprocal(y_rstd[:], y_rstd[:]).then_inc(yn_s, 1)
                wait(dve, yn_s, g * 9 + 1)
                for ck in range(TT):
                    v.tensor_scalar(y[:, ck, :], y[:, ck, :], y_rstd[:, ck:ck + 1], None,
                                    ALU.mult).then_inc(yn_s, 1)

            run(dve, group, 0, GROUPS, peel=1)
            for k in range(4):
                y_lo_part(Lin(GROUPS), Lin(T_TAIL), k)
            for s in range(16):
                add_ya(Q_TAIL + s, s)
            for k in range(KT):
                if k == 0:
                    dve.wait_ge(p_free, 1)
                v.tensor_scalar(diag[:, k, :], ident[:], gate_col[:, k:k + 1], 0.5, ALU.mult,
                                ALU.mult).then_inc(diag_s, 1)
            for f in range(KT):
                for t in range(2):
                    q = (Q_D + 2 * f if f else Q_D0) + t
                    dve.wait_ge(evac[q % 4], q // 4 + 1)
                if f == 0:
                    for q in range(Q_D - 2, Q_D + 2):
                        dve.wait_ge(evac[q % 4], q // 4 + 1)
                if f:
                    dve.wait_ge(mix_s, 3 * f)
                v.scalar_tensor_tensor(out=mt[:], in0=tga[:, f % 2, :], scalar=1.0, in1=ya[:, f, :], op0=ALU.add,
                                       op1=ALU.mult).then_inc(mix_s, 1)
                dve.wait_ge(mix_s, 3 * f + 1)
                dve.wait_ge(mixb_in[f % 2], 16 * (f // 2 + 1))
                v.tensor_tensor(mt[:], mt[:], mixb[:, f % 2, :], ALU.add).then_inc(mix_s, 1)
                dve.wait_ge(mixhi_s, f + 1)
                v.tensor_tensor(mix_lo[:, f, :], mt[:], mix_hi[:, f, :], ALU.subtract).then_inc(mix_s, 1)
            dve.wait_ge(gateb_s, 2)
            dve.wait_ge(lnp_in, 32)
            for t in range(TT):
                s0 = FIN * t
                if t:
                    dve.wait_ge(fin_s, s0)
                dve.wait_ge(xr_in[t % 2], 16 * (t // 2 + 1))
                for b in range(2):
                    h = slice(512 * b, 512 * (b + 1))
                    dve.wait_ge(e_filled, 2 * t + b + 1)
                    v.tensor_tensor(res[:, h], gate_b[:, h], banks8[2 * (t % 4) + b][:], ALU.mult).then_inc(e_evac, 1)
                    dve.wait_ge(e_evac, 2 * t + b + 1)
                    v.scalar_tensor_tensor(out=res[:, h], in0=xr[:, t % 2, h], scalar=ALPHA, in1=res[:, h],
                                           op0=ALU.mult, op1=ALU.add).then_inc(fin_s, 1)
                    dve.wait_ge(fin_s, s0 + 2 * b + 1)
                    v.bn_stats(stats_e[:, b, :], res[:, h]).then_inc(fin_s, 1)
                dve.wait_ge(fin_s, s0 + 4)
                v.bn_aggr(aggr_e[:], stats_e[:].rearrange("p a b -> p (a b)")).then_inc(fin_s, 2)
                if t >= 2:
                    dve.wait_ge(out_s[t % 2], 16 * (t // 2))
                dve.wait_ge(fin_s, s0 + 6)
                v.scalar_tensor_tensor(out=ob[:, t % 2, :], in0=res[:], scalar=aggr_e[:, 0:1], in1=lng_b[:],
                                       op0=ALU.subtract, op1=ALU.mult).then_inc(fin_s, 1)
                dve.wait_ge(fin_sqrt, t + 1)
                v.reciprocal(rstd_e[:], rstd_e[:]).then_inc(fin_s, 1)
                dve.wait_ge(fin_s, s0 + 8)
                v.scalar_tensor_tensor(out=ob[:, t % 2, :], in0=ob[:, t % 2, :], scalar=rstd_e[:, 0:1],
                                       in1=lnb_b[:], op0=ALU.mult, op1=ALU.add).then_inc(fin_s, 1)

        @block.tensor
        def _(pe):
            mm = nc.tensor.matmul
            tr = nc.tensor.transpose

            def three(bank, s_hi, s_lo, m_hi, m_lo, start, stop):
                mm(bank, s_hi, m_hi, start=start, stop=False)
                mm(bank, s_hi, m_lo, start=False, stop=False)
                return mm(bank, s_lo, m_hi, start=False, stop=stop)

            def half_unit(n, q, t, a_hi=u_hi, a_lo=u_lo):
                n, q = at(n), at(q)
                s = n.mod(4)
                h = slice(HALF * t, HALF * (t + 1))
                if t == 0:
                    wait(pe, lo_done, n + 1)
                if n.k == 0 and n.c == U_C:
                    pe.wait_ge(ulo_s, (12, 16)[t])
                wait(pe, evac[bank_of(q)], use_of(q))
                for k in range(KT):
                    f = slice(P * k, P * (k + 1))
                    last = three(dense[bank_of(q)][:], w_hi[:, s, f], w_lo[:, s, f],
                                 a_hi[:, k, h], a_lo[:, k, h], k == 0, k == KT - 1)
                last.then_inc(filled, 1)

            pe.wait_ge(rows_in, 16 * 7)
            pe.wait_ge(consts, 4)
            tr(tb[0][:, 0:P], rows[:, 0, :], ident[:])
            tr(tb[0][:, P:N_PAR], rows[0:N_PAR - P, 1, :], ident[0:N_PAR - P, 0:N_PAR - P]).then_inc(t_filled, 1)
            pe.wait_ge(t_free, 1)
            for k2 in range(2):
                def x_to_features(qs):
                    for q in qs:
                        kt, t = x_fill(q)
                        pe.wait_ge(ln_s, 17 * (t + 1))
                        wait(pe, evac[q % 4], q // 4)
                        for j in range(4):
                            last = tr(dense[q % 4][:, P * j:P * (j + 1)], xt[:, 4 * t + j, P * kt:P * (kt + 1)],
                                      ident[:])
                        last.then_inc(filled, 1)

                if k2 == 0:
                    x_to_features(range(4))
                for j in range(8):
                    col0 = P * (4 * k2 + j % 4) + (j // 4) * D
                    pe.wait_ge(wm_in[col0 // 512], 16)
                    for k in range(KT):
                        last = mm((pb, yb)[k2][:, j:j + 1], wm[:, k, col0:col0 + P],
                                  par[:, C_VEC + k:C_VEC + k + 1], start=k == 0, stop=k == KT - 1)
                last.then_inc(mod_filled, 1)
                x_to_features(range(4, 8) if k2 == 0 else range(8, 16))

            def sc_block(b):
                for j in range(4):
                    for t in range(2):
                        half_unit(b * 4 + U_C + j, b * 8 + (Q_C + 2 * j + t), t)

            run(pe, sc_block, 0, 8, peel=1)
            pe.wait_ge(mod_s, 4)
            pe.wait_ge(wg_in, 16)
            for j in range(8):
                for k in range(KT):
                    last = mm(pb[:, j:j + 1], wg[:, k, P * j:P * (j + 1)],
                              par[:, C_VEC + k:C_VEC + k + 1], start=k == 0, stop=k == KT - 1)
            last.then_inc(p_filled, 1)

            def c2_pair(f):
                for j in range(2):
                    n, q = f * 2 + (U_C2 + 2 * j), f * 4 + (Q_C2 + 4 * j)
                    for t in range(2):
                        half_unit(n, q + t, t)
                    if j == 0 and f.k == 0:
                        pe.wait_ge(sc_s, 48)
                    for t in range(2):
                        half_unit(n + 1, q + 2 + t, t, hb_hi, hb_lo)

            run(pe, c2_pair, 0, 8, step=2, peel=1)
            for t in range(2):
                half_unit(U_DT, Q_DT + t, t)

            def y_transposes(g, t0, k):
                t, j = k // 2, k % 2
                if k == 0:
                    wait(pe, yn_s, g * 9)
                wait(pe, t_free, t0 + (k - 1))
                for cc in range(4):
                    last = tr(tb[t_bank(t0 + k)][:, P * cc:P * (cc + 1)], y[:, 4 * t + cc, P * j:P * (j + 1)], ident[:])
                last.then_inc(t_filled, 1)

            def ya_fill(n, q, s):
                t, f = s // 8, s % 8
                h, fs = slice(HALF * t, HALF * (t + 1)), slice(P * f, P * (f + 1))
                wait(pe, evac[bank_of(q)], use_of(q))
                for j in range(2):
                    sl = (n + j).mod(4)
                    last = three(dense[bank_of(q)][:], w_hi[:, sl, fs], w_lo[:, sl, fs],
                                 y_hi[:, j, h], y_lo[:, j, h], j == 0, j == 1)
                last.then_inc(filled, 1)

            def group(g):
                first = g.k == 0
                n0, q0, t0 = units_b(g)
                k0 = 0 if first else 4

                def halves(u, t):
                    half_unit(n0 + u, q0 + (2 * u + t), t)

                def to_tokens(k):
                    wait(pe, conv_s, g * 20 + (5, 15, 20)[k % 3])
                    wait(pe, t_free, t0 + (k0 + k - 1))
                    src = (bf, xf[0], xf[1])[k % 3]
                    for cc in range(4):
                        cs = slice(HALF * (k // 3) + P * cc, HALF * (k // 3) + P * (cc + 1))
                        last = tr(tb[t_bank(t0 + (k0 + k))][:, P * cc:P * (cc + 1)], src[:, cs], ident[:])
                    last.then_inc(t_filled, 1)

                halves(0, 0)
                if first:
                    for t in range(2):
                        pe.wait_ge(evac[(Q_DT + t) % 4], (Q_DT + t) // 4 + 1)
                    for ck in range(TT):
                        last = tr(tb[1][:, 32 * ck:32 * (ck + 1)], dt_raw[:, P * ck:P * (ck + 1)], ident[0:32, 0:32])
                    last.then_inc(t_filled, 1)
                halves(0, 1)
                if not first:
                    y_transposes(g, t0, 0)
                halves(1, 0)
                if not first:
                    y_transposes(g, t0, 1)
                halves(1, 1)
                if first:
                    pe.wait_ge(dts, 10)
                    pe.wait_ge(p_free, 1)
                    at_ = a_t[:].rearrange("p c h -> p (c h)")
                    mm(tb[0][:, 0:256], tri[:], at_, start=True, stop=True)
                    mm(tb[0][:, 256:512], strict[:], at_, start=True, stop=True).then_inc(t_filled, 1)
                    mm(pb[:, 0:256], ones[:], at_, start=True, stop=True).then_inc(p_filled, 1)
                    for k in range(2):
                        pe.wait_ge(t_free, 2 + k)
                        for ck in range(4):
                            last = mm(tb[(3 + k) % 2][0:32, P * ck:P * (ck + 1)], a_t[:, 4 * k + ck, :], tri[:],
                                      start=True, stop=True)
                        last.then_inc(t_filled, 1)
                else:
                    y_transposes(g, t0, 2)
                halves(2, 0)
                if not first:
                    y_transposes(g, t0, 3)
                halves(2, 1)
                halves(3, 0)
                halves(3, 1)
                if first:
                    for k in range(6):
                        to_tokens(k)
                else:
                    wait(pe, lo_done, n0 + 6)
                    when = {1: 0, 3: 1, 6: 2, 8: 3, 10: 4, 12: 5}
                    for s in range(16):
                        if s == 0:
                            wait(pe, t_free, t0 + 4)
                        ya_fill(n0 + 4, q0 + (8 + s), s)
                        if s in when:
                            to_tokens(when[s])
                zn, zq = n0 + (4 if first else 6), q0 + (8 if first else 24)
                item = g * 8

                def prep(ck):
                    cs = slice(P * ck, P * (ck + 1))
                    if ck == 0:
                        wait(pe, conv_s, g * 20 + 20)
                    wait(pe, p_free, item + (ck + P_B))
                    last = mm(pb[:, 0:P], bf[:, cs], cf[:, cs], start=True, stop=True)
                    if ck < TT - 1:
                        wait(pe, xw_s, (item + ck) * 3 + 1)
                        if ck % 4 == 0:
                            wait(pe, t_free, t0 + (k0 + (1 if ck == 0 else 4)))
                        last = mm(pb[:, GW:2 * GW], bt[:, ck, :], x_end[:, ck % 2, :], start=True, stop=True)
                    last.then_inc(p_filled, 1)

                def main(ck):
                    cs = slice(P * ck, P * (ck + 1))
                    wait(pe, ssd_s, (item + ck) * 3 + (3 if ck in (0, TT - 1) else 2))
                    wait(pe, xw_s, (item + ck) * 3 + (3 if ck == TT - 1 else 2))
                    if ck:
                        wait(pe, p_free, item + (ck + P_B))
                    wait(pe, y_free, item + ck)
                    if ck:
                        mm(yb[:, 0:GW], cf[:, cs], state[:, (ck - 1) % 2, :], start=True, stop=True)
                    for h in range(HPG):
                        last = mm(yb[:, GW + HD * h:GW + HD * (h + 1)], m_t[:, ck % 2, h, :],
                                  xdt[:, ck % 2, HD * h:HD * (h + 1)], start=True, stop=True)
                    last.then_inc(y_filled, 1)

                def z_tile(ck):
                    q = zq + ck
                    s = zn.mod(4)
                    cs = slice(P * ck, P * (ck + 1))
                    if ck == 0:
                        wait(pe, lo_done, zn + 2)
                    wait(pe, evac[bank_of(q)], use_of(q))
                    for k in range(KT):
                        f = slice(P * k, P * (k + 1))
                        last = three(dense[bank_of(q)][:, 0:GW], u_hi[:, k, cs], u_lo[:, k, cs],
                                     w_hi[:, s:s + 2, f], w_lo[:, s:s + 2, f], k == 0, k == KT - 1)
                    last.then_inc(filled, 1)

                prep(0)
                for ck in range(TT):
                    z_tile(ck)
                    if ck < TT - 1:
                        prep(ck + 1)
                    main(ck)

            run(pe, group, 0, GROUPS, peel=1)
            for t in range(2):
                half_unit(U_D0, Q_D0 + t, t)
            for k in range(4):
                y_transposes(Lin(GROUPS), Lin(T_TAIL), k)
            pe.wait_ge(t_free, T_TAIL + 4)
            pe.wait_ge(lo_done, U_TAIL + 2)
            for s in range(16):
                ya_fill(Lin(U_TAIL), Q_TAIL + s, s)
            for f in range(1, KT):
                for t in range(2):
                    half_unit(U_D + f, Q_D + 2 * f + t, t)
                if f == 1:
                    pe.wait_ge(diag_s, 8)
                    for k in range(KT):
                        bank = tb[(T_TAIL + k // 4) % 2]
                        last = mm(bank[:, P * (k % 4):P * (k % 4 + 1)], ones[:], diag[:, k, :], start=True, stop=True)
                        if k % 4 == 3:
                            last.then_inc(t_filled, 1)
            for b in range(4):
                pe.wait_ge(evac[b], Q_END // 4 + (1 if Q_END % 4 > b else 0))
            pe.wait_ge(gateb_s, 2)
            pe.wait_ge(p_free, P_B + 64)
            pe.wait_ge(y_free, 64)

            def out_tile(t, k, b):
                ts, cs = slice(P * t, P * (t + 1)), slice(512 * b, 512 * (b + 1))
                return three(banks8[2 * (t % 4) + b][:], mix_hi[:, k, ts], mix_lo[:, k, ts],
                             wo[k][0][:, cs], wo[k][1][:, cs], k == 0, k == KT - 1)

            for k in range(KT):
                pe.wait_ge(mix_s, 3 * (k + 1))
                pe.wait_ge(lo_done, U_E + k + 1)
                for t in range(4):
                    for b in range(2):
                        last = out_tile(t, k, b)
                        if k == KT - 1:
                            last.then_inc(e_filled, 1)
            for t in range(4, TT):
                for b in range(2):
                    pe.wait_ge(e_evac, 2 * (t - 4) + b + 1)
                    for k in range(KT):
                        last = out_tile(t, k, b)
                    last.then_inc(e_filled, 1)


_INS = ["x", "c", "w_mod", "b_mod", "w_in", "conv_ssm_w", "conv_ssm_b", "dt_bias", "a_log", "d_skip",
        "ssm_norm_w", "conv_sc_w", "w_branch_a", "w_branch_b", "w_gate", "b_gate", "w_out", "ln_g", "ln_b"]


def kernel(**inputs):
    import numpy as np
    import concourse.bacc as bacc
    from concourse.bass_utils import run_bass_kernel_spmd

    nc = bacc.Bacc("TRN2", target_bir_lowering=False, num_devices=1, dynamic_dma_scratch_size=1024)
    arrays, args = {}, []
    for name in _INS:
        a = np.ascontiguousarray(inputs[name])
        arrays[f"in_{name}"] = a
        args.append(nc.dram_tensor(f"in_{name}", a.shape, mybir.dt.from_np(a.dtype), kind="ExternalInput").ap())
    args.append(nc.dram_tensor("spill", (KT, P, SEQ), F32, kind="Internal").ap())
    args.append(nc.dram_tensor("acum", (HEADS, SEQ), F32, kind="Internal").ap())
    args.append(nc.dram_tensor("out_0", (1, SEQ, D), F32, kind="ExternalOutput").ap())
    build(nc, *args)
    r = run_bass_kernel_spmd(nc, [arrays], core_ids=[0])
    return r.results[0]["out_0"]
```

```python
import concourse.bass as bass
from concourse import mybir

F32 = mybir.dt.float32
F32R = mybir.dt.float32r
ALU = mybir.AluOpType
ACT = mybir.ActivationFunctionType

P = 128
ACT_TILES = (*range(8), 8, 10, 12, 14)
DVE_TILES = 7
SEQ = 1024
D = 1024
KT = D // P
TT = SEQ // P
HALF = 512
INNER = 2 * D
GROUPS = 8
GW = INNER // GROUPS
HEADS = 32
HPG = HEADS // GROUPS
HD = 64
XB_COL = INNER
B_COL = XB_COL + INNER
C_COL = B_COL + GROUPS * P
DT_COL = C_COL + GROUPS * P
SCB_COL = DT_COL + HEADS
SCC_COL = SCB_COL + D
SCX_COL = SCC_COL + D
SCG_COL = SCX_COL + D
LN_EPS = 1e-5
RMS_EPS = 1e-5
ALPHA = 2.0 ** 0.25

CONV_B = 128
SC_W = CONV_B + 32
B_MOD = SC_W + 24
B_GATE = B_MOD + 24
NORM_W = B_GATE + 16
C_VEC = NORM_W + 16
N_PAR = C_VEC + 8

U_C, U_C2, U_DT, U_B0 = 0, 32, 48, 49
U_B = U_B0 + 6
U_D0 = U_B + 8 * 7
U_TAIL = U_D0 + 1
U_D = U_TAIL + 1
U_E = U_D + 8
Q_C = 16
Q_C2 = Q_C + 64
Q_DT = Q_C2 + 32
Q_B0 = Q_DT + 2
Q_B = Q_B0 + 16
Q_D0 = Q_B + 32 * 7
Q_TAIL = Q_D0 + 2
Q_D = Q_TAIL + 14
Q_END = Q_D + 16
T_B0 = 5
T_B = T_B0 + 6
T_TAIL = T_B + 10 * 7
P_B = 2
FIN = 9


class Lin:

    def __init__(self, c, k=0, i=None):
        self.c, self.k, self.i = c, k, i

    def __add__(self, o):
        return Lin(self.c + o, self.k, self.i)

    def __mul__(self, o):
        return Lin(self.c * o, self.k * o, self.i)

    def over(self, d):
        assert self.k % d == 0
        return Lin(self.c // d, self.k // d, self.i)

    def mod(self, d):
        assert self.k % d == 0
        return self.c % d

    def val(self):
        return self.c if self.k == 0 else self.i * self.k + self.c


def at(v):
    return v if isinstance(v, Lin) else Lin(v)


def wait(eng, sem, value):
    v = at(value)
    if v.k == 0 and v.c <= 0:
        return
    eng.wait_ge(sem, v.val())


def run(eng, body, first, stop, step=1, peel=0):
    for n in range(first, first + peel * step, step):
        body(Lin(n))
    lo = first + peel * step
    count = (stop - lo) // step
    with eng.Fori(0, count) as i:
        body(Lin(lo, step, i))


def build(nc, x, c, w_mod, b_mod, w_in, conv_ssm_w, conv_ssm_b, dt_bias, a_log, d_skip,
          ssm_norm_w, conv_sc_w, w_branch_a, w_branch_b, w_gate, b_gate, w_out, ln_g, ln_b,
          spill, acum_dram, out):
    base = [1152]

    def place(name, shape, dt=F32, offset=None):
        size = 4
        for n in shape[1:]:
            size *= n
        size = (size + 31) // 32 * 32
        where = base[0] if offset is None else offset
        if offset is None:
            base[0] += size
        return nc.alloc_sbuf_tensor_at(name, shape, dt, offset=where)

    K = 1024
    u_base = base[0]
    u_hi = place("u_hi", [P, KT, SEQ], F32R)
    u_lo = place("u_lo", [P, KT, SEQ], F32R)
    a32 = base[0]
    base[0] += 32 * K
    raw = place("raw", [P, 2, 1024])
    w_hi = place("w_hi", [P, 4, 1024], F32R)
    w_lo = place("w_lo", [P, 4, 1024], F32R)
    ident = place("ident", [P, P])
    tri = place("tri", [P, P])
    strict = place("strict", [P, P])
    ones = place("ones", [P, P])
    par = place("par", [P, N_PAR])
    conv_half = place("conv_half", [P, 160])
    sc_half = place("sc_half", [P, 24])
    gate_half = place("gate_half", [P, 16])
    gate_slot = place("gate_slot", [P, 2])
    ac_g = place("ac_g", [P, TT, HPG])
    dt_g = place("dt_g", [P, TT, HPG])
    te_g = place("te_g", [P, TT, HPG])
    d_g = place("d_g", [P, HPG])
    nw_g = place("nw_g", [P, 2])
    shift = place("shift", [P, 8])
    scale1 = place("scale1", [P, 8])
    gate_col = place("gate_col", [P, 8])
    eps = place("eps", [P, 2])
    stats = place("stats", [P, 2, 2, 6])
    aggr = place("aggr", [P, 4, 2, 2])
    rstd = place("rstd", [P, 4, 2])
    neg_mean = place("neg_mean", [P, 4, 2])
    d_row = place("d_row", [P, HEADS])
    dtb_row = place("dtb_row", [P, HEADS])
    exp_a = place("exp_a", [P, HEADS])
    dt_t = place("dt_t", [P, TT, HEADS])
    decay_in = place("decay_in", [P, TT, HEADS])
    to_end = place("to_end", [P, TT, HEADS])
    chunk_decay = place("chunk_decay", [P, TT, HEADS])
    acum = place("acum", [P, TT, HEADS])
    sq_sum = place("sq_sum", [P, TT])
    y_rstd = place("y_rstd", [P, TT])
    stats_e = place("stats_e", [P, 2, 6])
    aggr_e = place("aggr_e", [P, 2])
    rstd_e = place("rstd_e", [P, 1])
    r0 = base[0]

    def in_r(name, shape, kb, dt=F32):
        return place(name, shape, dt, offset=r0 + int(kb * K))

    xt = place("xt", [P, TT, D], F32, offset=a32)
    wm = in_r("wm", [P, KT, 2048], 0)
    uf = in_r("uf", [P, 2, HALF], 64)
    rows = in_r("rows", [P, 2, P], 68)
    ufv = in_r("ufv", [P, HALF], 70)
    alog_row = in_r("alog_row", [P, HEADS], 69)
    wg = place("wg", [P, KT, 1024], F32, offset=a32)
    hb_hi = in_r("hb_hi", [P, KT, SEQ], 0, F32R)
    hb_lo = in_r("hb_lo", [P, KT, SEQ], 32, F32R)
    cv = in_r("cv", [P, SEQ], 64)
    sg = in_r("sg", [P, SEQ], 68)
    prod = in_r("prod", [P, SEQ + 2], 72)
    tgb = in_r("tgb", [P, SEQ], 64)
    mb = in_r("mb", [P, 2, SEQ], 68)
    ya = place("ya", [P, KT, SEQ], F32, offset=a32)
    bf = in_r("bf", [P, SEQ], 0)
    cf = in_r("cf", [P, SEQ], 4)
    xf = [in_r("xf0", [P, SEQ], 8), in_r("xf1", [P, SEQ], 12)]
    xs = in_r("xs", [P, TT, GW], 16)
    bt = in_r("bt", [P, TT, P], 24)
    th = in_r("th", [P, SEQ], 28)
    cin = in_r("cin", [P, SEQ + 3], 32)
    y = in_r("y", [P, TT, GW], 36.25)
    x_end = in_r("x_end", [P, 2, GW], 44.25)
    xdt = in_r("xdt", [P, 2, GW], 46.25)
    dx = in_r("dx", [P, 2, GW], 48.25)
    acb = in_r("acb", [P, 2, HPG, 2 * P], 50.25)
    y_hi = in_r("y_hi", [P, 2, SEQ], 59.75, F32R)
    y_lo = in_r("y_lo", [P, 2, SEQ], 67.75, F32R)
    exp_s = in_r("exp_s", [P, 2, HPG, P], 59.75)
    m_t = in_r("m_t", [P, 2, HPG, P], 63.75)
    cbm = in_r("cbm", [P, P], 67.75)
    yt = in_r("yt", [P, GW], 68.25)
    state = in_r("state", [P, 2, GW], 69.25)
    tz = in_r("tz", [P, GW], 71.25)
    sz = in_r("sz", [P, GW], 72.25)
    sdec = in_r("sdec", [P, GW], 73.25)
    sqj = in_r("sqj", [P, GW], 74.25)
    dt_raw = in_r("dt_raw", [32, SEQ], 36.25)
    acum_t = in_r("acum_t", [32, SEQ], 40.25)
    dtv = [in_r(f"dtv{k}", [P, TT, HEADS], 59.75 + k) for k in range(9)]
    a_t = in_r("a_t", [P, TT, HEADS], 44.25)
    mix_hi = in_r("mix_hi", [P, KT, SEQ], 0, F32R)
    mix_lo = place("mix_lo", [P, KT, SEQ], F32R, offset=a32)
    gate_b = in_r("gate_b", [P, D], 32)
    lng_b = in_r("lng_b", [P, D], 36)
    lnb_b = in_r("lnb_b", [P, D], 40)
    diag = in_r("diag", [P, KT, P], 44)
    mt = in_r("mt", [P, SEQ], 48)
    tga = in_r("tga", [P, 2, SEQ], 52)
    mixb = in_r("mixb", [P, 2, SEQ], 60)
    xr = in_r("xr", [P, 2, D], 68)
    res = in_r("res", [P, D], 52)
    ob = in_r("ob", [P, 2, D], 56)
    wo_hi = place("wo_hi", [P, 4, D], F32R, offset=u_base)
    wo_lo = place("wo_lo", [P, 4, D], F32R, offset=u_base + 32 * K)

    wo = [(w_hi[:, (U_E + k) % 4, :], w_lo[:, (U_E + k) % 4, :]) if k < 4 else (wo_hi[:, k - 4, :], wo_lo[:, k - 4, :])
          for k in range(KT)]
    assert base[0] <= r0 and r0 + 76 * K <= nc.sbuf_usable_end, (base[0], r0)

    dense = [nc.alloc_psum_tensor(f"dense{k}", [P, 512], F32) for k in range(4)]
    tb = [nc.alloc_psum_tensor(f"tb{k}", [P, 512], F32) for k in range(2)]
    pb = nc.alloc_psum_tensor("pb", [P, 512], F32)
    yb = nc.alloc_psum_tensor("yb", [P, 512], F32)
    banks8 = tb + [pb, yb] + dense

    S = nc.alloc_semaphore
    x_in = [S(f"x_in{k}") for k in range(4)]
    wm_in = [S(f"wm_in{k}") for k in range(4)]
    wg_in = S("wg_in")
    rows_in = S("rows_in")
    heads_in = S("heads_in")
    w_in_s = [S("raw_in0"), S("raw_in1")]
    hi_done = S("hi_done")
    lo_done = S("lo_done")
    filled = S("filled")
    evac = [S(f"evac{k}") for k in range(4)]
    t_filled, t_free = S("t_filled"), S("t_free")
    exp_ready = S("exp_ready")
    acum_stored = S("acum_stored")
    acb_in = [S("acb_in0"), S("acb_in1")]
    p_filled, p_free = S("p_filled"), S("p_free")
    y_filled, y_free = S("y_filled"), S("y_free")
    consts = S("consts")
    par_ready = S("par_ready")
    ln_s = S("ln_steps")
    ln_sqrt = S("ln_sqrt")
    mod_filled = S("mod_filled")
    mod_s = S("mod_steps")
    uhi_s = S("u_hi_written")
    ulo_s = S("u_lo_by_pool")
    uv_s = S("u_steps_by_vector")
    sc_s = S("sc_steps")
    sc_tanh = S("sc_tanh")
    gslot_s = S("gate_slot_written")
    gpar_s = S("group_params")
    stored = [S("mb_stored0"), S("mb_stored1")]
    dts = S("dt_steps")
    xn_s = S("x_normed")
    nm_s = S("mean_and_deviation")
    wsum_s = S("weighted_row_steps")
    dta = S("dt_act_steps")
    ya_zero = S("ya_zeroed")
    conv_s = S("conv_steps")
    conv_tanh = S("conv_tanh")
    yhi_s = S("y_hi_written")
    xw_s = S("x_weighted")
    ssd_s = S("ssd_steps")
    z_tanh = S("z_tanh")
    comb_s = S("combine_steps")
    sq_s = S("squares")
    rms_s = S("rms_sqrt")
    yn_s = S("y_normed")
    mixb_in = [S("mixb_in0"), S("mixb_in1")]
    mix_s = S("mix_steps")
    mixhi_s = S("mix_hi_written")
    diag_s, gateb_s = S("diag_ready"), S("gate_b_ready")
    nw_s = S("norm_weight_slot")
    lnp_in = S("ln_params_in")
    xr_in = [S("xr_in0"), S("xr_in1")]
    e_filled, e_evac = S("out_filled"), S("out_evacuated")
    fin_s, fin_sqrt = S("final_steps"), S("final_sqrt")
    out_s = [S("out_stored0"), S("out_stored1")]

    def x_fill(q):
        return q // 8 * 4 + q % 4, q // 4 % 2

    def bank_of(q):
        return at(q).mod(4)

    def t_bank(k):
        return at(k).mod(2)

    def use_of(q):
        return at(q).over(4) if at(q).k else Lin(at(q).c // 4)

    def w_cols(w, col, width=P):
        v = at(col)
        cols = w[:, v.c:v.c + width] if v.k == 0 else w[:, bass.ds(nc.sync.snap(v.val()), width)]
        return cols.rearrange("(k p) f -> p k f", p=P)

    def w_rows(w, row_tile):
        v = at(row_tile) * P
        return w[v.c:v.c + P, :] if v.k == 0 else w[bass.ds(nc.sync.snap(v.val()), P), :]

    def col(t, j, n=1):
        v = at(j)
        return t[:, v.c:v.c + n] if v.k == 0 else t[:, bass.ds(v.val(), n)]

    def heads_of(t, ck, g):
        v = at(g) * HPG
        return t[:, ck, v.c:v.c + HPG] if v.k == 0 else t[:, ck, bass.ds(v.val(), HPG)]

    def head_col(t, ck, g, h):
        v = at(g) * HPG + h
        return t[:, ck, v.c:v.c + 1] if v.k == 0 else t[:, ck, bass.ds(v.val(), 1)]

    def tile_of(t, f):
        v = at(f)
        return t[:, v.c, :] if v.k == 0 else t[:, bass.ds(v.val(), 1), :].rearrange("p a n -> p (a n)")

    win, wmod, wgate = w_in[0], w_mod[0], w_gate[0]
    wa, wb, wout = w_branch_a[0], w_branch_b[0], w_out[0]

    def units_b(g):
        if at(g).k == 0 and at(g).c == 0:
            return Lin(U_B0), Lin(Q_B0), Lin(T_B0)
        g1 = at(g) + (-1)
        return g1 * 8 + U_B, g1 * 32 + Q_B, g1 * 10 + T_B

    with nc.Block() as block:

        @block.sync
        def _(sp):
            def load(n, src):
                n = at(n)
                wait(sp, lo_done, n + (-1))
                dst = raw[:, n.mod(2), :]
                if len(src.shape) == 3:
                    dst = dst.rearrange("p (k f) -> p k f", k=KT)
                sp.dma_start(dst, src).then_inc(w_in_s[n.mod(2)], 16)

            for t in range(4):
                sp.dma_start(xt[:, 2 * t:2 * t + 2, :],
                             x[0, 2 * P * t:2 * P * (t + 1), :].rearrange("(t p) d -> p t d", p=P)
                             ).then_inc(x_in[t], 16)
            sp.dma_start(rows[:, 0, :], conv_ssm_w.rearrange("a t (b p) -> (a t b) p", p=P)).then_inc(rows_in, 16)
            r = 0
            for src in (conv_ssm_b.rearrange("a (b p) -> (a b) p", p=P),
                        conv_sc_w.rearrange("a t (b p) -> (a t b) p", p=P),
                        b_mod.rearrange("a (b p) -> (a b) p", p=P),
                        b_gate.rearrange("a (b p) -> (a b) p", p=P),
                        ssm_norm_w.rearrange("a (b p) -> (a b) p", p=P),
                        c.rearrange("a (b p) -> (a b) p", p=P)):
                sp.dma_start(rows[r:r + src.shape[0], 1, :], src).then_inc(rows_in, 16)
                r += src.shape[0]
            for dst, src in ((dtb_row, dt_bias), (alog_row, a_log), (d_row, d_skip)):
                sp.dma_start(dst[:], src.partition_broadcast(P).rearrange("p a d -> p (a d)")).then_inc(heads_in, 16)
            for k in (0, 2, 1, 3):
                sp.dma_start(wm[:, :, 512 * k:512 * (k + 1)],
                             w_cols(wmod, 512 * k, 512)).then_inc(wm_in[k], 16)

            def sc_units(b):
                for j, start in enumerate((SCC_COL, SCX_COL, SCG_COL, SCB_COL)):
                    load(b * 4 + U_C + j, w_cols(win, b * P + start))
                    if b.k == 0 and j == 3:
                        sp.wait_ge(filled, 16)
                        sp.dma_start(wg[:], w_cols(wmod, 2048, 1024)).then_inc(wg_in, 16)

            run(sp, sc_units, 0, 8, peel=1)

            def c2_units(f):
                for j in range(2):
                    load(f * 2 + U_C2 + 2 * j, w_cols(wgate, f * P + D + j * P))
                    load(f * 2 + U_C2 + 2 * j + 1, w_cols(wb, f * P + j * P))

            for f in range(0, 8, 2):
                c2_units(Lin(f))
            load(U_DT, w_cols(win, DT_COL))

            def group_units(g):
                n0, _, _ = units_b(g)
                first = g.k == 0
                load(n0, w_cols(win, g * P + B_COL))
                load(n0 + 1, w_cols(win, g * P + C_COL))
                load(n0 + 2, w_cols(win, g * GW + XB_COL))
                load(n0 + 3, w_cols(win, g * GW + XB_COL + P))
                if not first:
                    load(n0 + 4, w_rows(wa, g * 2 + (-2)))
                    load(n0 + 5, w_rows(wa, g * 2 + (-1)))
                zn = n0 + (4 if first else 6)
                load(zn, w_cols(win, g * GW))
                load(zn + 1, w_cols(win, g * GW + P))

            run(sp, group_units, 0, GROUPS, peel=1)
            load(U_D0, w_cols(wgate, 0))
            load(U_TAIL, w_rows(wa, 14))
            load(U_TAIL + 1, w_rows(wa, 15))
            for f in range(1, 5):
                load(U_D + f, w_cols(wgate, f * P))
            sp.wait_ge(filled, Q_D + 2)
            sp.wait_ge(stored[0], 64)
            sp.wait_ge(stored[1], 64)
            sp.dma_start(mixb[:, 0, :], spill[0]).then_inc(mixb_in[0], 16)
            sp.dma_start(mixb[:, 1, :], spill[1]).then_inc(mixb_in[1], 16)
            sp.dma_start(lng_b[:], ln_g.partition_broadcast(P).rearrange("p a d -> p (a d)")).then_inc(lnp_in, 16)
            sp.dma_start(lnb_b[:], ln_b.partition_broadcast(P).rearrange("p a d -> p (a d)")).then_inc(lnp_in, 16)
            for f in range(2, KT):
                load(U_D + f + 3, w_cols(wgate, (f + 3) * P) if f + 3 < KT else w_rows(wout, f + 3 - KT))
                sp.wait_ge(mix_s, 3 * (f - 2) + 2)
                sp.dma_start(mixb[:, f % 2, :], spill[f]).then_inc(mixb_in[f % 2], 16)
            for t in range(2):
                sp.dma_start(xr[:, t, :], x[0, P * t:P * (t + 1), :]).then_inc(xr_in[t], 16)
            for k in range(3, KT):
                load(U_E + k, w_rows(wout, k))
            for t in range(TT):
                for b in range(2 if t == TT - 1 else 1):
                    h = slice(512 * b, 512 * (b + 1)) if t == TT - 1 else slice(0, D)
                    sp.wait_ge(fin_s, FIN * (t + 1) + b)
                    sp.dma_start(out[0, P * t:P * (t + 1), h], ob[:, t % 2, h]).then_inc(out_s[t % 2], 16)
                if t + 2 < TT:
                    sp.dma_start(xr[:, t % 2, :], x[0, P * (t + 2):P * (t + 3), :]).then_inc(xr_in[t % 2], 16)
            sp.wait_ge(out_s[0], 64)
            sp.wait_ge(out_s[1], 80)

        @block.scalar
        def _(act):
            nc_act = nc.scalar

            def split_hi(n, done):
                n = at(n)
                wait(act, w_in_s[n.mod(2)], (n.over(2) if n.k else Lin(n.c // 2)) * 16 + 16)
                wait(act, filled, done)
                nc_act.copy(w_hi[:, n.mod(4), :], raw[:, n.mod(2), :]).then_inc(hi_done, 1)

            act.wait_ge(consts, 6)
            nc_act.activation(rstd[:, 0, 0:1], eps[:, 0:1], ACT.Sqrt).then_inc(ln_sqrt, 1)
            act.wait_ge(ln_sqrt, 1)

            def deviation(t):
                act.wait_ge(ln_s, 6 * t + 6)
                nc_act.activation(rstd[:, t, :], aggr[:, t, :, 1], ACT.Sqrt, bias=eps[:, 0:1]).then_inc(ln_sqrt, 1)

            deviation(0)
            for t in range(4):
                act.wait_ge(nm_s, 2 * t + 1)
                for j in range(2):
                    x_tile = xt[:, 2 * t + j, :]
                    nc_act.activation(x_tile, x_tile, ACT.Identity, bias=neg_mean[:, t, j:j + 1]).then_inc(xn_s, 1)
                if t < 3:
                    deviation(t + 1)
                if t == 2:
                    act.wait_ge(t_filled, 1)
                    nc_act.copy(par[:], tb[0][:, 0:N_PAR]).then_inc(t_free, 1)
                act.wait_ge(nm_s, 2 * t + 2)
                for j in range(2):
                    x_tile = xt[:, 2 * t + j, :]
                    act.wait_ge(xn_s, 4 * t + j + 1)
                    nc_act.mul(x_tile, x_tile, rstd[:, t, j:j + 1]).then_inc(xn_s, 1)
            for i, q in enumerate(ACT_TILES):
                kt, t = x_fill(q)
                act.wait_ge(filled, q + 1)
                if q % 8 == 0:
                    act.wait_ge(mod_s, 4 * (q // 8 + 1))
                if i >= 2:
                    act.wait_ge(ulo_s, i - 1)
                nc_act.activation(uf[:, i % 2, :], dense[q % 4][:], ACT.Identity, bias=shift[:, kt:kt + 1],
                                  scale=scale1[:, kt:kt + 1]).then_inc(evac[q % 4], 1)
                act.wait_ge(evac[q % 4], q // 4 + 1)
                nc_act.copy(u_hi[:, kt, HALF * t:HALF * (t + 1)], uf[:, i % 2, :]).then_inc(uhi_s, 1)
                if i in (7, 9):
                    split_hi((i - 7) // 2, 0)
            for n in (2, 3):
                split_hi(n, 0)
            act.wait_ge(heads_in, 48)
            nc_act.activation(exp_a[:], alog_row[:], ACT.Exp).then_inc(dta, 1)

            def sc_block(b):
                n, q = b * 4 + U_C, b * 8 + Q_C
                for t in range(2):
                    if t == 0 and b.k == 0:
                        act.wait_ge(ulo_s, 12)
                    elif t == 0:
                        wait(act, sc_s, b * 6)
                    wait(act, filled, q + t + 1)
                    nc_act.copy(cv[:, HALF * t:HALF * (t + 1)],
                                dense[bank_of(q + t)][:]).then_inc(evac[bank_of(q + t)], 1)
                split_hi(n + 4, q + 2)
                split_hi(n + 5, q + 4)
                for t in range(2):
                    wait(act, filled, q + 4 + t + 1)
                    nc_act.activation(sg[:, HALF * t:HALF * (t + 1)], dense[bank_of(q + 4 + t)][:],
                                      ACT.Tanh, scale=0.5).then_inc(sc_tanh, 1)
                split_hi(n + 6, q + 6)
                split_hi(n + 7, q + 8)

            run(act, sc_block, 0, 8, peel=1)

            def store_mb(f, j):
                q = f * 4 + Q_C2 + 2
                for t in range(2):
                    wait(act, evac[bank_of(q + t)], use_of(q + t) + 1)
                dst = spill[f.c] if f.k == 0 else spill[bass.ds(f.val(), 1)].rearrange("a p n -> (a p) n")
                act.dma_start(dst, mb[:, j, :]).then_inc(stored[j], 16)

            def c2_pair(f):
                for j in range(2):
                    n, q = f * 2 + U_C2 + 2 * j, f * 4 + Q_C2 + 4 * j
                    if j == 0:
                        wait(act, gslot_s, f.over(2) + 1 if f.k else 1)
                    if j or f.k:
                        store_mb(f + (j - 1), 1 - j)
                    for t in range(2):
                        if j == 0 and t == 0 and f.k == 0:
                            act.wait_ge(sc_s, 48)
                        wait(act, filled, q + t + 1)
                        wait(act, evac[bank_of(q + t + 2)], use_of(q + t + 2))
                        nc_act.activation(tgb[:, HALF * t:HALF * (t + 1)], dense[bank_of(q + t)][:],
                                          ACT.Tanh, scale=0.5, bias=gate_slot[:, j:j + 1]
                                          ).then_inc(evac[bank_of(q + t)], 1)
                    split_hi(n + 4, q + 2)
                    split_hi(n + 5, q + 4)

            run(act, c2_pair, 0, 8, step=2, peel=1)
            store_mb(Lin(7), 1)

            for t in range(2):
                act.wait_ge(filled, Q_DT + t + 1)
                nc_act.copy(dt_raw[:, HALF * t:HALF * (t + 1)],
                            dense[(Q_DT + t) % 4][0:32, :]).then_inc(evac[(Q_DT + t) % 4], 1)
            split_hi(U_DT + 4, Q_DT + 2)

            def dt_acts():
                act.wait_ge(dts, 1)
                nc_act.activation(dtv[2][:], dtv[1][:], ACT.Exp, scale=-1.0).then_inc(dta, 1)
                act.wait_ge(dts, 2)
                nc_act.activation(dtv[4][:], dtv[3][:], ACT.Ln).then_inc(dta, 1)

            def decay_acts():
                act.wait_ge(t_filled, 3)
                flat = "p c h -> p (c h)"
                nc_act.activation(decay_in[:].rearrange(flat), tb[0][:, 0:256], ACT.Exp).then_inc(dta, 1)
                nc_act.activation(to_end[:].rearrange(flat), tb[0][:, 256:512], ACT.Exp).then_inc(dta, 1)
                nc_act.copy(acum[:].rearrange(flat), tb[0][:, 0:256]).then_inc(t_free, 1)
                act.wait_ge(p_filled, 2)
                nc_act.activation(chunk_decay[:].rearrange(flat), pb[:, 0:256], ACT.Exp).then_inc(p_free, 1)

            def store_acum():
                for k in range(2):
                    act.wait_ge(t_filled, 4 + k)
                    nc_act.copy(acum_t[:, HALF * k:HALF * (k + 1)], tb[(3 + k) % 2][0:32, :]).then_inc(t_free, 1)
                act.wait_ge(t_free, 5)
                act.dma_start(acum_dram, acum_t[:]).then_inc(acum_stored, 16)

            def group(g):
                first = g.k == 0
                n0, q0, t0 = units_b(g)
                conv0 = g * 25
                tt = [0]

                def load_acb(g, cp):
                    v = at(g) * HPG
                    rows_ = slice(v.c, v.c + HPG) if v.k == 0 else bass.ds(nc.scalar.snap(v.val()), HPG)
                    src = acum_dram[rows_, 2 * P * cp:2 * P * (cp + 1)].partition_broadcast(P)
                    wait(act, exp_ready, g * 40 + 10 * (cp - 1))
                    act.dma_start(acb[:, cp % 2, :, :], src).then_inc(acb_in[cp % 2], 16)

                def evac_half(u, t):
                    q = q0 + 2 * u + t
                    if t == 0:
                        wait(act, conv_s, conv0 + (5 * u - 1))
                    wait(act, filled, q + 1)
                    nc_act.copy(cin[:, 3 + HALF * t:3 + HALF * (t + 1)],
                                dense[bank_of(q)][:]).then_inc(evac[bank_of(q)], 1)

                def tanh(u, t=None):
                    src = (bf, cf, xf[0], xf[1])[u]
                    h = slice(0, SEQ) if t is None else slice(HALF * t, HALF * (t + 1))
                    wait(act, conv_s, conv0 + (5 * (u + (t or 0)) + 4))
                    nc_act.activation(th[:, h], src[:, h], ACT.Tanh).then_inc(conv_tanh, 1)

                def y_hi_part():
                    k = tt[0]
                    if k == 0:
                        wait(act, nw_s, g)
                    t, j = k // 2, k % 2
                    wait(act, t_filled, t0 + k + 1)
                    nc_act.activation(y_hi[:, j, HALF * t:HALF * (t + 1)], tb[t_bank(t0 + k)][:], ACT.Copy,
                                      scale=nw_g[:, j:j + 1]).then_inc(yhi_s, 1)
                    tt[0] += 1

                def from_transposes(k):
                    k0 = 0 if first else 4
                    wait(act, t_filled, t0 + (k0 + k + 1))
                    src = tb[t_bank(t0 + (k0 + k))][:].rearrange("p (c n) -> p c n", c=4)
                    cs = slice(4 * (k // 3), 4 * (k // 3) + 4)
                    dst = bt[:, cs, :] if k % 3 == 0 else xs[:, cs, P * (k % 3 - 1):P * (k % 3)]
                    nc_act.copy(dst, src).then_inc(t_free, 1)

                evac_half(0, 0)
                evac_half(0, 1)
                split_hi(n0 + 4, q0 + 2)
                if first:
                    dt_acts()
                else:
                    y_hi_part()
                tanh(0)
                evac_half(1, 0)
                if not first:
                    y_hi_part()
                evac_half(1, 1)
                split_hi(n0 + 5, q0 + 4)
                if first:
                    decay_acts()
                else:
                    y_hi_part()
                tanh(1)
                evac_half(2, 0)
                if first:
                    store_acum()
                else:
                    y_hi_part()
                evac_half(2, 1)
                split_hi(n0 + 6, q0 + 6)
                tanh(2)
                evac_half(3, 0)
                wait(act, acum_stored, 16)
                for cp in range(2):
                    load_acb(g, cp)
                tanh(3, 0)
                evac_half(3, 1)
                if first:
                    for k in range(2):
                        from_transposes(k)
                if first:
                    from_transposes(2)
                else:
                    split_hi(n0 + 7, q0 + 8)
                tanh(3, 1)
                if not first:
                    for k in range(6):
                        from_transposes(k)
                zq = q0 + (8 if first else 24)
                item = g * 8

                def square(ck):
                    wait(act, comb_s, (item + (ck + 1)) * 4)
                    if ck:
                        wait(act, sq_s, item + ck)
                    nc_act.activation(sqj[:], y[:, ck, :], ACT.Square,
                                      accum_out=sq_sum[:, ck:ck + 1]).then_inc(sq_s, 1)

                def decay(ck):
                    if ck % 2 == 0:
                        wait(act, acb_in[ck // 2 % 2], g * 32 + 16 * (ck // 4 + 1))
                    wait(act, ssd_s, (item + (ck - 1)) * 3)
                    for h in range(HPG):
                        nc_act.activation(exp_s[:, ck % 2, h, :], acb[:, ck // 2 % 2, h, P * (ck % 2):P * (ck % 2 + 1)],
                                          ACT.Relu, scale=-1.0, bias=ac_g[:, ck, h:h + 1]).then_inc(exp_ready, 1)
                    wait(act, exp_ready, (item + ck) * 5 + 4)
                    nc_act.activation(exp_s[:, ck % 2, :, :], exp_s[:, ck % 2, :, :], ACT.Exp,
                                      scale=-1.0).then_inc(exp_ready, 1)
                    if ck in (1, 3):
                        load_acb(g, ck // 2 + 2)

                wait(act, gpar_s, g * 4 + 4)
                if not first:
                    wait(act, filled, q0 + 24)
                decay(0)
                decay(1)
                for ck in range(TT):
                    wait(act, filled, zq + (ck + 1))
                    if ck:
                        wait(act, evac[bank_of(zq + (ck - 1))], use_of(zq + (ck - 1)) + 1)
                    nc_act.activation(tz[:], dense[bank_of(zq + ck)][:, 0:GW], ACT.Tanh,
                                      scale=0.5).then_inc(z_tanh, 1)
                    if ck:
                        square(ck - 1)
                    if ck + 2 < TT:
                        decay(ck + 2)
                    if first and ck < 3:
                        from_transposes(3 + ck)
                    if first and ck == 3:
                        split_hi(n0 + 7, q0 + 8)
                    if not first and ck < 2:
                        split_hi(n0 + 8 + ck, q0 + 24)
                square(TT - 1)
                wait(act, sq_s, item + 8)
                nc_act.activation(y_rstd[:], sq_sum[:], ACT.Sqrt, bias=eps[:, 1:2],
                                  scale=1.0 / GW).then_inc(rms_s, 1)
                split_hi(n0 + (8 if first else 10), zq + 8)
                split_hi(n0 + (9 if first else 11), zq + 8)

            run(act, group, 0, GROUPS, peel=1)

            def gate_tanh(f, t):
                q = (Q_D + 2 * f if f else Q_D0) + t
                act.wait_ge(filled, q + 1)
                if t == 0 and f >= 2:
                    act.wait_ge(mix_s, 3 * f - 5)
                nc_act.activation(tga[:, f % 2, HALF * t:HALF * (t + 1)], dense[q % 4][:], ACT.Tanh,
                                  scale=0.5, bias=gate_half[:, f:f + 1]).then_inc(evac[q % 4], 1)

            for t in range(2):
                gate_tanh(0, t)
                for j in range(2):
                    k = 2 * t + j
                    act.wait_ge(t_filled, T_TAIL + k + 1)
                    nc_act.activation(y_hi[:, j, HALF * t:HALF * (t + 1)], tb[(T_TAIL + k) % 2][:], ACT.Copy,
                                      scale=par[:, NORM_W + 14 + j:NORM_W + 15 + j]).then_inc(yhi_s, 1)
            split_hi(U_D0 + 4, Q_TAIL)
            split_hi(U_TAIL + 4, Q_D + 2)
            split_hi(U_TAIL + 5, Q_D + 2)
            for f in range(KT):
                if f == 2:
                    for b in range(2):
                        act.wait_ge(t_filled, T_TAIL + 5 + b)
                        nc_act.copy(gate_b[:, 512 * b:512 * (b + 1)], tb[(T_TAIL + b) % 2][:]).then_inc(gateb_s, 1)
                act.wait_ge(mix_s, 3 * f + 2)
                nc_act.copy(mix_hi[:, f, :], mt[:]).then_inc(mixhi_s, 1)
                if f + 1 < KT:
                    for t in range(2):
                        gate_tanh(f + 1, t)
                    split_hi(U_D + f + 5, Q_D + 2 * f + 4)
            for k in range(4, KT):
                n = U_E + k
                act.wait_ge(filled, Q_END)
                act.wait_ge(w_in_s[n % 2], 16 * (n // 2 + 1))
                nc_act.copy(wo[k][0], raw[:, n % 2, :]).then_inc(hi_done, 1)
            for t in range(TT):
                act.wait_ge(fin_s, FIN * t + 6)
                nc_act.activation(rstd_e[:], aggr_e[:, 1:2], ACT.Sqrt, bias=eps[:, 0:1]).then_inc(fin_sqrt, 1)

        @block.gpsimd
        def _(pool):
            g_ = nc.gpsimd
            g_.memset(ones[:], 1.0).then_inc(consts, 1)
            g_.memset(eps[:, 0:1], LN_EPS).then_inc(consts, 1)
            g_.memset(eps[:, 1:2], 4 * RMS_EPS).then_inc(consts, 1)
            pool.wait_ge(consts, 3)
            g_.affine_select(out=ident[:], in_=ones[:], compare_op=ALU.is_equal, fill=0.0, base=0,
                             pattern=[[-1, P]], channel_multiplier=1).then_inc(consts, 1)
            g_.affine_select(out=tri[:], in_=ones[:], compare_op=ALU.is_ge, fill=0.0, base=0,
                             pattern=[[1, P]], channel_multiplier=-1).then_inc(consts, 1)
            g_.affine_select(out=strict[:], in_=ones[:], compare_op=ALU.is_gt, fill=0.0, base=0,
                             pattern=[[-1, P]], channel_multiplier=1).then_inc(consts, 1)

            def split_lo(n, dst=None):
                n = at(n)
                wait(pool, hi_done, n + 1)
                hi = w_hi[:, n.mod(4), :] if dst is None else wo[dst][0]
                lo = w_lo[:, n.mod(4), :] if dst is None else wo[dst][1]
                g_.tensor_tensor(lo, raw[:, n.mod(2), :], hi, ALU.subtract).then_inc(lo_done, 1)

            def four(n):
                for j in range(4):
                    split_lo(n + j)

            for i, q in enumerate(ACT_TILES):
                kt, t = x_fill(q)
                h = slice(HALF * t, HALF * (t + 1))
                pool.wait_ge(uhi_s, i + 1)
                g_.tensor_tensor(u_lo[:, kt, h], uf[:, i % 2, :], u_hi[:, kt, h], ALU.subtract).then_inc(ulo_s, 1)
                if i in (7, 9):
                    split_lo((i - 7) // 2)
            for n in range(2, 4):
                split_lo(n)
            pool.wait_ge(ulo_s, 12)
            g_.memset(prod[:, 0:2], 0.0).then_inc(consts, 1)
            run(pool, four, 4, U_DT, step=4)
            for n in range(U_DT, U_DT + 4):
                split_lo(n)
            pool.wait_ge(p_filled, 1)
            g_.memset(ya[:], 0.0).then_inc(ya_zero, 1)
            pool.wait_ge(filled, Q_DT)
            g_.memset(cin[:, 0:3], 0.0).then_inc(consts, 1)
            split_lo(U_DT + 4)

            def group(g):
                first = g.k == 0
                n0, q0, _ = units_b(g)
                for j in range(3 if first else 4):
                    split_lo(n0 + 4 + j)
                item = g * 8
                xs_ready = units_b(g)[2] + (6 if first else 10)
                wait(pool, gpar_s, g * 4 + 4)
                for ck in range(TT):
                    if ck % 4 == 0:
                        wait(pool, t_free, xs_ready + (-3 if ck == 0 else 0))
                    x4 = xs[:, ck, :].rearrange("p (h d) -> p h d", h=HPG)

                    def weigh(dst, w, n=1):
                        g_.tensor_tensor(dst[:, ck % 2, :].rearrange("p (h d) -> p h d", h=HPG), x4,
                                         w.unsqueeze(2).broadcast_to([P, HPG, HD]), ALU.mult).then_inc(xw_s, n)

                    wait(pool, y_filled, item + (ck - 1))
                    if ck < TT - 1:
                        weigh(x_end, te_g[:, ck, :])
                    weigh(xdt, dt_g[:, ck, :], 1 if ck < TT - 1 else 2)
                    wait(pool, comb_s, (item + (ck - 1)) * 4)
                    weigh(dx, d_g[:])
                    if not first and ck in (2, 3):
                        split_lo(n0 + 6 + ck)
                    if first and ck == 5:
                        split_lo(n0 + 7)
                e = 8 if first else 10
                split_lo(n0 + e)
                split_lo(n0 + e + 1)

            run(pool, group, 0, GROUPS, peel=1)
            for n in range(U_D0 + 4, U_E):
                split_lo(n)
            for k in range(KT):
                split_lo(U_E + k, dst=k)

        @block.vector
        def _(dve):
            v = nc.vector
            for t in range(4):
                dve.wait_ge(x_in[t], 16)
                if t:
                    dve.wait_ge(ln_s, 6 * t)
                for j in range(2):
                    for k in range(2):
                        v.bn_stats(stats[:, j, k, :], xt[:, 2 * t + j, 512 * k:512 * (k + 1)]).then_inc(ln_s, 1)
                for j in range(2):
                    dve.wait_ge(ln_s, 6 * t + 4)
                    v.bn_aggr(aggr[:, t, j, :], stats[:, j, :, :].rearrange("p a b -> p (a b)")).then_inc(ln_s, 1)
                dve.wait_ge(ln_s, 6 * t + 6)
                v.tensor_scalar(neg_mean[:, t, :], aggr[:, t, :, 0], -1.0, None, ALU.mult).then_inc(nm_s, 1)
                dve.wait_ge(ln_sqrt, t + 2)
                v.reciprocal(rstd[:, t, :], rstd[:, t, :]).then_inc(nm_s, 1)
            dve.wait_ge(t_free, 1)
            v.tensor_scalar(conv_half[:], par[:, 0:160], 0.5, None, ALU.mult).then_inc(par_ready, 1)
            v.tensor_scalar(sc_half[:], par[:, SC_W:SC_W + 24], 0.5, None, ALU.mult).then_inc(par_ready, 1)
            v.tensor_scalar(gate_half[:], par[:, B_GATE:B_GATE + 16], 0.5, None, ALU.mult).then_inc(par_ready, 1)

            def weighted_rows(w, cols, tiles, done, between=None):
                acc = w[:, 0, cols]
                v.tensor_scalar(acc, acc, par[:, C_VEC:C_VEC + 1], None, ALU.mult).then_inc(wsum_s, 1)
                for k in range(1, tiles):
                    if k == tiles // 2 and between:
                        between()
                    dve.wait_ge(wsum_s, done + k)
                    v.scalar_tensor_tensor(out=acc, in0=w[:, k, cols], scalar=par[:, C_VEC + k:C_VEC + k + 1],
                                           in1=acc, op0=ALU.mult, op1=ALU.add).then_inc(wsum_s, 1)

            def shift_scale(k):
                h = slice(4 * k, 4 * k + 4)
                bank, part = (pb, yb)[k], tb[1 - k]
                dve.wait_ge(mod_filled, 2 * k + 1)
                v.tensor_tensor(shift[:, h], part[:, 0:4], par[:, B_MOD + 4 * k:B_MOD + 4 * k + 4],
                                ALU.add).then_inc(mod_s, 1)
                v.scalar_tensor_tensor(out=scale1[:, h], in0=part[:, 4:8], scalar=1.0,
                                       in1=par[:, B_MOD + 8 + 4 * k:B_MOD + 12 + 4 * k],
                                       op0=ALU.add, op1=ALU.add).then_inc(mod_s, 1)
                dve.wait_ge(mod_filled, 2 * k + 2)
                for j, dst in enumerate((shift, scale1)):
                    dve.wait_ge(mod_s, 4 * k + j + 1)
                    v.tensor_tensor(dst[:, h], dst[:, h], bank[:, 4 * j:4 * j + 4], ALU.add).then_inc(mod_s, 1)

            for i, k in enumerate((0, 2, 1, 3)):
                dve.wait_ge(wm_in[k], 16)
                weighted_rows(wm, slice(512 * k, 512 * (k + 1)), DVE_TILES, DVE_TILES * i,
                              between=(lambda: shift_scale(0)) if i == 2 else None)
            shift_scale(1)
            for i, q in enumerate(range(9, 16, 2)):
                kt, t = x_fill(q)
                h = slice(HALF * t, HALF * (t + 1))
                dve.wait_ge(filled, q + 1)
                dve.wait_ge(mod_s, 8)
                if i:
                    dve.wait_ge(uv_s, 2 * i)
                v.tensor_scalar(ufv[:], dense[q % 4][:], scale1[:, kt:kt + 1], shift[:, kt:kt + 1], ALU.mult,
                                ALU.add).then_inc(evac[q % 4], 1)
                dve.wait_ge(evac[q % 4], q // 4 + 1)
                v.tensor_scalar(u_hi[:, kt, h], ufv[:], 1.0, None, ALU.mult).then_inc(uv_s, 1)
                dve.wait_ge(uv_s, 2 * i + 1)
                v.tensor_tensor(u_lo[:, kt, h], ufv[:], u_hi[:, kt, h], ALU.subtract).then_inc(uv_s, 1)

            def sc_block(b):
                q = b * 8 + Q_C
                if b.k == 0:
                    dve.wait_ge(consts, 7)
                    dve.wait_ge(par_ready, 3)
                for t in range(2):
                    wait(dve, evac[bank_of(q + t)], use_of(q + t) + 1)
                    wait(dve, filled, q + 2 + t + 1)
                    v.tensor_tensor(prod[:, 2 + HALF * t:2 + HALF * (t + 1)], cv[:, HALF * t:HALF * (t + 1)],
                                    dense[bank_of(q + 2 + t)][:], ALU.mult).then_inc(evac[bank_of(q + 2 + t)], 1)
                for t in range(2):
                    wait(dve, evac[bank_of(q + 2 + t)], use_of(q + 2 + t) + 1)
                v.tensor_scalar(cv[:], prod[:, 2:2 + SEQ], col(sc_half, b + 16), None, ALU.mult).then_inc(sc_s, 1)
                for k in (1, 0):
                    wait(dve, sc_s, b * 6 + (2 - k))
                    v.scalar_tensor_tensor(out=cv[:], in0=prod[:, k:k + SEQ], scalar=col(sc_half, b + 8 * k),
                                           in1=cv[:], op0=ALU.mult, op1=ALU.add).then_inc(sc_s, 1)
                for t in range(2):
                    h = slice(HALF * t, HALF * (t + 1))
                    wait(dve, sc_tanh, b * 2 + (t + 1))
                    v.scalar_tensor_tensor(out=sg[:, h], in0=sg[:, h], scalar=1.0, in1=dense[bank_of(q + 4 + t)][:],
                                           op0=ALU.add, op1=ALU.mult).then_inc(evac[bank_of(q + 4 + t)], 1)
                for t in range(2):
                    h = slice(HALF * t, HALF * (t + 1))
                    wait(dve, evac[bank_of(q + 4 + t)], use_of(q + 4 + t) + 1)
                    wait(dve, filled, q + 6 + t + 1)
                    v.tensor_tensor(sg[:, h], sg[:, h], dense[bank_of(q + 6 + t)][:],
                                    ALU.mult).then_inc(evac[bank_of(q + 6 + t)], 1)
                for t in range(2):
                    wait(dve, evac[bank_of(q + 6 + t)], use_of(q + 6 + t) + 1)
                wait(dve, sc_s, b * 6 + 3)
                v.tensor_tensor(cv[:], cv[:], sg[:], ALU.mult).then_inc(sc_s, 1)
                wait(dve, sc_s, b * 6 + 4)
                v.tensor_scalar(tile_of(hb_hi, b), cv[:], 1.0, None, ALU.mult).then_inc(sc_s, 1)
                wait(dve, sc_s, b * 6 + 5)
                v.tensor_tensor(tile_of(hb_lo, b), cv[:], tile_of(hb_hi, b), ALU.subtract).then_inc(sc_s, 1)

            run(dve, sc_block, 0, 8, peel=1)
            dve.wait_ge(wg_in, 16)
            weighted_rows(wg, slice(0, D), KT, 4 * DVE_TILES)

            def c2_pair(f):
                v.tensor_scalar(gate_slot[:], col(gate_half, f + 8, 2), 1.0, None, ALU.mult).then_inc(gslot_s, 1)
                for j in range(2):
                    q = f * 4 + Q_C2 + 4 * j
                    if f.k:
                        wait(dve, stored[j], (f.over(2)) * 16)
                    for t in range(2):
                        h = slice(HALF * t, HALF * (t + 1))
                        wait(dve, evac[bank_of(q + t)], use_of(q + t) + 1)
                        wait(dve, filled, q + 2 + t + 1)
                        v.scalar_tensor_tensor(out=mb[:, j, h], in0=tgb[:, h], scalar=1.0,
                                               in1=dense[bank_of(q + 2 + t)][:], op0=ALU.add,
                                               op1=ALU.mult).then_inc(evac[bank_of(q + 2 + t)], 1)

            run(dve, c2_pair, 0, 8, step=2, peel=1)
            dve.wait_ge(p_filled, 1)
            v.tensor_tensor(gate_col[:], pb[:, 0:8], par[:, B_MOD + 16:B_MOD + 24], ALU.add).then_inc(p_free, 1)

            def dt_steps():
                bc = dtb_row[:].unsqueeze(1).broadcast_to([P, TT, HEADS])
                dve.wait_ge(t_filled, 2)
                dve.wait_ge(heads_in, 48)
                v.tensor_tensor(dtv[0][:], tb[1][:, 0:256].rearrange("p (c h) -> p c h", c=TT), bc,
                                ALU.add).then_inc(t_free, 1)
                dve.wait_ge(t_free, 2)
                v.scalar_tensor_tensor(out=dtv[1][:], in0=dtv[0][:], scalar=-1.0, in1=dtv[0][:],
                                       op0=ALU.mult, op1=ALU.max).then_inc(dts, 1)
                dve.wait_ge(dta, 2)
                v.tensor_scalar(dtv[3][:], dtv[2][:], 1.0, None, ALU.add).then_inc(dts, 1)
                dve.wait_ge(dts, 2)
                v.tensor_scalar(dtv[5][:], dtv[3][:], -1.0, None, ALU.add).then_inc(dts, 1)
                dve.wait_ge(dts, 3)
                v.tensor_tensor(dtv[6][:], dtv[2][:], dtv[5][:], ALU.subtract).then_inc(dts, 1)
                v.reciprocal(dtv[7][:], dtv[3][:]).then_inc(dts, 1)
                dve.wait_ge(dts, 5)
                v.tensor_tensor(dtv[6][:], dtv[6][:], dtv[7][:], ALU.mult).then_inc(dts, 1)
                v.tensor_scalar(dtv[8][:], dtv[0][:], 0.0, None, ALU.max).then_inc(dts, 1)
                dve.wait_ge(dts, 7)
                v.tensor_tensor(dtv[8][:], dtv[8][:], dtv[6][:], ALU.add).then_inc(dts, 1)
                dve.wait_ge(dts, 8)
                dve.wait_ge(dta, 3)
                v.tensor_tensor(dt_t[:], dtv[8][:], dtv[4][:], ALU.add).then_inc(dts, 1)
                dve.wait_ge(dts, 9)
                v.scalar_tensor_tensor(out=a_t[:], in0=dt_t[:], scalar=-1.0,
                                       in1=exp_a[:].unsqueeze(1).broadcast_to([P, TT, HEADS]),
                                       op0=ALU.mult, op1=ALU.mult).then_inc(dts, 1)

            def y_lo_part(g, t0, k):
                t, j = k // 2, k % 2
                h = slice(HALF * t, HALF * (t + 1))
                wait(dve, yhi_s, (g + (-1)) * 4 + (k + 1))
                v.scalar_tensor_tensor(out=y_lo[:, j, h], in0=tb[t_bank(t0 + k)][:], scalar=col(par, g * 2 + (NORM_W - 2 + j)),
                                       in1=y_hi[:, j, h], op0=ALU.mult, op1=ALU.subtract).then_inc(t_free, 1)

            def add_ya(q, s):
                t, f = s // 8, s % 8
                h = slice(HALF * t, HALF * (t + 1))
                wait(dve, filled, q + 1)
                v.tensor_tensor(ya[:, f, h], ya[:, f, h], dense[bank_of(q)][:],
                                ALU.add).then_inc(evac[bank_of(q)], 1)

            def group(g):
                first = g.k == 0
                n0, q0, t0 = units_b(g)
                conv0 = g * 25

                def group_params():
                    v.tensor_scalar(ac_g[:], heads_of(acum, slice(None), g), 1.0, None, ALU.mult).then_inc(gpar_s, 1)
                    v.tensor_scalar(dt_g[:], heads_of(dt_t, slice(None), g), 1.0, None, ALU.mult).then_inc(gpar_s, 1)
                    v.tensor_scalar(te_g[:], heads_of(to_end, slice(None), g), 1.0, None, ALU.mult).then_inc(gpar_s, 1)
                    v.tensor_scalar(d_g[:], col(d_row, g * HPG, HPG), 1.0, None, ALU.mult).then_inc(gpar_s, 1)

                if not first:
                    v.tensor_scalar(nw_g[:], col(par, g * 2 + (NORM_W - 2), 2), 1.0, None, ALU.mult).then_inc(nw_s, 1)
                    group_params()
                if first:
                    dve.wait_ge(stored[0], 64)
                    dve.wait_ge(stored[1], 64)
                    dve.wait_ge(consts, 8)
                    dve.wait_ge(ya_zero, 1)

                def taps(u, t=None):
                    dst = (bf, cf, xf[0], xf[1])[u]
                    blk = (g + 16, g + 24, g * 2, g * 2 + 1)[u]
                    a, b = (0, SEQ) if t is None else (HALF * t, HALF * (t + 1))
                    for half in (range(2) if t is None else (t,)):
                        q = q0 + 2 * u + half
                        wait(dve, evac[bank_of(q)], use_of(q) + 1)
                    v.tensor_scalar(dst[:, a:b], cin[:, 3 + a:3 + b], col(conv_half, blk + 96), col(conv_half, blk + 128),
                                    ALU.mult, ALU.add).then_inc(conv_s, 1)
                    for k in (2, 1, 0):
                        wait(dve, conv_s, conv0 + (5 * (u + (t or 0)) + 3 - k))
                        v.scalar_tensor_tensor(out=dst[:, a:b], in0=cin[:, k + a:k + b],
                                               scalar=col(conv_half, blk + 32 * k), in1=dst[:, a:b],
                                               op0=ALU.mult, op1=ALU.add).then_inc(conv_s, 1)

                def silu(u, t=None):
                    dst = (bf, cf, xf[0], xf[1])[u]
                    h = slice(0, SEQ) if t is None else slice(HALF * t, HALF * (t + 1))
                    wait(dve, conv_tanh, g * 5 + (u + (t or 0) + 1))
                    v.scalar_tensor_tensor(out=dst[:, h], in0=th[:, h], scalar=1.0, in1=dst[:, h],
                                           op0=ALU.add, op1=ALU.mult).then_inc(conv_s, 1)

                if first:
                    dt_steps()
                    taps(0)
                    silu(0)
                    dve.wait_ge(t_free, 3)
                    v.tensor_tensor(to_end[:], to_end[:], dt_t[:], ALU.mult).then_inc(dts, 1)
                    dve.wait_ge(dts, 11)
                    group_params()
                    taps(1)
                    silu(1)
                    taps(2)
                    silu(2)
                    for t in range(2):
                        taps(3, t)
                        silu(3, t)
                else:
                    taps(0)
                    y_lo_part(g, t0, 0)
                    silu(0)
                    y_lo_part(g, t0, 1)
                    taps(1)
                    y_lo_part(g, t0, 2)
                    silu(1)
                    y_lo_part(g, t0, 3)
                    taps(2)
                    silu(2)
                    taps(3, 0)
                    silu(3, 0)
                    taps(3, 1)
                    add_ya(q0 + 8, 0)
                    silu(3, 1)
                    for s in range(1, 16):
                        add_ya(q0 + (8 + s), s)
                zq = q0 + (8 if first else 24)
                item = g * 8

                def combine(ck):
                    k = (item + ck) * 4
                    wait(dve, xw_s, (item + (ck + 1)) * 3)
                    wait(dve, y_filled, item + (ck + 1))
                    wait(dve, comb_s, k)
                    add = dx[:, ck % 2, :]
                    if ck:
                        v.tensor_tensor(yt[:].rearrange("p (h d) -> p h d", h=HPG),
                                        yb[:, 0:GW].rearrange("p (h d) -> p h d", h=HPG),
                                        heads_of(decay_in, ck, g).unsqueeze(2).broadcast_to([P, HPG, HD]),
                                        ALU.mult).then_inc(comb_s, 1)
                        wait(dve, comb_s, k + 1)
                        v.tensor_tensor(yt[:], yt[:], dx[:, ck % 2, :], ALU.add).then_inc(comb_s, 1)
                        wait(dve, comb_s, k + 2)
                        add = yt[:]
                    v.tensor_tensor(yt[:], yb[:, GW:2 * GW], add, ALU.add).then_inc(y_free, 1)
                    wait(dve, y_free, item + (ck + 1))
                    wait(dve, evac[bank_of(zq + ck)], use_of(zq + ck) + 1)
                    if ck == 0:
                        v.tensor_tensor(y[:, ck, :], yt[:], sz[:], ALU.mult).then_inc(comb_s, 4)
                    else:
                        v.tensor_tensor(y[:, ck, :], yt[:], sz[:], ALU.mult).then_inc(comb_s, 2)

                for ck in range(TT):
                    k = (item + ck) * 3
                    last = ck == TT - 1
                    wait(dve, p_filled, item + (ck + P_B + 1))
                    wait(dve, ssd_s, k)
                    v.tensor_tensor(cbm[:], pb[:, 0:P], tri[:],
                                    ALU.mult).then_inc(p_free if last else ssd_s, 1)
                    if ck:
                        wait(dve, y_filled, item + ck)
                    if ck == 0:
                        v.tensor_copy(state[:, 0, :], pb[:, GW:2 * GW]).then_inc(p_free, 1)
                    elif not last:
                        wait(dve, p_free, item + (ck + P_B))
                        v.tensor_tensor(sdec[:].rearrange("p (h d) -> p h d", h=HPG),
                                        state[:, (ck - 1) % 2, :].rearrange("p (h d) -> p h d", h=HPG),
                                        heads_of(chunk_decay, ck, g).unsqueeze(2).broadcast_to([P, HPG, HD]),
                                        ALU.mult).then_inc(ssd_s, 1)
                        wait(dve, ssd_s, k + 2)
                        v.tensor_tensor(state[:, ck % 2, :], sdec[:], pb[:, GW:2 * GW], ALU.add).then_inc(p_free, 1)
                    wait(dve, exp_ready, (item + (ck + 1)) * 5)
                    wait(dve, y_filled, item + (ck - 1))
                    wait(dve, *((p_free, item + (ck + P_B + 1)) if last else (ssd_s, k + 1)))
                    v.tensor_tensor(m_t[:, ck % 2, :, :], exp_s[:, ck % 2, :, :],
                                    cbm[:].unsqueeze(1).broadcast_to([P, HPG, P]),
                                    ALU.mult).then_inc(ssd_s, 3 if last else 2 if ck == 0 else 1)
                    if ck:
                        combine(ck - 1)
                    wait(dve, z_tanh, item + (ck + 1))
                    wait(dve, comb_s, (item + ck) * 4)
                    v.scalar_tensor_tensor(out=sz[:], in0=tz[:], scalar=1.0, in1=dense[bank_of(zq + ck)][:, 0:GW],
                                           op0=ALU.add, op1=ALU.mult).then_inc(evac[bank_of(zq + ck)], 1)
                combine(TT - 1)
                wait(dve, rms_s, g + 1)
                v.reciprocal(y_rstd[:], y_rstd[:]).then_inc(yn_s, 1)
                wait(dve, yn_s, g * 9 + 1)
                for ck in range(TT):
                    v.tensor_scalar(y[:, ck, :], y[:, ck, :], y_rstd[:, ck:ck + 1], None,
                                    ALU.mult).then_inc(yn_s, 1)

            run(dve, group, 0, GROUPS, peel=1)
            for k in range(4):
                y_lo_part(Lin(GROUPS), Lin(T_TAIL), k)
            for s in range(16):
                add_ya(Q_TAIL + s, s)
            for k in range(KT):
                if k == 0:
                    dve.wait_ge(p_free, 1)
                v.tensor_scalar(diag[:, k, :], ident[:], gate_col[:, k:k + 1], 0.5, ALU.mult,
                                ALU.mult).then_inc(diag_s, 1)
            for f in range(KT):
                for t in range(2):
                    q = (Q_D + 2 * f if f else Q_D0) + t
                    dve.wait_ge(evac[q % 4], q // 4 + 1)
                if f == 0:
                    for q in range(Q_D - 2, Q_D + 2):
                        dve.wait_ge(evac[q % 4], q // 4 + 1)
                if f:
                    dve.wait_ge(mix_s, 3 * f)
                v.scalar_tensor_tensor(out=mt[:], in0=tga[:, f % 2, :], scalar=1.0, in1=ya[:, f, :], op0=ALU.add,
                                       op1=ALU.mult).then_inc(mix_s, 1)
                dve.wait_ge(mix_s, 3 * f + 1)
                dve.wait_ge(mixb_in[f % 2], 16 * (f // 2 + 1))
                v.tensor_tensor(mt[:], mt[:], mixb[:, f % 2, :], ALU.add).then_inc(mix_s, 1)
                dve.wait_ge(mixhi_s, f + 1)
                v.tensor_tensor(mix_lo[:, f, :], mt[:], mix_hi[:, f, :], ALU.subtract).then_inc(mix_s, 1)
            dve.wait_ge(gateb_s, 2)
            dve.wait_ge(lnp_in, 32)
            for t in range(TT):
                s0 = FIN * t
                if t:
                    dve.wait_ge(fin_s, s0)
                dve.wait_ge(xr_in[t % 2], 16 * (t // 2 + 1))
                for b in range(2):
                    h = slice(512 * b, 512 * (b + 1))
                    dve.wait_ge(e_filled, 2 * t + b + 1)
                    v.tensor_tensor(res[:, h], gate_b[:, h], banks8[2 * (t % 4) + b][:], ALU.mult).then_inc(e_evac, 1)
                    dve.wait_ge(e_evac, 2 * t + b + 1)
                    v.scalar_tensor_tensor(out=res[:, h], in0=xr[:, t % 2, h], scalar=ALPHA, in1=res[:, h],
                                           op0=ALU.mult, op1=ALU.add).then_inc(fin_s, 1)
                    dve.wait_ge(fin_s, s0 + 2 * b + 1)
                    v.bn_stats(stats_e[:, b, :], res[:, h]).then_inc(fin_s, 1)
                dve.wait_ge(fin_s, s0 + 4)
                v.bn_aggr(aggr_e[:], stats_e[:].rearrange("p a b -> p (a b)")).then_inc(fin_s, 2)
                if t >= 2:
                    dve.wait_ge(out_s[t % 2], 16 * (t // 2))
                dve.wait_ge(fin_s, s0 + 6)
                v.scalar_tensor_tensor(out=ob[:, t % 2, :], in0=res[:], scalar=aggr_e[:, 0:1], in1=lng_b[:],
                                       op0=ALU.subtract, op1=ALU.mult).then_inc(fin_s, 1)
                dve.wait_ge(fin_sqrt, t + 1)
                v.reciprocal(rstd_e[:], rstd_e[:]).then_inc(fin_s, 1)
                dve.wait_ge(fin_s, s0 + 8)
                for b in range(2 if t == TT - 1 else 1):
                    h = slice(512 * b, 512 * (b + 1)) if t == TT - 1 else slice(0, D)
                    v.scalar_tensor_tensor(out=ob[:, t % 2, h], in0=ob[:, t % 2, h], scalar=rstd_e[:, 0:1],
                                           in1=lnb_b[:, h], op0=ALU.mult, op1=ALU.add).then_inc(fin_s, 1)

        @block.tensor
        def _(pe):
            mm = nc.tensor.matmul
            tr = nc.tensor.transpose

            def three(bank, s_hi, s_lo, m_hi, m_lo, start, stop):
                mm(bank, s_hi, m_hi, start=start, stop=False)
                mm(bank, s_hi, m_lo, start=False, stop=False)
                return mm(bank, s_lo, m_hi, start=False, stop=stop)

            def half_unit(n, q, t, a_hi=u_hi, a_lo=u_lo):
                n, q = at(n), at(q)
                s = n.mod(4)
                h = slice(HALF * t, HALF * (t + 1))
                if t == 0:
                    wait(pe, lo_done, n + 1)
                if n.k == 0 and n.c == U_C:
                    pe.wait_ge(ulo_s, (10, 12)[t])
                    pe.wait_ge(uv_s, (4, 8)[t])
                wait(pe, evac[bank_of(q)], use_of(q))
                for k in range(KT):
                    f = slice(P * k, P * (k + 1))
                    last = three(dense[bank_of(q)][:], w_hi[:, s, f], w_lo[:, s, f],
                                 a_hi[:, k, h], a_lo[:, k, h], k == 0, k == KT - 1)
                last.then_inc(filled, 1)

            pe.wait_ge(rows_in, 16 * 7)
            pe.wait_ge(consts, 4)
            tr(tb[0][:, 0:P], rows[:, 0, :], ident[:])
            tr(tb[0][:, P:N_PAR], rows[0:N_PAR - P, 1, :], ident[0:N_PAR - P, 0:N_PAR - P]).then_inc(t_filled, 1)
            pe.wait_ge(t_free, 1)
            def x_to_features(qs):
                for q in qs:
                    kt, t = x_fill(q)
                    pe.wait_ge(xn_s, 8 * (t + 1))
                    wait(pe, evac[q % 4], q // 4)
                    for j in range(4):
                        last = tr(dense[q % 4][:, P * j:P * (j + 1)], xt[:, 4 * t + j, P * kt:P * (kt + 1)],
                                  ident[:])
                    last.then_inc(filled, 1)

            def mod_column(half, j):
                return P * (4 * half + j % 4) + (j // 4) * D

            def mod_part(half):
                pe.wait_ge(wm_in[half], 16)
                pe.wait_ge(wm_in[half + 2], 16)
                for j in range(8):
                    c0 = mod_column(half, j)
                    for k in range(DVE_TILES, KT):
                        last = mm(tb[1 - half][:, j:j + 1], wm[:, k, c0:c0 + P], par[:, C_VEC + k:C_VEC + k + 1],
                                  start=k == DVE_TILES, stop=k == KT - 1)
                last.then_inc(mod_filled, 1)

            def mod_sum(half):
                for j in range(8):
                    c0 = mod_column(half, j)
                    if j % 4 == 0:
                        pe.wait_ge(wsum_s, DVE_TILES * (2 * half + j // 4 + 1))
                    last = mm((pb, yb)[half][:, j:j + 1], wm[:, 0, c0:c0 + P], ones[:, 0:1], start=True, stop=True)
                last.then_inc(mod_filled, 1)

            x_to_features(range(4))
            mod_part(0)
            mod_sum(0)
            x_to_features(range(4, 6))
            mod_part(1)
            x_to_features(range(6, 8))
            mod_sum(1)
            x_to_features(range(8, 16))

            def sc_block(b):
                for j in range(4):
                    for t in range(2):
                        half_unit(b * 4 + U_C + j, b * 8 + (Q_C + 2 * j + t), t)

            run(pe, sc_block, 0, 8, peel=1)

            def c2_pair(f):
                for j in range(2):
                    n, q = f * 2 + (U_C2 + 2 * j), f * 4 + (Q_C2 + 4 * j)
                    for t in range(2):
                        half_unit(n, q + t, t)
                    if j == 0 and f.k == 0:
                        pe.wait_ge(sc_s, 48)
                    for t in range(2):
                        half_unit(n + 1, q + 2 + t, t, hb_hi, hb_lo)

            run(pe, c2_pair, 0, 8, step=2, peel=1)
            pe.wait_ge(wsum_s, 4 * DVE_TILES + KT)
            for j in range(8):
                last = mm(pb[:, j:j + 1], wg[:, 0, P * j:P * (j + 1)], ones[:, 0:1], start=True, stop=True)
            last.then_inc(p_filled, 1)
            for t in range(2):
                half_unit(U_DT, Q_DT + t, t)

            def y_transposes(g, t0, k):
                t, j = k // 2, k % 2
                if j == 0:
                    wait(pe, yn_s, g * 9 + (0 if t else -4))
                wait(pe, t_free, t0 + (k - 1))
                for cc in range(4):
                    last = tr(tb[t_bank(t0 + k)][:, P * cc:P * (cc + 1)], y[:, 4 * t + cc, P * j:P * (j + 1)], ident[:])
                last.then_inc(t_filled, 1)

            def ya_fill(n, q, s):
                t, f = s // 8, s % 8
                h, fs = slice(HALF * t, HALF * (t + 1)), slice(P * f, P * (f + 1))
                wait(pe, evac[bank_of(q)], use_of(q))
                for j in range(2):
                    sl = (n + j).mod(4)
                    last = three(dense[bank_of(q)][:], w_hi[:, sl, fs], w_lo[:, sl, fs],
                                 y_hi[:, j, h], y_lo[:, j, h], j == 0, j == 1)
                last.then_inc(filled, 1)

            def group(g):
                first = g.k == 0
                n0, q0, t0 = units_b(g)
                k0 = 0 if first else 4

                def halves(u, t):
                    half_unit(n0 + u, q0 + (2 * u + t), t)

                def to_tokens(k):
                    wait(pe, conv_s, g * 25 + (5, 15, 20 if k < 3 else 25)[k % 3])
                    wait(pe, t_free, t0 + (k0 + k - 1))
                    src = (bf, xf[0], xf[1])[k % 3]
                    for cc in range(4):
                        cs = slice(HALF * (k // 3) + P * cc, HALF * (k // 3) + P * (cc + 1))
                        last = tr(tb[t_bank(t0 + (k0 + k))][:, P * cc:P * (cc + 1)], src[:, cs], ident[:])
                    last.then_inc(t_filled, 1)

                halves(0, 0)
                if first:
                    for t in range(2):
                        pe.wait_ge(evac[(Q_DT + t) % 4], (Q_DT + t) // 4 + 1)
                    for ck in range(TT):
                        last = tr(tb[1][:, 32 * ck:32 * (ck + 1)], dt_raw[:, P * ck:P * (ck + 1)], ident[0:32, 0:32])
                    last.then_inc(t_filled, 1)
                halves(0, 1)
                if not first:
                    y_transposes(g, t0, 0)
                halves(1, 0)
                if not first:
                    y_transposes(g, t0, 1)
                halves(1, 1)
                if first:
                    pe.wait_ge(dts, 10)
                    pe.wait_ge(p_free, 1)
                    at_ = a_t[:].rearrange("p c h -> p (c h)")
                    mm(tb[0][:, 0:256], tri[:], at_, start=True, stop=True)
                    mm(tb[0][:, 256:512], strict[:], at_, start=True, stop=True).then_inc(t_filled, 1)
                    mm(pb[:, 0:256], ones[:], at_, start=True, stop=True).then_inc(p_filled, 1)
                else:
                    y_transposes(g, t0, 2)
                halves(2, 0)
                if first:
                    for k in range(2):
                        pe.wait_ge(t_free, 2 + k)
                        for ck in range(4):
                            last = mm(tb[(3 + k) % 2][0:32, P * ck:P * (ck + 1)], a_t[:, 4 * k + ck, :], tri[:],
                                      start=True, stop=True)
                        last.then_inc(t_filled, 1)
                else:
                    y_transposes(g, t0, 3)
                halves(2, 1)
                halves(3, 0)
                halves(3, 1)
                if first:
                    for k in range(2):
                        to_tokens(k)
                else:
                    wait(pe, lo_done, n0 + 6)
                    when = {1: 0, 3: 1, 6: 2, 8: 3, 10: 4, 12: 5}
                    for s in range(16):
                        if s == 0:
                            wait(pe, t_free, t0 + 4)
                        ya_fill(n0 + 4, q0 + (8 + s), s)
                        if s in when:
                            to_tokens(when[s])
                zn, zq = n0 + (4 if first else 6), q0 + (8 if first else 24)
                item = g * 8

                def prep(ck):
                    cs = slice(P * ck, P * (ck + 1))
                    if ck == 0:
                        wait(pe, conv_s, g * 25 + 10)
                    wait(pe, p_free, item + (ck + P_B))
                    last = mm(pb[:, 0:P], bf[:, cs], cf[:, cs], start=True, stop=True)
                    if ck < TT - 1:
                        wait(pe, xw_s, (item + ck) * 3 + 1)
                        if ck % 4 == 0:
                            wait(pe, t_free, t0 + (k0 + (1 if ck == 0 else 4)))
                        last = mm(pb[:, GW:2 * GW], bt[:, ck, :], x_end[:, ck % 2, :], start=True, stop=True)
                    last.then_inc(p_filled, 1)

                def main(ck):
                    cs = slice(P * ck, P * (ck + 1))
                    wait(pe, ssd_s, (item + ck) * 3 + 3)
                    wait(pe, xw_s, (item + ck) * 3 + (3 if ck == TT - 1 else 2))
                    if ck:
                        wait(pe, p_free, item + (ck + P_B))
                    wait(pe, y_free, item + ck)
                    if ck:
                        mm(yb[:, 0:GW], cf[:, cs], state[:, (ck - 1) % 2, :], start=True, stop=True)
                    for h in range(HPG):
                        last = mm(yb[:, GW + HD * h:GW + HD * (h + 1)], m_t[:, ck % 2, h, :],
                                  xdt[:, ck % 2, HD * h:HD * (h + 1)], start=True, stop=True)
                    last.then_inc(y_filled, 1)

                def z_tile(ck):
                    q = zq + ck
                    s = zn.mod(4)
                    cs = slice(P * ck, P * (ck + 1))
                    if ck == 0:
                        wait(pe, lo_done, zn + 2)
                    wait(pe, evac[bank_of(q)], use_of(q))
                    for k in range(KT):
                        f = slice(P * k, P * (k + 1))
                        last = three(dense[bank_of(q)][:, 0:GW], u_hi[:, k, cs], u_lo[:, k, cs],
                                     w_hi[:, s:s + 2, f], w_lo[:, s:s + 2, f], k == 0, k == KT - 1)
                    last.then_inc(filled, 1)

                if first:
                    z_tile(0)
                    to_tokens(2)
                prep(0)
                for ck in range(TT):
                    if not first or ck:
                        z_tile(ck)
                    if ck < TT - 1:
                        prep(ck + 1)
                    main(ck)
                    if first and ck < 3:
                        to_tokens(3 + ck)

            run(pe, group, 0, GROUPS, peel=1)
            for t in range(2):
                half_unit(U_D0, Q_D0 + t, t)
                for j in range(2):
                    y_transposes(Lin(GROUPS), Lin(T_TAIL), 2 * t + j)
            pe.wait_ge(lo_done, U_TAIL + 2)
            for s in range(16):
                if s % 8 == 0:
                    pe.wait_ge(t_free, T_TAIL + (2 if s == 0 else 4))
                ya_fill(Lin(U_TAIL), Q_TAIL + s, s)
            for f in range(1, KT):
                for t in range(2):
                    half_unit(U_D + f, Q_D + 2 * f + t, t)
                if f == 1:
                    pe.wait_ge(diag_s, 8)
                    for k in range(KT):
                        bank = tb[(T_TAIL + k // 4) % 2]
                        last = mm(bank[:, P * (k % 4):P * (k % 4 + 1)], ones[:], diag[:, k, :], start=True, stop=True)
                        if k % 4 == 3:
                            last.then_inc(t_filled, 1)
            pe.wait_ge(gateb_s, 2)
            pe.wait_ge(p_free, P_B + 64)
            pe.wait_ge(y_free, 64)

            def out_tile(t, k, b):
                ts, cs = slice(P * t, P * (t + 1)), slice(512 * b, 512 * (b + 1))
                return three(banks8[2 * (t % 4) + b][:], mix_hi[:, k, ts], mix_lo[:, k, ts],
                             wo[k][0][:, cs], wo[k][1][:, cs], k == 0, k == KT - 1)

            for k in range(KT):
                pe.wait_ge(mix_s, 3 * (k + 1))
                pe.wait_ge(lo_done, U_E + k + 1)
                for t in range(2):
                    for b in range(2):
                        last = out_tile(t, k, b)
                        if k == KT - 1:
                            last.then_inc(e_filled, 1)
            for t in range(2, TT):
                for b in range(2):
                    if t < 4:
                        q = 2 * (t - 2) + b
                        pe.wait_ge(evac[q], Q_END // 4 + (1 if Q_END % 4 > q else 0))
                    else:
                        pe.wait_ge(e_evac, 2 * (t - 4) + b + 1)
                    for k in range(KT):
                        last = out_tile(t, k, b)
                    last.then_inc(e_filled, 1)


_INS = ["x", "c", "w_mod", "b_mod", "w_in", "conv_ssm_w", "conv_ssm_b", "dt_bias", "a_log", "d_skip",
        "ssm_norm_w", "conv_sc_w", "w_branch_a", "w_branch_b", "w_gate", "b_gate", "w_out", "ln_g", "ln_b"]


def kernel(**inputs):
    import numpy as np
    import concourse.bacc as bacc
    from concourse.bass_utils import run_bass_kernel_spmd

    nc = bacc.Bacc("TRN2", target_bir_lowering=False, num_devices=1, dynamic_dma_scratch_size=1024)
    arrays, args = {}, []
    for name in _INS:
        a = np.ascontiguousarray(inputs[name])
        arrays[f"in_{name}"] = a
        args.append(nc.dram_tensor(f"in_{name}", a.shape, mybir.dt.from_np(a.dtype), kind="ExternalInput").ap())
    args.append(nc.dram_tensor("spill", (KT, P, SEQ), F32, kind="Internal").ap())
    args.append(nc.dram_tensor("acum", (HEADS, SEQ), F32, kind="Internal").ap())
    args.append(nc.dram_tensor("out_0", (1, SEQ, D), F32, kind="ExternalOutput").ap())
    build(nc, *args)
    r = run_bass_kernel_spmd(nc, [arrays], core_ids=[0])
    return r.results[0]["out_0"]
```
